# Optimizing a Trainium2 kernel written in Bass

```python
import jax, jax.numpy as jnp
from jax import lax
import numpy as np

D_MODEL = 1024
BATCH = 1
SEQ = 256
DEPTH = 2

D_A = 512
CONV_WIDTH = 3
H_B = 4
DK_B = 128
DV_B = 128
D_BK = H_B * DK_B
D_BV = H_B * DV_B
HGRN_CHUNK = 16
G_C = 4
GC_CH = 128
D_C = G_C * GC_CH
SGU_CHUNK = 128
D_FF = 2816
N_EXPERTS = 8
TOP_K = 2
D_FF_EXPERT = 2816
N_DENSE = (DEPTH + 1) // 2
N_MOE = DEPTH // 2
N_IN = 3 * D_A + 2 * D_BK + 2 * D_BV + 2 * D_C + 3 * D_MODEL
EPS = 1e-6
LB_FLOOR = 1e-30

kernel_name = "hybrid_conv_hgrn2_gmlp_moe_adaln"

def rmsnorm(x, w):
    xf = x.astype(jnp.float32)
    y = xf * lax.rsqrt(jnp.mean(xf * xf, axis=-1, keepdims=True) + EPS)
    return (y * w.astype(jnp.float32)).astype(x.dtype)

def short_conv_mixer(gate_b, gate_c, h, conv_w):
    z = gate_c * h
    seq = z.shape[1]
    zp = jnp.pad(z, ((0, 0), (CONV_WIDTH - 1, 0), (0, 0)))
    y = conv_w[0] * zp[:, CONV_WIDTH - 1:CONV_WIDTH - 1 + seq]
    for k in range(1, CONV_WIDTH):
        y = y + conv_w[k] * zp[:, CONV_WIDTH - 1 - k:CONV_WIDTH - 1 - k + seq]
    return gate_b * y

def hgrn2_mixer(q, f_raw, i, g, lb, norm_w):
    bsz, seq, _ = q.shape
    nc = seq // HGRN_CHUNK
    f32 = jnp.float32
    fr = f_raw.astype(f32)
    lb = lb.astype(f32)
    log_f = jnp.logaddexp(jnp.log(jnp.maximum(lb, LB_FLOOR)), jnp.log1p(-lb) + jax.nn.log_sigmoid(fr))
    k = (1.0 - lb) * jax.nn.sigmoid(-fr)
    qf = jax.nn.silu(q.astype(f32))
    v = i.astype(f32)

    def to_chunks(t, d):
        return t.reshape(bsz, nc, HGRN_CHUNK, H_B, d).transpose(1, 0, 3, 2, 4)

    xs = (to_chunks(qf, DK_B), to_chunks(k, DK_B), to_chunks(v, DV_B), to_chunks(log_f, DK_B))
    causal = jnp.tril(jnp.ones((HGRN_CHUNK, HGRN_CHUNK), dtype=bool))[:, :, None]

    def chunk_step(state, inp):
        qc, kc, vc, lc = inp
        b = jnp.cumsum(lc, axis=2)
        diff = b[:, :, :, None, :] - b[:, :, None, :, :]
        decay = jnp.where(causal, jnp.exp(jnp.where(causal, diff, 0.0)), 0.0)
        scores = jnp.einsum('bhtd,bhsd,bhtsd->bhts', qc, kc, decay)
        o = (jnp.einsum('bhts,bhsv->bhtv', scores, vc)
             + jnp.einsum('bhtd,bhdv->bhtv', qc * jnp.exp(b), state))
        b_last = b[:, :, -1:, :]
        new_state = (jnp.exp(b_last[:, :, 0, :])[..., None] * state
                     + jnp.einsum('bhsd,bhsv->bhdv', kc * jnp.exp(b_last - b), vc))
        return new_state, o

    state0 = jnp.zeros((bsz, H_B, DK_B, DV_B), f32)
    _, o = lax.scan(chunk_step, state0, xs)
    o = o.transpose(1, 0, 3, 2, 4).reshape(bsz, seq, H_B, DV_B)
    o = o * lax.rsqrt(jnp.mean(o * o, axis=-1, keepdims=True) + EPS) * norm_w.astype(f32).reshape(H_B, DV_B)
    o = o.reshape(bsz, seq, D_BV) * jax.nn.silu(g.astype(f32))
    return o.astype(q.dtype)

def chunked_sgu(u, v, norm_w, w_s, b_s):
    bsz, seq, _ = u.shape
    v = rmsnorm(v, norm_w)
    vg = v.reshape(bsz, seq // SGU_CHUNK, SGU_CHUNK, G_C, GC_CH)
    tril = jnp.tril(jnp.ones((SGU_CHUNK, SGU_CHUNK), dtype=w_s.dtype))
    mixed = jnp.einsum('gts,bnsgc->bntgc', w_s * tril, vg) + b_s.T[None, None, :, :, None]
    return u * mixed.reshape(bsz, seq, D_C)

def hybrid_mixer(h, lb, w_in, conv_w, hgrn_norm_w, sgu_norm_w, sgu_w, sgu_b, w_br_a, w_br_b, w_br_c, w_o):
    sizes = (D_A, D_A, D_A, D_BK, D_BK, D_BV, D_BV, D_C, D_C, D_MODEL, D_MODEL, D_MODEL)
    split_idx = np.cumsum(sizes)[:-1].tolist()
    proj = h @ w_in
    (a_b, a_c, a_h, b_q, b_f, b_i, b_g, c_u, c_v, gate_a, gate_b, gate_c) = jnp.split(proj, split_idx, axis=-1)
    y_a = short_conv_mixer(a_b, a_c, a_h, conv_w) @ w_br_a
    y_b = hgrn2_mixer(b_q, b_f, b_i, b_g, lb, hgrn_norm_w) @ w_br_b
    y_c = chunked_sgu(c_u, c_v, sgu_norm_w, sgu_w, sgu_b) @ w_br_c
    merged = jax.nn.sigmoid(gate_a) * y_a + jax.nn.sigmoid(gate_b) * y_b + jax.nn.sigmoid(gate_c) * y_c
    return merged @ w_o

def swiglu(h, w1, w3, w2):
    return (jax.nn.silu(h @ w1) * (h @ w3)) @ w2

def moe_swiglu(h, router_w, router_b, w1, w3, w2):
    logits = (h @ router_w).astype(jnp.float32) + router_b.astype(jnp.float32)
    top_v, top_i = lax.top_k(logits, TOP_K)
    top_p = jax.nn.softmax(top_v, axis=-1)
    gates = jnp.sum(jax.nn.one_hot(top_i, N_EXPERTS, dtype=jnp.float32) * top_p[..., None], axis=-2)
    gates = gates.astype(h.dtype)
    out = jnp.zeros_like(h)
    for e in range(N_EXPERTS):
        out = out + gates[..., e:e + 1] * swiglu(h, w1[e], w3[e], w2[e])
    return out

def setup_inputs(seed: int = 0) -> dict:
    key = jax.random.key(seed)
    ks = jax.random.split(key, 32)
    f32 = jnp.float32

    def nrm(k, shape, scale):
        return jax.random.normal(k, shape, f32) * scale

    return {
        "x": nrm(ks[0], (BATCH, SEQ, D_MODEL), 1.0),
        "c": nrm(ks[1], (BATCH, D_MODEL), 1.0),
        "ada_w": nrm(ks[2], (DEPTH, D_MODEL, 6 * D_MODEL), D_MODEL ** -0.5),
        "ada_b": nrm(ks[3], (DEPTH, 6 * D_MODEL), 0.02),
        "norm_mix_w": 1.0 + nrm(ks[4], (DEPTH, D_MODEL), 0.02),
        "norm_ffn_w": 1.0 + nrm(ks[5], (DEPTH, D_MODEL), 0.02),
        "w_in": nrm(ks[6], (DEPTH, D_MODEL, N_IN), D_MODEL ** -0.5),
        "conv_w": nrm(ks[7], (DEPTH, CONV_WIDTH, D_A), CONV_WIDTH ** -0.5),
        "hgrn_lb_logits": nrm(ks[8], (DEPTH, D_BK), 0.5),
        "hgrn_norm_w": 1.0 + nrm(ks[9], (DEPTH, D_BV), 0.02),
        "sgu_norm_w": 1.0 + nrm(ks[10], (DEPTH, D_C), 0.02),
        "sgu_w": nrm(ks[11], (DEPTH, G_C, SGU_CHUNK, SGU_CHUNK), SGU_CHUNK ** -0.5),
        "sgu_b": 1.0 + nrm(ks[12], (DEPTH, G_C, SGU_CHUNK), 0.1),
        "w_br_a": nrm(ks[13], (DEPTH, D_A, D_MODEL), D_A ** -0.5),
        "w_br_b": nrm(ks[14], (DEPTH, D_BV, D_MODEL), D_BV ** -0.5),
        "w_br_c": nrm(ks[15], (DEPTH, D_C, D_MODEL), D_C ** -0.5),
        "w_o": nrm(ks[16], (DEPTH, D_MODEL, D_MODEL), D_MODEL ** -0.5),
        "ffn_w1": nrm(ks[17], (N_DENSE, D_MODEL, D_FF), D_MODEL ** -0.5),
        "ffn_w3": nrm(ks[18], (N_DENSE, D_MODEL, D_FF), D_MODEL ** -0.5),
        "ffn_w2": nrm(ks[19], (N_DENSE, D_FF, D_MODEL), D_FF ** -0.5),
        "moe_router_w": nrm(ks[20], (N_MOE, D_MODEL, N_EXPERTS), D_MODEL ** -0.5),
        "moe_router_b": nrm(ks[21], (N_MOE, N_EXPERTS), 0.01),
        "moe_w1": nrm(ks[22], (N_MOE, N_EXPERTS, D_MODEL, D_FF_EXPERT), D_MODEL ** -0.5),
        "moe_w3": nrm(ks[23], (N_MOE, N_EXPERTS, D_MODEL, D_FF_EXPERT), D_MODEL ** -0.5),
        "moe_w2": nrm(ks[24], (N_MOE, N_EXPERTS, D_FF_EXPERT, D_MODEL), D_FF_EXPERT ** -0.5),
        "final_norm_w": 1.0 + nrm(ks[25], (D_MODEL,), 0.02),
    }

def reference(x, c, ada_w, ada_b, norm_mix_w, norm_ffn_w, w_in, conv_w, hgrn_lb_logits, hgrn_norm_w,
              sgu_norm_w, sgu_w, sgu_b, w_br_a, w_br_b, w_br_c, w_o, ffn_w1, ffn_w3, ffn_w2,
              moe_router_w, moe_router_b, moe_w1, moe_w3, moe_w2, final_norm_w):
    p = jax.nn.softmax(hgrn_lb_logits.astype(jnp.float32), axis=0)
    lb_all = jnp.clip(jnp.cumsum(p, axis=0) - p[0:1], 0.0, 1.0)
    c_act = jax.nn.silu(c)
    for l in range(DEPTH):
        mod = (c_act @ ada_w[l] + ada_b[l])[:, None, :]
        sh1, sc1, g1, sh2, sc2, g2 = jnp.split(mod, 6, axis=-1)
        h = rmsnorm(x, norm_mix_w[l]) * (1.0 + sc1) + sh1
        x = x + g1 * hybrid_mixer(h, lb_all[l], w_in[l], conv_w[l], hgrn_norm_w[l], sgu_norm_w[l], sgu_w[l],
                                  sgu_b[l], w_br_a[l], w_br_b[l], w_br_c[l], w_o[l])
        h = rmsnorm(x, norm_ffn_w[l]) * (1.0 + sc2) + sh2
        j = l // 2
        if l % 2 == 0:
            ffn = swiglu(h, ffn_w1[j], ffn_w3[j], ffn_w2[j])
        else:
            ffn = moe_swiglu(h, moe_router_w[j], moe_router_b[j], moe_w1[j], moe_w3[j], moe_w2[j])
        x = x + g2 * ffn
    return rmsnorm(x, final_norm_w)


_drawn_inputs = setup_inputs


def setup_inputs(seed=0):
    import zlib

    import numpy as np

    out = dict(_drawn_inputs(seed))
    spreads = {}
    factors = {'hgrn_lb_logits': 3.821,
     'hgrn_norm_w': 14.009,
     'sgu_norm_w': 17.71,
     'moe_router_b': 33.455,
     'final_norm_w': 7.944,
     'norm_ffn_w': 3.29}
    for name, (base, spread) in spreads.items():
        noise = np.random.default_rng([zlib.crc32(name.encode()), seed]).standard_normal(out[name].shape)
        drawn = base * np.exp(spread * noise) if base else spread * noise
        out[name] = __import__('jax').numpy.asarray(drawn.astype(out[name].dtype))
    for name, factor in factors.items():
        out[name] = (out[name] * factor).astype(out[name].dtype)
    return out
```

```python
from contextlib import ExitStack

import concourse.bass as bass
from concourse import mybir

P = 128
F32 = mybir.dt.float32
I32 = mybir.dt.int32
U32 = mybir.dt.uint32
U8 = mybir.dt.uint8
ALU = mybir.AluOpType
ACT = mybir.ActivationFunctionType
AX_X = mybir.AxisListType.X

T = 256
TT = T // P
D = 1024
KD = D // P
HB = 4
FF = 2816
NF = FF // P
NE = 8
DEPTH = 2
EPS = 1e-6
LB_FLOOR = 1e-30
GROUP = 512
RING = 11
PANEL = 2048
NLEV = 9

CAP = 104
JEX = -(-T // CAP) - 1
REX = (2 * T) // (CAP + 1)
MAXI = NE + REX

COLS = {n: 512 * c for c, n in enumerate(["ab", "ac", "ah", "q", "f", "i", "g", "u", "v"])}
GATE0 = {"a": 4608, "b": 5632, "c": 6656}
HEAD_GROUPS = ["f", "q", "ab", "ac", "ah", "i", "v", "u", "g"]
BRANCHES = ["a", "c", "b"]

ADA_B, C_ROW, LB_ROW, NA_ROWS = 0, 96, 104, 112
NMIX, NFFN, CONV, HNW, SNW, NB_ROWS = 0, 16, 32, 56, 64, 72

ADA_PANELS = 8
DOWN0 = NF // 2 - 1
EXP_UNITS = NF + 5


def unit_plan():
    plan = [(("x", j), "A") for j in range(4)] + [(("vec", 0), "A"), (("wt", 0), "D"), (("wt", 1), "D")]
    for l in range(DEPTH):
        for g in HEAD_GROUPS:
            plan += [((l, g, j), "A" if g in ("f", "ab", "ac", "i", "u") else "D") for j in range(2)]
        for b in BRANCHES:
            plan += [((l, "gate" + b, j), "A") for j in range(4)]
            plan += [((l, "y" + b, j), "D") for j in range(4)]
        plan += [((l, "wo", j), "D") for j in range(4)]
        if l == 0:
            plan += [(("ffn", j), "D") for j in range(NF)]
    plan += [("logits", "D"), ("rank", "D")]
    plan += [(("htok", j), "A") for j in range(4)] + [(("xtok", j), "A") for j in range(4)]
    plan += [(("g2", j), "A") for j in range(2)] + [("sel0", "D")]
    return plan


def event_plan():
    plan = [(("ada", 0), "D"), (("ada", 1), "D")]
    for l in range(DEPTH):
        plan += [((l, "norm1"), "A")] + [((l, "lev", j), "D") for j in range(NLEV)]
        plan += [((l, "sgu"), "D"), ((l, "o"), "D"), ((l, "ostat"), "A")]
        if l == 0:
            plan += [(("ada", s), "D") for s in (2, 3, 4)]
        plan += [((l, "norm2"), "A")]
        if l == 0:
            plan += [(("ada", s), "D") for s in range(5, 12)]
            plan += [("down0", "D"), ("down1", "D")]
    plan += [("gather0", "A")]
    return plan


def panel_plan():
    plan = [("ada", j + 1) for j in range(ADA_PANELS)]
    down = 0
    for l in range(DEPTH):
        for g in HEAD_GROUPS:
            plan += [("unit", UNIT_AT[(l, g, 1)] + 1)] * 2
        for b in BRANCHES:
            plan += [("unit", UNIT_AT[(l, "gate" + b, 1)] + 1)] * 2 + [("unit", UNIT_AT[(l, "gate" + b, 3)] + 1)] * 2
            plan += [("unit", UNIT_AT[(l, "y" + b, 3)] + 1)] * 2
        plan += [("unit", UNIT_AT[(l, "wo", 1)] + 1)] * 2 + [("unit", UNIT_AT[(l, "wo", 3)] + 1)] * 2
        if l == 0:
            for g in range(FF // GROUP):
                plan += [("unit", UNIT_AT[("ffn", 4 * g + 3)] + 1)] * 4
            plan += [("unit", UNIT_AT[("ffn", NF - 1)] + 1)] * 2
            plan += [("down", j + 1) for j in range(NF // 2 - 1)] + [("event", EVENT_AT["down1"] + 1)]
    return plan


UNITS = unit_plan()
EVENTS = event_plan()
UNIT_AT = {k: n for n, (k, _) in enumerate(UNITS)}
EVENT_AT = {k: n for n, (k, _) in enumerate(EVENTS)}


PANELS = panel_plan()


def emptied(plan, upto, who):
    return sum(1 for _, w in plan[:upto + 1] if w == who)


def program(nc, x, c, ada_w, ada_b, norm_mix_w, norm_ffn_w, w_in, conv_w, lb_logits, hgrn_norm_w,
            sgu_norm_w, sgu_w, sgu_b, w_br_a, w_br_b, w_br_c, w_o, ffn_w1, ffn_w3, ffn_w2,
            router_w, router_b, moe_w1, moe_w3, moe_w2, final_norm_w, out):
    W_BR = {"a": w_br_a, "b": w_br_b, "c": w_br_c}
    with ExitStack() as ctx:
        def sb(name, shape, dt=F32):
            return ctx.enter_context(nc.sbuf_tensor(name, shape, dt))

        def sem(name):
            return ctx.enter_context(nc.semaphore(name))

        psU = [ctx.enter_context(nc.psum_tensor(f"psU{i}", [P, 512], F32)) for i in range(4)]
        psA = [ctx.enter_context(nc.psum_tensor(f"psA{i}", [P, 512], F32)) for i in range(4)]

        ring = sb("ring", [P, RING, PANEL])
        adar = sb("adar", [P, 2, PANEL])
        adacc = sb("adacc", [P, 2, D])
        xT = sb("xT", [P, KD, T])
        hT = sb("hT", [P, KD, T])
        merged = sb("merged", [P, KD, T])
        sig = sb("sig", [P, 4, 512])
        work = sb("work", [P, 10, 1024])
        sc = sb("sc", [P, 3, HB, P])
        masks = sb("masks", [P, NLEV - 1, P], U8)
        wT = sb("wT", [P, DEPTH, HB, P])
        sgub = sb("sgub", [P, DEPTH, HB, P])
        vecs = sb("vecs", [P, NA_ROWS + NB_ROWS])
        mod = sb("mod", [P, DEPTH, 48])
        wm = sb("wm", [P, DEPTH, 2, KD])
        cact = sb("cact", [P, KD])
        lbs = sb("lbs", [P, DEPTH, 3, HB])
        ident = sb("ident", [P, P])
        ones = sb("ones", [P, P])
        tri = sb("tri", [P, P])
        rstd = sb("rstd", [P, T])
        vst = sb("vst", [P, 8])
        eps = sb("eps", [P, 1])
        small = sb("small", [P, 16])
        iotas = sb("iotas", [P, 2, P], I32)
        rtw = sb("rtw", [P, KD, NE])
        rtb = sb("rtb", [P, NE])
        route = sb("route", [P, 12, 2 * NE])
        cur = sb("cur", [P, 8])
        slots = sb("slots", [P, CAP])
        items = sb("items", [P, MAXI + 1, 2])
        itemi = sb("itemi", [P, MAXI + 1], I32)
        nitem = sb("nitem", [P, 1], I32)
        mx8 = sb("mx8", [P, 2, 8])
        ix8 = sb("ix8", [P, 2, 8], U32)
        ov = sb("ov", [P, 8, NE * JEX])

        FB, KB, QB, GB, QT, KT, ITOK, AB, AC, AH = (work[:, j, :] for j in range(10))
        VTOK, UB, GS, YB, OSQ, OSD = AB, AC, KB, FB, KT, QT
        hidden0 = work[:, 0:6, :].rearrange("p a b -> p (a b)")[:, 0:NF * T].rearrange("p (f t) -> p f t", t=T)
        xrow = sig[:, :, :].rearrange("p a b -> p (a b)").rearrange("p (t d) -> p t d", t=TT)
        stackA = merged[:, 0, 0:P]
        stackB = merged[:, 1, 0:P]
        wrow = merged[:, 2:6, :].rearrange("p a b -> p (a b)").rearrange("p (l g s) -> p l g s", l=DEPTH, g=HB)
        htok = work[:, 0:2, :]
        xtok = work[:, 2:4, :]
        oacc = work[:, 4:6, :]
        ye = work[:, 6, :]
        hidE = work[:, 7:10, :].rearrange("p a b -> p (a b)")[:, 0:NF * CAP].rearrange("p (f s) -> p f s", s=CAP)
        xE = merged[:, :, :].rearrange("p a b -> p (a b)")[:, 0:KD * CAP].rearrange("p (k s) -> p k s", s=CAP)
        scf = sc[:, :, :, :].rearrange("p a b c -> p (a b c)")
        gwT = scf[:, 0:2 * T].rearrange("p (a t) -> p a t", t=T)
        sel = scf[:, 2 * T:2 * T + 4 * CAP].rearrange("p (a t s) -> p a t s", a=2, t=TT)
        g2bc = adacc[:, 0, :]
        fwbc = adacc[:, 1, :]

        s_small = sem("small_loaded")
        s_x = sem("x_loaded")
        s_panel = [sem(f"panel{i}_loaded") for i in range(RING)]
        s_adap = [sem(f"adapanel{i}_loaded") for i in range(2)]
        s_fw = sem("finalw_loaded")
        s_out = sem("out_stored")
        s_down = sem("down_panel_used")
        s_afree = sem("dve_adapanel_used")
        s_pool = sem("pool_step")
        s_const = sem("constants_ready")
        s_masks = sem("masks_ready")
        s_unit = sem("unit_ready")
        s_uA = sem("act_unit_emptied")
        s_uD = sem("dve_unit_emptied")
        s_ev = sem("event_ready")
        s_eA = sem("act_event_emptied")
        s_eD = sem("dve_event_emptied")
        s_cact = sem("cact_ready")
        s_lbsig = sem("lb_sigmoid_ready")
        s_mod = sem("modulation_ready")
        s_sq = sem("squares_ready")
        s_r = sem("rstd_ready")
        s_xr = sem("normed_chunk_ready")
        s_h = sem("h_chunk_ready")
        s_a = sem("act_step")
        s_v = sem("dve_step")
        s_sig = sem("sigmoid_ready")
        s_qk = sem("level_operands_ready")
        s_sc = sem("scores_zeroed")
        s_vst = sem("v_stat_ready")
        s_osq = sem("o_squares_ready")
        s_y = sem("branch_input_ready")
        s_mg = sem("merged_ready")
        s_sel = sem("selection_ready")
        s_gw = sem("gate_rows_ready")
        s_items = sem("items_ready")
        s_prob = sem("top2_prob_ready")
        s_zero = sem("expert_buffers_zeroed")
        s_rt = sem("routing_ready")
        s_fin = sem("final_rows_ready")
        s_fst = sem("final_stat_ready")

        block = ctx.enter_context(nc.Block())

        def panel(pos):
            return ring[:, pos % RING, :]

        def khalf(w, half, col):
            return w[half * 512:(half + 1) * 512, col:col + GROUP].rearrange("(k p) n -> p k n", p=P)

        def rows2(w, j):
            return w[j * 256:(j + 1) * 256, :].rearrange("(k p) n -> p k n", p=P)

        def mixer_sources(l):
            src = []
            for g in HEAD_GROUPS:
                src += [(4, khalf(w_in[l], h, COLS[g])) for h in range(2)]
            for b in BRANCHES:
                for gg in range(2):
                    src += [(4, khalf(w_in[l], h, GATE0[b] + gg * GROUP)) for h in range(2)]
                src += [(2, rows2(W_BR[b][l], j)) for j in range(2)]
            for gg in range(2):
                src += [(4, khalf(w_o[l], h, gg * GROUP)) for h in range(2)]
            return src

        def ffn_sources(w1, w3, w2):
            src = []
            for g in range(FF // GROUP):
                src += [(4, khalf(w, h, g * GROUP)) for w in (w1, w3) for h in range(2)]
            rest = FF // GROUP * GROUP
            src += [(8, w[:, rest:FF].rearrange("(k p) n -> p k n", p=P)) for w in (w1, w3)]
            return src + [(2, rows2(w2, j)) for j in range(NF // 2)]

        N_SMALL = 12

        @block.sync
        def _(sp):
            def load(pos, k, src):
                sp.dma_start(panel(pos).rearrange("p (k n) -> p k n", k=k), src).then_inc(s_panel[pos % RING], 16)

            xr = x[0].rearrange("(t p) d -> p t d", p=P)
            sp.dma_start(xrow, xr).then_inc(s_x, 16)
            for j in range(ADA_PANELS):
                s, q = j // 4, j % 4
                load(j, 2, ada_w[0][q * 256:(q + 1) * 256, s * D:(s + 1) * D].rearrange("(k p) n -> p k n", p=P))
            used = {"unit": s_unit, "down": s_down, "event": s_ev, "ada": s_afree}
            srcs = mixer_sources(0) + ffn_sources(ffn_w1[0], ffn_w3[0], ffn_w2[0]) + mixer_sources(1)
            assert len(PANELS) == ADA_PANELS + len(srcs) and len(PANELS) % RING == 0
            for n, (k, src) in enumerate(srcs):
                pos = ADA_PANELS + n
                if pos >= RING:
                    what, count = PANELS[pos - RING]
                    sp.wait_ge(used[what], count)
                load(pos, k, src)

            def item_sources(e):
                return ffn_sources(moe_w1[0, bass.ds(e, 1)].rearrange("a d f -> (a d) f"),
                                   moe_w3[0, bass.ds(e, 1)].rearrange("a d f -> (a d) f"),
                                   moe_w2[0, bass.ds(e, 1)].rearrange("a f d -> (a f) d"))

            def first_panels(i, e):
                for n, (k, src) in enumerate(item_sources(e)[:RING]):
                    sp.lower_ap(src)
                    if n < RING - 1:
                        sp.wait_ge(s_down, (i - 1) * (RING - 1) + (DOWN0 + n + 1))
                    else:
                        sp.wait_ge(s_ev, (i - 1) * 2 + (len(EVENTS) + 2))
                    load(n, k, src)

            def other_panels(i, e):
                for n, (k, src) in enumerate(item_sources(e)[RING:]):
                    sp.lower_ap(src)
                    unit = min(4 * (n // 4) + 4, NF)
                    sp.wait_ge(s_unit, i * EXP_UNITS + (len(UNITS) + unit))
                    load(n, k, src)

            for n, (k, src) in enumerate(item_sources(0)[:RING]):
                what, count = PANELS[len(PANELS) - RING + n]
                sp.wait_ge(used[what], count)
                load(n, k, src)
            with sp.Fori(0, NE - 1) as e:
                other_panels(e, e)
                first_panels(e + 1, e + 1)
            other_panels(NE - 1, NE - 1)
            sp.wait_ge(s_items, 1)
            n_items = sp.value_load(nitem[0:1, 0:1], min_val=NE, max_val=MAXI)
            with sp.If(n_items > NE):
                with sp.Fori(NE, n_items) as i:
                    e = sp.value_load(itemi[0:1, bass.ds(i, 1)], min_val=0, max_val=NE - 1)
                    first_panels(i, e)
                    other_panels(i, e)
            sp.wait_ge(s_fin, 2)
            sp.dma_start(out[0].rearrange("(t p) d -> p t d", p=P), oacc).then_inc(s_out, 16)
            sp.wait_ge(s_out, 16)

        @block.gpsimd
        def _(pool):
            step = 0

            def link(ins):
                nonlocal step
                step += 1
                ins.then_inc(s_pool, 1)
                pool.wait_ge(s_pool, step)

            pool.memset(ones[:, :], 1.0).then_inc(s_const, 1)
            link(pool.memset(ident[:, :], 0.0))
            pool.affine_select(out=ident[:, :], in_=ident[:, :], compare_op=ALU.not_equal, fill=1.0, base=0,
                               pattern=[[-1, P]], channel_multiplier=1).then_inc(s_const, 1)
            pool.iota(iotas[:, 0, :], pattern=[[0, P]], base=0, channel_multiplier=1).then_inc(s_const, 1)
            pool.iota(iotas[:, 1, :], pattern=[[1, P]], base=0, channel_multiplier=0).then_inc(s_const, 1)
            link(pool.memset(tri[:, :], 1.0))
            pool.affine_select(out=tri[:, :], in_=tri[:, :], compare_op=ALU.is_ge, fill=0.0, base=0,
                               pattern=[[1, P]], channel_multiplier=-1).then_inc(s_const, 1)
            pool.iota(slots[:, :], pattern=[[1, CAP]], base=1, channel_multiplier=0,
                      allow_small_or_imprecise_dtypes=True).then_inc(s_const, 1)
            pool.iota(small[:, 8:16], pattern=[[1, NE]], base=0, channel_multiplier=0,
                      allow_small_or_imprecise_dtypes=True).then_inc(s_const, 1)
            pool.iota(ov[:, 0, :], pattern=[[0, JEX], [1, NE]], base=1, channel_multiplier=0,
                      allow_small_or_imprecise_dtypes=True).then_inc(s_const, 1)
            pool.iota(ov[:, 1, :], pattern=[[CAP, JEX], [0, NE]], base=CAP, channel_multiplier=0,
                      allow_small_or_imprecise_dtypes=True).then_inc(s_const, 1)
            pool.memset(sc[:, :, :, :], 0.0).then_inc(s_sc, 1)
            for j in range(40):
                s, q = 2 + j // 4, j % 4
                if j >= 2:
                    pool.wait_ge(s_afree, ADA_PANELS + j - 1)
                pool.dma_start(adar[:, j % 2, :].rearrange("p (k n) -> p k n", k=2),
                               ada_w[s // 6][q * 256:(q + 1) * 256, (s % 6) * D:(s % 6 + 1) * D]
                               .rearrange("(k p) n -> p k n", p=P)).then_inc(s_adap[j % 2], 16)
                if j == 20:
                    pool.wait_ge(s_ev, EVENT_AT[(0, "o")] + 1)
                    pool.memset(sc[:, :, :, :], 0.0).then_inc(s_sc, 1)
            pool.wait_ge(s_ev, EVENT_AT[("ada", 11)] + 1)
            pool.dma_start(fwbc, final_norm_w.rearrange("(a d) -> a d", a=1).to_broadcast([P, D])).then_inc(s_fw, 16)
            pool.wait_ge(s_uD, emptied(UNITS, UNIT_AT[(1, "wo", 3)], "D"))
            pool.memset(oacc, 0.0).then_inc(s_zero, 1)
            pool.memset(ye, 0.0).then_inc(s_zero, 1)
            pool.memset(gwT[:, 0, :], 0.0).then_inc(s_zero, 1)

        @block.tensor
        def _(pe):
            units, events, panels = [0], [0], [ADA_PANELS]

            def open_unit(key):
                n = units[0]
                assert UNITS[n][0] == key, (key, UNITS[n])
                if n >= 4:
                    who = UNITS[n - 4][1]
                    pe.wait_ge(s_uA if who == "A" else s_uD, emptied(UNITS, n - 4, who))
                units[0] += 1
                return psU[n % 4]

            def open_event(key):
                n = events[0]
                assert EVENTS[n][0] == key, (key, EVENTS[n])
                if n >= 2:
                    who = EVENTS[n - 2][1]
                    pe.wait_ge(s_eA if who == "A" else s_eD, emptied(EVENTS, n - 2, who))
                events[0] += 1
                return psA[2 * (n % 2)], psA[2 * (n % 2) + 1]

            def take_panels(count):
                got = list(range(panels[0], panels[0] + count))
                panels[0] += count
                return got

            def arrived(pos):
                pe.wait_ge(s_panel[pos % RING], 16 * (pos // RING + 1))

            def mm(o, a, b, start, stop):
                return pe.matmul(o, a, b, start=start, stop=stop, skip_group_check=True)

            def project(key, rhs, split_first=None):
                lo, hi = take_panels(2)
                for j in range(2):
                    bank = open_unit(key(j))
                    if j == 0:
                        arrived(lo)
                    for m in range(2):
                        for k in range(KD):
                            if j == 0 and m == 0:
                                if k == 4:
                                    arrived(hi)
                                if split_first:
                                    split_first(k)
                            w = panel(lo if k < 4 else hi).rearrange("p (k n) -> p k n", k=4)
                            col = (2 * j + m) * P
                            last = mm(bank[:, m * T:(m + 1) * T], w[:, k % 4, col:col + P], rhs[:, k, :],
                                      k == 0, k == KD - 1)
                    last.then_inc(s_unit, 1)
                    yield j

            def project_rows(key):
                lo, hi = take_panels(2)
                for tt in range(TT):
                    bank = open_unit(key(tt))
                    if tt == 0:
                        arrived(lo)
                        arrived(hi)
                    for k in range(KD):
                        w = panel(lo if k < 4 else hi).rearrange("p (k n) -> p k n", k=4)
                        last = mm(bank[:, :], hT[:, k, tt * P:(tt + 1) * P], w[:, k % 4, :], k == 0, k == KD - 1)
                    last.then_inc(s_unit, 1)
                    yield tt

            def norm_stat(key, count):
                pe.wait_ge(s_sq, count)
                bank, _ = open_event(key)
                for k in range(KD):
                    last = mm(bank[:, 0:T], ones[:, :], merged[:, k, :], k == 0, k == KD - 1)
                last.then_inc(s_ev, 1)

            def ada_sum(s):
                pe.wait_ge(s_afree, 4 * (s + 1))
                bank, _ = open_event(("ada", s))
                for k in range(KD):
                    last = mm(bank[:, k:k + 1], adacc[:, s % 2, k * P:(k + 1) * P], ones[:, 0:1], True, True)
                last.then_inc(s_ev, 1)

            def level(l, j):
                if j == 0:
                    pe.wait_ge(s_uD, emptied(UNITS, UNIT_AT[(l, "q", 1)], "D"))
                else:
                    pe.wait_ge(s_qk, l * (NLEV - 1) + j)
                banks = open_event((l, "lev", j))
                ks, qs = (KB, QB) if j == 0 else (KT, QT)
                for tt in range(TT if j < NLEV - 1 else 1):
                    for h in range(HB):
                        s0 = h * T + tt * P
                        t0 = s0 if j < NLEV - 1 else h * T + P
                        last = mm(banks[tt][:, h * P:(h + 1) * P], ks[:, s0:s0 + P], qs[:, t0:t0 + P], True, True)
                last.then_inc(s_ev, 1)

            def sgu_mix(l):
                pe.wait_ge(s_uD, emptied(UNITS, UNIT_AT[(l, "v", 1)], "D"))
                banks = open_event((l, "sgu"))
                for g in range(HB):
                    for tt in range(TT):
                        col = (g % 2) * T + tt * P
                        last = mm(banks[g // 2][:, col:col + P], VTOK[:, tt * 512 + g * P:tt * 512 + (g + 1) * P],
                                  wT[:, l, g, :], True, True)
                last.then_inc(s_ev, 1)

            def attend(l):
                pe.wait_ge(s_eD, emptied(EVENTS, EVENT_AT[(l, "lev", NLEV - 1)], "D"))
                pe.wait_ge(s_uA, emptied(UNITS, UNIT_AT[(l, "i", 1)], "A"))
                banks = open_event((l, "o"))
                for h in range(HB):
                    v0, v1 = (ITOK[:, tt * 512 + h * P:tt * 512 + (h + 1) * P] for tt in range(TT))
                    col = (h % 2) * T
                    o = banks[h // 2]
                    mm(o[:, col:col + P], v0, sc[:, 0, h, :], True, True)
                    mm(o[:, col + P:col + T], v0, sc[:, 2, h, :], True, False)
                    last = mm(o[:, col + P:col + T], v1, sc[:, 1, h, :], False, True)
                last.then_inc(s_ev, 1)

            def head_stat(l):
                pe.wait_ge(s_osq, l + 1)
                banks = open_event((l, "ostat"))
                for j in range(2):
                    last = mm(banks[j][:, :], ones[:, :], OSQ[:, j * 512:(j + 1) * 512], True, True)
                last.then_inc(s_ev, 1)

            def mixer(l):
                if l == 0:
                    for s in range(2):
                        ada_sum(s)
                norm_stat((l, "norm1"), 2 * l + 1)

                def chunk(k):
                    pe.wait_ge(s_h, 2 * KD * l + k + 1)
                lev = 0
                for g in HEAD_GROUPS:
                    rows = g in ("i", "v")
                    run = project_rows(lambda j: (l, g, j)) if rows else \
                        project(lambda j: (l, g, j), hT, chunk if g == "f" else None)
                    for j in run:
                        if lev < NLEV and (g, j) not in (("f", 0), ("f", 1), ("q", 0), ("q", 1), ("ab", 0)):
                            level(l, lev)
                            lev += 1
                        if (g, j) == ("g", 0):
                            sgu_mix(l)
                            attend(l)
                for b in BRANCHES:
                    for gg in range(2):
                        for j in project(lambda j: (l, "gate" + b, 2 * gg + j), hT):
                            if b == "a" and gg == 0 and j == 0:
                                head_stat(l)
                    ps = take_panels(2)
                    src = {"a": AH, "c": UB, "b": YB}[b]
                    pe.wait_ge(s_y, 3 * l + {"a": 1, "c": 2, "b": 3}[b])
                    for j in range(4):
                        bank = open_unit((l, "y" + b, j))
                        if j == 0:
                            for pos in ps:
                                arrived(pos)
                        for m in range(2):
                            for k in range(4):
                                w = panel(ps[k // 2]).rearrange("p (k n) -> p k n", k=2)
                                col = (2 * j + m) * P
                                last = mm(bank[:, m * T:(m + 1) * T], w[:, k % 2, col:col + P],
                                          src[:, k * T:(k + 1) * T], k == 0, k == 3)
                        last.then_inc(s_unit, 1)
                    if l == 0 and b in ("a", "c"):
                        ada_sum({"a": 2, "c": 3}[b])

                def chunk_m(k):
                    if k % 2 == 0:
                        pe.wait_ge(s_mg, 8 * l + 4 + k // 2 + 1)
                for gg in range(2):
                    for _ in project(lambda j: (l, "wo", 2 * gg + j), merged, chunk_m if gg == 0 else None):
                        pass
                if l == 0:
                    ada_sum(4)
                norm_stat((l, "norm2"), 2 * l + 2)

            def hidden(key, rhs, width, arrive, panel_at, first_wait, after=None, open_=None):
                for f in range(NF):
                    g, m = f // 4, f % 4
                    full = g < FF // GROUP
                    bank = open_(f)
                    for which in range(2):
                        for k in range(KD):
                            if full:
                                n = 4 * g + 2 * which + k // 4
                                w = panel_at(n).rearrange("p (k n) -> p k n", k=4)[:, k % 4, m * P:(m + 1) * P]
                                fresh = m == 0 and k % 4 == 0
                            else:
                                n = 4 * g + which
                                w = panel_at(n).rearrange("p (k n) -> p k n", k=8)[:, k, m * P:(m + 1) * P]
                                fresh = m == 0 and k == 0
                            if fresh:
                                arrive(n)
                            if f == 0 and which == 0:
                                first_wait(k)
                            last = mm(bank[:, which * T:which * T + width], w, rhs[:, k, :], k == 0, k == KD - 1)
                    last.then_inc(s_unit, 1)
                    if after:
                        after(f)

            def dense_ffn():
                base = panels[0]
                take_panels(3 * RING)
                sums = {-(-8 * (n + 1) // 3) + 1: 5 + n for n in range(7)}

                def after(f):
                    if f in sums:
                        ada_sum(sums[f])
                hidden("ffn", hT, T, lambda n: arrived(base + n), lambda n: panel(base + n),
                       lambda k: pe.wait_ge(s_h, KD + k + 1), after, lambda f: open_unit(("ffn", f)))
                for key in ("down0", "down1"):
                    banks = open_event(key)
                    if key == "down0":
                        four = list(banks)
                    else:
                        four += list(banks)
                for j in range(NF // 2):
                    pos = base + 2 * RING + j
                    arrived(pos)
                    for kk in range(2):
                        f = 2 * j + kk
                        pe.wait_ge(s_uD, emptied(UNITS, UNIT_AT[("ffn", f)], "D"))
                        w = panel(pos).rearrange("p (k n) -> p k n", k=2)
                        for m in range(KD):
                            last = mm(four[m // 2][:, (m % 2) * T:(m % 2 + 1) * T], w[:, kk, m * P:(m + 1) * P],
                                      hidden0[:, f, :], f == 0 and m % 2 == 0, f == NF - 1)
                            if f == NF - 1 and m == 3:
                                last.then_inc(s_ev, 1)
                    last.then_inc(s_down if j < NF // 2 - 1 else s_ev, 1)

            pe.wait_ge(s_const, 2)
            pe.wait_ge(s_x, 16)
            for j in range(4):
                bank = open_unit(("x", j))
                for m in range(2):
                    for tt in range(TT):
                        last = pe.transpose(bank[:, m * T + tt * P:m * T + (tt + 1) * P],
                                            xrow[:, tt, (2 * j + m) * P:(2 * j + m + 1) * P], ident[:, :])
                last.then_inc(s_unit, 1)
            pe.wait_ge(s_small, 16 * N_SMALL)
            bank = open_unit(("vec", 0))
            pe.transpose(bank[:, 0:NA_ROWS], stackA[0:NA_ROWS, :], ident[0:NA_ROWS, 0:NA_ROWS])
            pe.transpose(bank[:, NA_ROWS:NA_ROWS + NB_ROWS], stackB[0:NB_ROWS, :],
                         ident[0:NB_ROWS, 0:NB_ROWS]).then_inc(s_unit, 1)
            for l in range(DEPTH):
                bank = open_unit(("wt", l))
                for g in range(HB):
                    last = pe.transpose(bank[:, g * P:(g + 1) * P], wrow[:, l, g, :], ident[:, :])
                last.then_inc(s_unit, 1)
            mixer(0)
            dense_ffn()
            mixer(1)

            bank = open_unit("logits")
            for tt in range(TT):
                for k in range(KD):
                    if tt == 0:
                        pe.wait_ge(s_h, 3 * KD + k + 1)
                    last = mm(bank[:, tt * NE:(tt + 1) * NE], hT[:, k, tt * P:(tt + 1) * P], rtw[:, k, :],
                              k == 0, k == KD - 1)
            last.then_inc(s_unit, 1)
            pe.wait_ge(s_rt, 1)
            bank = open_unit("rank")
            mm(bank[:, 0:NE], tri[:, :], route[:, 0, 0:NE], True, True)
            mm(bank[:, NE:2 * NE], ones[:, :], route[:, 0, 0:NE], True, False)
            mm(bank[:, NE:2 * NE], tri[:, :], route[:, 0, NE:2 * NE], False, True)
            mm(bank[:, 2 * NE:3 * NE], ones[:, :], route[:, 0, 0:NE], True, False)
            mm(bank[:, 2 * NE:3 * NE], ones[:, :], route[:, 0, NE:2 * NE], False, True).then_inc(s_unit, 1)
            for key, src in (("htok", hT), ("xtok", xT)):
                for j in range(4):
                    bank = open_unit((key, j))
                    tt, half = j // 2, j % 2
                    for m in range(4):
                        last = pe.transpose(bank[:, m * P:(m + 1) * P],
                                            src[:, 4 * half + m, tt * P:(tt + 1) * P], ident[:, :])
                    last.then_inc(s_unit, 1)
            pe.wait_ge(s_gw, 1)
            for j in range(2):
                bank = open_unit(("g2", j))
                for m in range(4):
                    last = mm(bank[:, m * P:(m + 1) * P], merged[:, 4 * j + m, 0:P], ident[:, :], True, True)
                last.then_inc(s_unit, 1)

            def gather(banks):
                for m in range(KD):
                    for tt in range(TT):
                        last = mm(banks[m // 4][:, (m % 4) * CAP:(m % 4 + 1) * CAP], htok[:, tt, m * P:(m + 1) * P],
                                  sel[:, 0, tt, :], tt == 0, tt == 1)
                last.then_inc(s_ev, 1)

            def turn_gates(bank):
                for tt in range(TT):
                    last = pe.transpose(bank[0:CAP, tt * P:(tt + 1) * P], sel[:, 1, tt, :], ident[:, :])
                last.then_inc(s_unit, 1)

            pe.wait_ge(s_sel, 1)
            pe.wait_ge(s_uA, emptied(UNITS, UNIT_AT[("htok", 3)], "A"))
            turn_gates(open_unit("sel0"))
            gather(open_event("gather0"))
            assert units[0] == len(UNITS) and events[0] == len(EVENTS) and panels[0] == len(PANELS)
            U0, E0 = len(UNITS), len(EVENTS)
            uD0, eA0, eD0 = (emptied(UNITS, U0, "D"), emptied(EVENTS, E0, "A"), emptied(EVENTS, E0, "D"))
            base = len(PANELS)

            def scatter(i):
                for j in range(4):
                    tt, half = j // 2, j % 2
                    n = NF + j
                    bank = psU[(U0 + n) % 4]
                    pe.wait_ge(s_uD, i * EXP_UNITS + (uD0 + n - 3))
                    mm(bank[:, :], gwT[0:CAP, 0, tt * P:(tt + 1) * P], ye[0:CAP, half * 512:(half + 1) * 512],
                       True, True).then_inc(s_unit, 1)

            pe.wait_ge(s_uA, emptied(UNITS, U0, "A"))
            pe.wait_ge(s_zero, 3)
            pe.wait_ge(s_items, 1)
            n_items = pe.value_load(nitem[0:1, 0:1], min_val=NE, max_val=MAXI)
            with pe.Fori(0, n_items) as i:
                def item_arrived(n):
                    pe.wait_ge(s_panel[n % RING], i * 48 + 16 * ((base + n) // RING + 1))

                def item_unit(f):
                    pe.wait_ge(s_uD, i * EXP_UNITS + (uD0 + (f - 3 if f > 3 else 0)))
                    return psU[(U0 + f) % 4]

                def tokens_in(k):
                    if k == 0:
                        pe.wait_ge(s_eA, i + eA0)
                hidden("item", xE, CAP, item_arrived, lambda n: panel(n), tokens_in, None, item_unit)
                scatter(i)
                pe.wait_ge(s_sel, i + 2)
                pe.wait_ge(s_uD, i * EXP_UNITS + (uD0 + NF + 1))
                turn_gates(psU[(U0 + NF + 4) % 4])
                pe.wait_ge(s_eA, i + eA0)
                gather((psA[2 * (E0 % 2)], psA[2 * (E0 % 2) + 1]))
                pair = (psA[2 * ((E0 + 1) % 2)], psA[2 * ((E0 + 1) % 2) + 1])
                pe.wait_ge(s_eD, i + eD0)
                for j in range(NF // 2):
                    item_arrived(2 * RING + j)
                    for kk in range(2):
                        f = 2 * j + kk
                        pe.wait_ge(s_uD, i * EXP_UNITS + (uD0 + f + 1))
                        w = panel(2 * RING + j).rearrange("p (k n) -> p k n", k=2)
                        for half in range(2):
                            last = mm(pair[half][0:CAP, :], hidE[:, f, :], w[:, kk, half * 512:(half + 1) * 512],
                                      f == 0, f == NF - 1)
                    last.then_inc(s_down if j < NF // 2 - 1 else s_ev, 1)
            pe.wait_ge(s_eD, n_items + eD0)
            pe.wait_ge(s_uD, n_items * EXP_UNITS + uD0)
            for j in range(4):
                tt, half = j // 2, j % 2
                mm(psU[(U0 + NF + j) % 4][:, :], gwT[0:CAP, 0, tt * P:(tt + 1) * P],
                   ye[0:CAP, half * 512:(half + 1) * 512], True, True).then_inc(s_unit, 1)

        @block.scalar
        def _(act):
            step = [0]

            def link(ins):
                step[0] += 1
                ins.then_inc(s_a, 1)
                act.wait_ge(s_a, step[0])

            def unit(key):
                n = UNIT_AT[key]
                act.wait_ge(s_unit, n + 1)
                return psU[n % 4]

            def event(key):
                n = EVENT_AT[key]
                act.wait_ge(s_ev, n + 1)
                return psA[2 * (n % 2)], psA[2 * (n % 2) + 1]

            def copy(o, i):
                return act.activation(o, i, ACT.Copy)

            small_loads = [
                (stackA[ADA_B:ADA_B + 96, :], ada_b.rearrange("l (r p) -> (l r) p", p=P)),
                (stackA[C_ROW:C_ROW + KD, :], c.rearrange("b (r p) -> (b r) p", p=P)),
                (stackA[LB_ROW:LB_ROW + 8, :], lb_logits.rearrange("l (r p) -> (l r) p", p=P)),
                (stackB[NMIX:NMIX + 16, :], norm_mix_w.rearrange("l (r p) -> (l r) p", p=P)),
                (stackB[NFFN:NFFN + 16, :], norm_ffn_w.rearrange("l (r p) -> (l r) p", p=P)),
                (stackB[CONV:CONV + 24, :], conv_w.rearrange("l w (r p) -> (l w r) p", p=P)),
                (stackB[HNW:HNW + 8, :], hgrn_norm_w.rearrange("l (r p) -> (l r) p", p=P)),
                (stackB[SNW:SNW + 8, :], sgu_norm_w.rearrange("l (r p) -> (l r) p", p=P)),
                (wrow.rearrange("p l g s -> p (l g) s"), sgu_w.rearrange("l g t s -> t (l g) s")),
                (sgub[:, :, :, :].rearrange("p l g t -> p (l g t)"),
                 sgu_b.rearrange("(a l) g t -> a (l g t)", a=1).to_broadcast([P, DEPTH * HB * P])),
                (rtw[:, :, :], router_w[0].rearrange("(k p) e -> p k e", p=P)),
                (rtb[:, :], router_b.to_broadcast([P, NE])),
            ]
            assert len(small_loads) == N_SMALL
            for dst, src in small_loads:
                act.dma_start(dst, src).then_inc(s_small, 16)

            for j in range(4):
                copy(xT[:, 2 * j:2 * j + 2, :].rearrange("p a b -> p (a b)"), unit(("x", j))[:, :]).then_inc(s_uA, 1)
            copy(vecs[:, :], unit(("vec", 0))[:, 0:NA_ROWS + NB_ROWS]).then_inc(s_uA, 1)
            act.wait_ge(s_uA, 5)
            act.activation(cact[:, :], vecs[:, C_ROW:C_ROW + KD], ACT.Sigmoid).then_inc(s_cact, 1)
            act.wait_ge(s_lbsig, 1)
            act.activation(lbs[:, 1, 0, :], lbs[:, 1, 1, :], ACT.Sigmoid).then_inc(s_cact, 1)
            act.wait_ge(s_uD, 2)

            def std(o, i, n):
                return act.activation(o, i, ACT.Sqrt, scale=1.0 / n, bias=eps[:, :])

            def norm(l, second):
                if second:
                    act.wait_ge(s_uD, emptied(UNITS, UNIT_AT[(l, "wo", 3)], "D"))
                elif l:
                    act.wait_ge(s_eD, emptied(EVENTS, EVENT_AT["down1"], "D"))
                act.activation(merged[:, :, :].rearrange("p a b -> p (a b)"),
                               xT[:, :, :].rearrange("p a b -> p (a b)"), ACT.Square).then_inc(s_sq, 1)
                bank, _ = event((l, "norm2" if second else "norm1"))
                std(rstd[:, :], bank[:, 0:T], D).then_inc(s_eA, 1)
                act.wait_ge(s_mod, 2 * l + 1 + second)
                for k in range(KD):
                    n = KD * (2 * l + second) + k
                    act.wait_ge(s_xr, n + 1)
                    sh = 24 * second + k
                    act.activation(hT[:, k, :], hT[:, k, :], ACT.Identity, scale=wm[:, l, second, k:k + 1],
                                   bias=mod[:, l, sh:sh + 1]).then_inc(s_h, 1)

            def half(buf, j):
                return buf[:, j * 512:(j + 1) * 512]

            def mixer(l):
                norm(l, 0)
                for g in HEAD_GROUPS:
                    for j in range(2):
                        if g == "ah":
                            continue
                        bank = unit((l, g, j))
                        if g == "f":
                            act.activation(half(FB, j), bank[:, :], ACT.Sigmoid)
                            act.activation(half(KB, j), bank[:, :], ACT.Sigmoid, scale=-1.0).then_inc(s_uA, 1)
                        elif g in ("q", "g"):
                            act.activation(sig[:, j, :], bank[:, :], ACT.Sigmoid).then_inc(s_sig, 1)
                        elif g == "v":
                            link(act.activation(sig[:, 2 + j, :], bank[:, :], ACT.Square, accum_out=vst[:, j:j + 1]))
                            std(vst[:, 2 + j:3 + j], vst[:, j:j + 1], 512).then_inc(s_vst, 1)
                        else:
                            if g == "u" and j == 0:
                                act.wait_ge(s_y, 3 * l + 1)
                            copy(half({"ab": AB, "ac": AC, "i": ITOK, "u": UB}[g], j), bank[:, :]).then_inc(s_uA, 1)
                        if (g, j) == ("g", 0):
                            banks = event((l, "o"))
                            act.activation(half(OSQ, 0), banks[0][:, :], ACT.Square)
                            act.activation(half(OSQ, 1), banks[1][:, :], ACT.Square).then_inc(s_osq, 1)
                for n, b in enumerate(BRANCHES):
                    for j in range(4):
                        bank = unit((l, "gate" + b, j))
                        if n == 0:
                            act.wait_ge(s_uD, emptied(UNITS, UNIT_AT[(l, "g", 1)], "D"))
                        elif n == 1:
                            act.wait_ge(s_uD, emptied(UNITS, UNIT_AT[(l, "ya", j)], "D"))
                        else:
                            act.wait_ge(s_mg, 8 * l + j + 1)
                        act.activation(sig[:, j, :], bank[:, :], ACT.Sigmoid).then_inc(s_uA, 1)
                        if n == 0 and j == 0:
                            banks = event((l, "ostat"))
                            std(half(OSD, 0), banks[0][:, :], P)
                            std(half(OSD, 1), banks[1][:, :], P).then_inc(s_eA, 1)
                norm(l, 1)

            mixer(0)
            for f in range(NF):
                bank = unit(("ffn", f))
                act.activation(sig[:, f % 4, 0:T], bank[:, 0:T], ACT.Sigmoid).then_inc(s_sig, 1)
            mixer(1)

            act.wait_ge(s_prob, 1)
            act.activation(cur[:, 2:4], cur[:, 0:2], ACT.Sigmoid)
            act.activation(cur[:, 4:6], cur[:, 0:2], ACT.Sigmoid, scale=-1.0).then_inc(s_prob, 1)
            for key, dst in (("htok", htok), ("xtok", xtok)):
                for j in range(4):
                    copy(dst[:, j // 2, (j % 2) * 512:(j % 2 + 1) * 512], unit((key, j))[:, :]).then_inc(s_uA, 1)
            for j in range(2):
                copy(g2bc[:, j * 512:(j + 1) * 512], unit(("g2", j))[:, :]).then_inc(s_uA, 1)

            def tokens(banks):
                for j in range(2):
                    last = copy(xE[:, 4 * j:4 * j + 4, :].rearrange("p a b -> p (a b)"), banks[j][:, 0:4 * CAP])
                last.then_inc(s_eA, 1)
            tokens(event("gather0"))
            U0, E0 = len(UNITS), len(EVENTS)
            act.wait_ge(s_items, 1)
            n_items = act.value_load(nitem[0:1, 0:1], min_val=NE, max_val=MAXI)
            with act.Fori(0, n_items) as i:
                for f in range(NF):
                    act.wait_ge(s_unit, i * EXP_UNITS + (U0 + f + 1))
                    act.activation(sig[:, f % 4, 0:CAP], psU[(U0 + f) % 4][:, 0:CAP], ACT.Sigmoid).then_inc(s_sig, 1)
                act.wait_ge(s_ev, i * 2 + (E0 + 1))
                tokens((psA[2 * (E0 % 2)], psA[2 * (E0 % 2) + 1]))
            for tt in range(TT):
                act.wait_ge(s_fst, tt + 1)
                act.activation(work[:, 7 + tt, :], oacc[:, tt, :], ACT.Square, accum_out=vst[:, tt:tt + 1]).then_inc(s_a, 1)
                step[0] += 1
                act.wait_ge(s_a, step[0])
                std(vst[:, 2 + tt:3 + tt], vst[:, tt:tt + 1], D).then_inc(s_vst, 1)

        @block.vector
        def _(dve):
            step = [0]

            def link(ins):
                step[0] += 1
                ins.then_inc(s_v, 1)

            def settle():
                dve.wait_ge(s_v, step[0])

            def unit(key):
                n = UNIT_AT[key]
                dve.wait_ge(s_unit, n + 1)
                return psU[n % 4]

            def unit_done(key):
                dve.wait_ge(s_uD, emptied(UNITS, UNIT_AT[key], "D"))

            def event(key):
                n = EVENT_AT[key]
                dve.wait_ge(s_ev, n + 1)
                return psA[2 * (n % 2)], psA[2 * (n % 2) + 1]

            TTN, TS, STT = dve.tensor_tensor, dve.tensor_scalar, dve.scalar_tensor_tensor
            BV = NA_ROWS

            link(dve.memset(eps[:, :], EPS))
            link(dve.memset(work[:, 4:6, :], 0.0))
            link(dve.memset(items[:, :, :], 0.0))
            dve.wait_ge(s_const, 9)
            xor = work[:, 0, 0:P].bitcast(I32)
            above = work[:, 1, 0:P]
            link(TTN(xor, iotas[:, 0, :], iotas[:, 1, :], ALU.bitwise_xor))
            link(TTN(above, iotas[:, 1, :], iotas[:, 0, :], ALU.is_gt))
            settle()
            for j in range(8):
                link(STT(work[:, 2, j * P:(j + 1) * P], xor, float(2 ** j), above, ALU.is_ge, ALU.mult))
            link(dve.tensor_copy(masks[:, 0, :], ident[:, :]))
            settle()
            for j in range(1, 8):
                a = work[:, 2, (j - 1) * P:j * P]
                link(TTN(masks[:, j, :], a, work[:, 2, j * P:(j + 1) * P], ALU.subtract))
            dve.wait_ge(s_cact, 1)
            link(TTN(cact[:, :], cact[:, :], vecs[:, C_ROW:C_ROW + KD], ALU.mult))
            TTN(lbs[:, 1, 1, :], vecs[:, LB_ROW + HB:LB_ROW + 2 * HB], vecs[:, LB_ROW:LB_ROW + HB],
                ALU.subtract).then_inc(s_lbsig, 1)
            link(dve.memset(lbs[:, 0, 1, :], 1.0))
            link(dve.memset(lbs[:, 0, 2, :], LB_FLOOR))
            for l in range(DEPTH):
                bank = unit(("wt", l))
                for g in range(HB):
                    ins = TTN(wT[:, l, g, :], bank[:, g * P:(g + 1) * P], tri[:, :], ALU.mult)
                ins.then_inc(s_uD, 1)
            dve.wait_ge(s_cact, 2)
            link(TS(lbs[:, 1, 0, :], lbs[:, 1, 0, :], 0.0, 1.0, ALU.max, ALU.min))
            settle()
            link(TS(lbs[:, 1, 1, :], lbs[:, 1, 0, :], -1.0, 1.0, ALU.mult, ALU.add))
            link(TS(lbs[:, 1, 2, :], lbs[:, 1, 0, :], LB_FLOOR, None, ALU.max))
            settle()

            def product(s, k):
                n = 4 * s + k // 2
                if s < 2:
                    src, ready, turn = ring[:, n, :], s_panel[n], 1
                else:
                    m = n - ADA_PANELS
                    src, ready, turn = adar[:, m % 2, :], s_adap[m % 2], m // 2 + 1
                src = src[:, (k % 2) * D:(k % 2 + 1) * D]
                acc = adacc[:, s % 2, :]
                if k % 2 == 0:
                    dve.wait_ge(ready, 16 * turn)
                    if k:
                        dve.wait_ge(s_afree, n)
                else:
                    settle()
                if k == 0:
                    if s >= 2:
                        dve.wait_ge(s_ev, EVENT_AT[("ada", s - 2)] + 1)
                    ins = TS(acc, src, cact[:, 0:1], None, ALU.mult)
                else:
                    ins = STT(acc, src, cact[:, k:k + 1], acc, ALU.mult, ALU.add)
                if k % 2:
                    ins.then_inc(s_afree, 1)
                else:
                    link(ins)

            def modulate(s):
                l, part = s // 6, s % 6
                bank, _ = event(("ada", s))
                dst = mod[:, l, 8 * part:8 * part + 8]
                TTN(dst, bank[:, 0:KD], vecs[:, ADA_B + 8 * s:ADA_B + 8 * s + 8], ALU.add).then_inc(s_eD, 1)
                if part in (1, 4):
                    second = part // 4
                    dve.wait_ge(s_eD, emptied(EVENTS, EVENT_AT[("ada", s)], "D"))
                    w = BV + (NFFN if second else NMIX) + KD * l
                    STT(wm[:, l, second, :], dst, 1.0, vecs[:, w:w + KD], ALU.add, ALU.mult).then_inc(s_mod, 1)

            def norm(l, second):
                dve.wait_ge(s_eA, emptied(EVENTS, EVENT_AT[(l, "norm2" if second else "norm1")], "A"))
                link(dve.reciprocal(rstd[:, :], rstd[:, :]))
                settle()
                for k in range(KD):
                    TTN(hT[:, k, :], xT[:, k, :], rstd[:, :], ALU.mult).then_inc(s_xr, 1)

            def half(buf, j):
                return buf[:, j * 512:(j + 1) * 512]

            def prepare(l, j):
                h = 2 ** (j - 1)
                F, G, q, k, qt, kt = (b.rearrange("p (n c h) -> p n c h", c=2, h=h) for b in (FB, GB, QB, KB, QT, KT))
                if j > 1:
                    dve.wait_ge(s_ev, EVENT_AT[(l, "lev", j - 1)] + 1)
                settle()
                if j == 1:
                    link(dve.tensor_copy(kt[:, :, 0, :], k[:, :, 0, :]))
                else:
                    link(TTN(kt[:, :, 0, :], k[:, :, 0, :], G[:, :, 0, :], ALU.mult))
                TTN(qt[:, :, 1, :], q[:, :, 1, :], F[:, :, 1, :], ALU.mult).then_inc(s_qk, 1)
                if j == NLEV - 1:
                    return
                n = 1024 // (2 * h)
                if j == 1:
                    link(dve.tensor_copy(G[:, :, 0, :], F[:, :, 1, :]))
                else:
                    link(TTN(G[:, :, 0, :], G[:, :, 0, :], F[:, :, 1, h - 1:h].to_broadcast([P, n, h]), ALU.mult))
                settle()
                dve.wait_ge(s_qk, l * (NLEV - 1) + j)
                link(TTN(F[:, :, 1, :], F[:, :, 1, :], F[:, :, 0, h - 1:h].to_broadcast([P, n, h]), ALU.mult))

            def keep_scores(l, j):
                banks = event((l, "lev", j))
                if j == 0:
                    dve.wait_ge(s_sc, l + 1)
                else:
                    dve.wait_ge(s_eD, emptied(EVENTS, EVENT_AT[(l, "lev", j - 1)], "D"))
                if j == NLEV - 1:
                    ins = dve.tensor_copy(sc[:, 2, :, :].rearrange("p h t -> p (h t)"), banks[0][:, :])
                else:
                    m = masks[:, j:j + 1, :].to_broadcast([P, HB, P])
                    for tt in range(TT):
                        ins = dve.copy_predicated(sc[:, tt, :, :], m, banks[tt][:, :].rearrange("p (h t) -> p h t", h=HB))
                ins.then_inc(s_eD, 1)

            def gated(l, g, j, dst):
                bank = unit((l, g, j))
                dve.wait_ge(s_sig, SIG0[l] + {"q": 0, "g": 2}[g] + j + 1)
                TTN(half(dst, j), sig[:, j, :], bank[:, :], ALU.mult).then_inc(s_uD, 1)

            SIG0 = [0, 4 + NF]

            def mixer(l):
                if l == 0:
                    for s in range(2):
                        for k in range(KD):
                            product(s, k)
                    for s in range(2):
                        modulate(s)
                norm(l, 0)
                settle()
                link(dve.memset(GB, 1.0))
                for h in range(HB):
                    dve.wait_ge(s_uA, emptied(UNITS, UNIT_AT[(l, "f", h // 2)], "A"))
                    o = slice(h * T, (h + 1) * T)
                    link(TS(FB[:, o], FB[:, o], lbs[:, l, 1, h:h + 1], lbs[:, l, 2, h:h + 1], ALU.mult, ALU.add))
                    link(TS(KB[:, o], KB[:, o], lbs[:, l, 1, h:h + 1], None, ALU.mult))
                for j in range(2):
                    gated(l, "q", j, QB)
                unit_done((l, "q", 1))
                prepare(l, 1)
                ada = [0]

                def more_ada(n):
                    if l == 0:
                        for _ in range(n):
                            if ada[0] < 24:
                                product(2 + ada[0] // 8, ada[0] % 8)
                                ada[0] += 1
                for j in range(2):
                    keep_scores(l, j)
                    more_ada(2)
                    prepare(l, j + 2)
                for j in range(2):
                    bank = unit((l, "ah", j))
                    dve.wait_ge(s_uA, emptied(UNITS, UNIT_AT[(l, "ac", j)], "A"))
                    TTN(half(AC, j), half(AC, j), bank[:, :], ALU.mult).then_inc(s_uD, 1)
                    keep_scores(l, j + 2)
                    more_ada(1)
                    prepare(l, j + 4)
                unit_done((l, "ah", 1))
                z, y = (b.rearrange("p (c t) -> p c t", t=T) for b in (AC, AH))
                cw = BV + CONV + 12 * l
                for cc in range(4):
                    link(TS(y[:, cc, :], z[:, cc, :], vecs[:, cw + cc:cw + cc + 1], None, ALU.mult))
                for back in (1, 2):
                    settle()
                    for cc in range(4):
                        w = cw + 4 * back + cc
                        link(STT(y[:, cc, back:T], z[:, cc, 0:T - back], vecs[:, w:w + 1], y[:, cc, back:T],
                                 ALU.mult, ALU.add))
                settle()
                TTN(AH, AH, AB, ALU.mult).then_inc(s_y, 1)
                for j in range(4, 6):
                    keep_scores(l, j)
                    prepare(l, j + 2)
                keep_scores(l, 6)
                for j in range(2):
                    bank = unit((l, "v", j))
                    dve.wait_ge(s_vst, 2 * l + j + 1)
                    link(dve.reciprocal(vst[:, 4 + j:5 + j], vst[:, 2 + j:3 + j]))
                    settle()
                    if j == 0:
                        dve.wait_ge(s_y, 3 * l + 1)
                    TS(half(VTOK, j), bank[:, :], vst[:, 4 + j:5 + j], None, ALU.mult).then_inc(s_uD, 1)
                    if j == 0:
                        prepare(l, 8)
                    keep_scores(l, 7 + j)
                more_ada(4)
                settle()
                dve.wait_ge(s_qk, (l + 1) * (NLEV - 1))
                gated(l, "g", 0, GS)
                banks = event((l, "sgu"))
                for g in range(HB):
                    w = BV + SNW + HB * l + g
                    ins = STT(YB[:, g * T:(g + 1) * T].rearrange("p (n t) -> p n t", n=TT),
                              banks[g // 2][:, (g % 2) * T:(g % 2 + 1) * T].rearrange("p (n t) -> p n t", n=TT),
                              vecs[:, w:w + 1], sgub[:, l, g:g + 1, :].to_broadcast([P, TT, P]), ALU.mult, ALU.add)
                    if g < HB - 1:
                        link(ins)
                ins.then_inc(s_eD, 1)
                dve.wait_ge(s_eD, emptied(EVENTS, EVENT_AT[(l, "sgu")], "D"))
                dve.wait_ge(s_uA, emptied(UNITS, UNIT_AT[(l, "u", 1)], "A"))
                TTN(UB, UB, YB, ALU.mult).then_inc(s_y, 1)
                gated(l, "g", 1, GS)
                dve.wait_ge(s_eA, emptied(EVENTS, EVENT_AT[(l, "ostat")], "A"))
                link(dve.reciprocal(OSD, OSD))
                settle()
                dve.wait_ge(s_y, 3 * l + 2)
                banks = event((l, "o"))
                link(TTN(half(YB, 0), half(OSD, 0), banks[0][:, :], ALU.mult))
                TTN(half(YB, 1), half(OSD, 1), banks[1][:, :], ALU.mult).then_inc(s_eD, 1)
                settle()
                dve.wait_ge(s_eD, emptied(EVENTS, EVENT_AT[(l, "o")], "D"))
                unit_done((l, "g", 1))
                for h in range(HB):
                    w = BV + HNW + HB * l + h
                    o = slice(h * T, (h + 1) * T)
                    ins = STT(YB[:, o], YB[:, o], vecs[:, w:w + 1], GS[:, o], ALU.mult, ALU.mult)
                ins.then_inc(s_y, 1)
                for n, b in enumerate(BRANCHES):
                    for j in range(4):
                        bank = unit((l, "y" + b, j))
                        dve.wait_ge(s_uA, emptied(UNITS, UNIT_AT[(l, "gate" + b, j)], "A"))
                        m = merged[:, 2 * j:2 * j + 2, :].rearrange("p a b -> p (a b)")
                        if n == 0:
                            TTN(m, sig[:, j, :], bank[:, :], ALU.mult).then_inc(s_uD, 1)
                        else:
                            TTN(sig[:, j, :], sig[:, j, :], bank[:, :], ALU.mult).then_inc(s_uD, 1)
                            unit_done((l, "y" + b, j))
                            if n == 2:
                                dve.wait_ge(s_mg, 8 * l + j + 1)
                            TTN(m, m, sig[:, j, :], ALU.add).then_inc(s_mg, 1)
                        more_ada(2)
                    if l == 0 and n < 2:
                        modulate(2 + n)
                dve.wait_ge(s_eD, emptied(EVENTS, EVENT_AT[("ada", 6 * l + 2)], "D"))
                for j in range(4):
                    bank = unit((l, "wo", j))
                    for m in range(2):
                        ch = 2 * j + m
                        ins = STT(xT[:, ch, :], bank[:, m * T:(m + 1) * T], mod[:, l, 16 + ch:17 + ch], xT[:, ch, :],
                                  ALU.mult, ALU.add)
                        if m:
                            ins.then_inc(s_uD, 1)
                        else:
                            link(ins)
                if l == 0:
                    assert ada[0] == 24
                    modulate(4)
                settle()
                unit_done((l, "wo", 3))
                norm(l, 1)

            mixer(0)
            turn = {-(-8 * (n + 1) // 3) + 2: 5 + n for n in range(7)}
            done = 0
            for f in range(NF):
                bank = unit(("ffn", f))
                dve.wait_ge(s_sig, 4 + f + 1)
                link(TTN(sig[:, f % 4, 0:T], sig[:, f % 4, 0:T], bank[:, 0:T], ALU.mult))
                settle()
                TTN(hidden0[:, f, :], sig[:, f % 4, 0:T], bank[:, T:2 * T], ALU.mult).then_inc(s_uD, 1)
                if f in turn:
                    modulate(turn[f])
                for _ in range(3):
                    if done < 56:
                        product(5 + done // 8, done % 8)
                        done += 1
            dve.wait_ge(s_eD, emptied(EVENTS, EVENT_AT[("ada", 11)], "D"))
            for e in range(2):
                banks = event(f"down{e}")
                for m in range(4):
                    ch = 4 * e + m
                    ins = STT(xT[:, ch, :], banks[m // 2][:, (m % 2) * T:(m % 2 + 1) * T],
                              mod[:, 0, 40 + ch:41 + ch], xT[:, ch, :], ALU.mult, ALU.add)
                    if m == 3:
                        ins.then_inc(s_eD, 1)
                    else:
                        link(ins)
            settle()
            dve.wait_ge(s_eD, emptied(EVENTS, EVENT_AT["down1"], "D"))
            mixer(1)

            iota8 = small[:, 8:16]

            def pair(row):
                return route[:, row, :].rearrange("p (t e) -> p t e", t=TT)
            SEL, LG, ONE, TWO, GATE, POS, IDX, TMP, CNT = 0, 1, 2, 3, 4, 5, 6, 7, 11
            bank = unit("logits")
            TTN(pair(LG), bank[:, 0:2 * NE].rearrange("p (t e) -> p t e", t=TT),
                rtb[:, :].rearrange("p (a e) -> p a e", a=1).to_broadcast([P, TT, NE]), ALU.add).then_inc(s_uD, 1)
            unit_done("logits")
            for tt in range(TT):
                link(dve.max(mx8[:, tt, :], route[:, LG, tt * NE:(tt + 1) * NE]))
            settle()
            TTN(cur[:, 0:2], mx8[:, :, 0], mx8[:, :, 1], ALU.subtract).then_inc(s_prob, 1)
            for tt in range(TT):
                link(dve.max_index(ix8[:, tt, :], mx8[:, tt, :], route[:, LG, tt * NE:(tt + 1) * NE]))
            settle()
            link(dve.tensor_copy(route[:, IDX, :], ix8[:, :, :].rearrange("p t e -> p (t e)")))
            settle()
            for tt in range(TT):
                for row, k in ((ONE, 0), (TWO, 1)):
                    link(TS(route[:, row, tt * NE:(tt + 1) * NE], iota8,
                            route[:, IDX, tt * NE + k:tt * NE + k + 1], None, ALU.is_equal))
            settle()
            TTN(route[:, SEL, :], route[:, ONE, :], route[:, TWO, :], ALU.add).then_inc(s_rt, 1)
            dve.wait_ge(s_prob, 2)
            for tt in range(TT):
                o = slice(tt * NE, (tt + 1) * NE)
                link(TS(route[:, TMP, o], route[:, ONE, o], cur[:, 2 + tt:3 + tt], None, ALU.mult))
            settle()
            for tt in range(TT):
                o = slice(tt * NE, (tt + 1) * NE)
                link(STT(route[:, GATE, o], route[:, TWO, o], cur[:, 4 + tt:5 + tt], route[:, TMP, o],
                         ALU.mult, ALU.add))
            dve.wait_ge(s_rt, 1)
            bank = unit("rank")
            link(TTN(route[:, POS, :], bank[:, 0:2 * NE], route[:, SEL, :], ALU.mult))
            dve.tensor_copy(route[:, CNT, 0:NE], bank[:, 2 * NE:3 * NE]).then_inc(s_uD, 1)
            unit_done("rank")
            NO = NE * JEX
            link(dve.memset(items[:, MAXI, 0:1], -1.0))
            link(dve.tensor_copy(items[:, 0:NE, 0], iota8))
            for j in range(JEX):
                link(TS(ov[:, 2, j * NE:(j + 1) * NE], route[:, CNT, 0:NE], float(CAP * (j + 1)), None, ALU.is_gt))
            src, shift = 2, 1
            while shift < NO:
                dst = 4 if src == 3 else 3
                settle()
                link(dve.tensor_copy(ov[:, dst, 0:shift], ov[:, src, 0:shift]))
                link(TTN(ov[:, dst, shift:NO], ov[:, src, shift:NO], ov[:, src, 0:NO - shift], ALU.add))
                src, shift = dst, 2 * shift
            settle()
            for r in range(REX):
                link(STT(ov[:, 5, :], ov[:, src, :], float(r + 1), ov[:, 2, :], ALU.is_equal, ALU.mult))
                settle()
                for col in range(2):
                    link(TTN(ov[:, 6 + col, :], ov[:, 5, :], ov[:, col, :], ALU.mult))
                settle()
                for col in range(2):
                    link(dve.reduce_sum(items[:, NE + r, col:col + 1], ov[:, 6 + col, :], AX_X))
            settle()
            link(TS(items[:, NE:MAXI, 0], items[:, NE:MAXI, 0], -1.0, None, ALU.add))
            link(TS(nitem[:, :], ov[:, src, NO - 1:NO], float(NE), None, ALU.add))
            settle()
            dve.tensor_copy(itemi[:, :], items[:, :, 0]).then_inc(s_items, 1)

            both = route[:, GATE:POS + 1, :].rearrange("p r (t e) -> p (r t) e", t=TT)
            picked = route[:, TMP:TMP + 3, :].rearrange("p r e -> p (r e)")[:, 0:4 * NE] \
                .rearrange("p (r e) -> p r e", e=NE)
            hot = route[:, 10, 0:NE]

            def select(row, last):
                if last is not None:
                    dve.wait_ge(s_sel, last)
                link(dve.tensor_copy(cur[:, 6:8], row))
                settle()
                link(TS(hot, iota8, cur[:, 6:7], None, ALU.is_equal))
                settle()
                link(TTN(picked, both, route[:, 10:11, 0:NE].to_broadcast([P, 4, NE]), ALU.mult))
                settle()
                link(dve.reduce_sum(cur[:, 0:4], picked, AX_X))
                settle()
                link(TS(cur[:, 4:6], cur[:, 2:4], cur[:, 7:8], None, ALU.subtract))
                settle()
                for tt in range(TT):
                    link(TS(sel[:, 0, tt, :], slots[:, :], cur[:, 4 + tt:5 + tt], None, ALU.is_equal))
                    ins = TS(sel[:, 1, tt, :], slots[:, :], cur[:, 4 + tt:5 + tt], cur[:, tt:tt + 1],
                             ALU.is_equal, ALU.mult)
                    if tt == 0:
                        link(ins)
                ins.then_inc(s_sel, 1)

            for ch in range(KD):
                ins = TS(merged[:, ch, 0:P], ones[:, :], mod[:, 1, 40 + ch:41 + ch], None, ALU.mult)
            ins.then_inc(s_gw, 1)
            select(items[:, 0, :], None)
            bank = unit("sel0")
            dve.tensor_copy(gwT[0:CAP, 1, :], bank[0:CAP, 0:T]).then_inc(s_uD, 1)
            dve.wait_ge(s_zero, 3)
            dve.wait_ge(s_items, 1)
            U0, E0 = len(UNITS), len(EVENTS)
            uD0 = emptied(UNITS, U0, "D")
            sig0 = 2 * 4 + NF
            n_items = dve.value_load(nitem[0:1, 0:1], min_val=NE, max_val=MAXI)
            before = step[0]
            STEPS = NF + 10
            with dve.Fori(0, n_items) as i:
                n_link = [0]

                def ilink(ins):
                    n_link[0] += 1
                    ins.then_inc(s_v, 1)

                def isettle():
                    dve.wait_ge(s_v, i * STEPS + (before + n_link[0]))
                link, settle = ilink, isettle
                for f in range(NF):
                    bank = psU[(U0 + f) % 4]
                    dve.wait_ge(s_unit, i * EXP_UNITS + (U0 + f + 1))
                    dve.wait_ge(s_sig, i * NF + (sig0 + f + 1))
                    link(TTN(sig[:, f % 4, 0:CAP], sig[:, f % 4, 0:CAP], bank[:, 0:CAP], ALU.mult))
                    settle()
                    TTN(hidE[:, f, :], sig[:, f % 4, 0:CAP], bank[:, T:T + CAP], ALU.mult).then_inc(s_uD, 1)
                    if f == 1:
                        select(items[:, bass.ds(i + 1, 1), :].rearrange("p a b -> p (a b)"), i + 1)
                for j in range(4):
                    tt, part = j // 2, j % 2
                    n = NF + j
                    dve.wait_ge(s_unit, i * EXP_UNITS + (U0 + n + 1))
                    o = oacc[:, tt, part * 512:(part + 1) * 512]
                    TTN(o, o, psU[(U0 + n) % 4][:, :], ALU.add).then_inc(s_uD, 1)
                link(dve.tensor_copy(gwT[0:CAP, 0, :], gwT[0:CAP, 1, :]))
                settle()
                n = NF + 4
                dve.wait_ge(s_unit, i * EXP_UNITS + (U0 + n + 1))
                dve.tensor_copy(gwT[0:CAP, 1, :], psU[(U0 + n) % 4][0:CAP, 0:T]).then_inc(s_uD, 1)
                dve.wait_ge(s_ev, i * 2 + (E0 + 2))
                pair_ = (psA[2 * ((E0 + 1) % 2)], psA[2 * ((E0 + 1) % 2) + 1])
                link(dve.tensor_copy(ye[0:CAP, 0:512], pair_[0][0:CAP, :]))
                dve.tensor_copy(ye[0:CAP, 512:1024], pair_[1][0:CAP, :]).then_inc(s_eD, 1)
                assert n_link[0] == STEPS
            dve.wait_ge(s_v, n_items * STEPS + before)
            dve.wait_ge(s_uD, n_items * EXP_UNITS + uD0)
            for j in range(4):
                tt, part = j // 2, j % 2
                dve.wait_ge(s_unit, n_items * EXP_UNITS + (U0 + j + 1))
                o = oacc[:, tt, part * 512:(part + 1) * 512]
                TTN(o, o, psU[(U0 + NF + j) % 4][:, :], ALU.add).then_inc(s_uD, 1)
            dve.wait_ge(s_uD, n_items * EXP_UNITS + (uD0 + 4))
            dve.wait_ge(s_uA, emptied(UNITS, len(UNITS), "A"))
            dve.wait_ge(s_fw, 16)
            for tt in range(TT):
                TTN(oacc[:, tt, :], oacc[:, tt, :], g2bc, ALU.mult).then_inc(s_gw, 1)
            for tt in range(TT):
                dve.wait_ge(s_gw, 2 + tt)
                TTN(oacc[:, tt, :], oacc[:, tt, :], xtok[:, tt, :], ALU.add).then_inc(s_fst, 1)
            for tt in range(TT):
                dve.wait_ge(s_vst, 2 * TT + tt + 1)
                dve.reciprocal(vst[:, 4 + tt:5 + tt], vst[:, 2 + tt:3 + tt]).then_inc(s_gw, 1)
                dve.wait_ge(s_gw, 4 + tt)
                STT(oacc[:, tt, :], oacc[:, tt, :], vst[:, 4 + tt:5 + tt], fwbc, ALU.mult,
                    ALU.mult).then_inc(s_fin, 1)


_INS = ["x", "c", "ada_w", "ada_b", "norm_mix_w", "norm_ffn_w", "w_in", "conv_w", "hgrn_lb_logits", "hgrn_norm_w",
        "sgu_norm_w", "sgu_w", "sgu_b", "w_br_a", "w_br_b", "w_br_c", "w_o", "ffn_w1", "ffn_w3", "ffn_w2",
        "moe_router_w", "moe_router_b", "moe_w1", "moe_w3", "moe_w2", "final_norm_w"]


def kernel(**inputs):
    import numpy as _np
    import concourse.bacc as _bacc
    from concourse import mybir as _mybir
    from concourse.bass_utils import run_bass_kernel_spmd as _run

    nc = _bacc.Bacc("TRN2", target_bir_lowering=False, num_devices=1)
    arrays, args = {}, []
    for name in _INS:
        a = _np.ascontiguousarray(inputs[name])
        arrays[f"in_{name}_dram"] = a
        args.append(nc.dram_tensor(f"in_{name}_dram", a.shape, _mybir.dt.from_np(a.dtype), kind="ExternalInput").ap())
    o = nc.dram_tensor("out_0_dram", (1, T, D), F32, kind="ExternalOutput").ap()
    program(nc, *args, o)
    r = _run(nc, [arrays], core_ids=[0])
    return r.results[0]["out_0_dram"]
```

```python
from contextlib import ExitStack

import concourse.bass as bass
from concourse import mybir

P = 128
F32 = mybir.dt.float32
F32R = mybir.dt.float32r
I32 = mybir.dt.int32
U32 = mybir.dt.uint32
U8 = mybir.dt.uint8
ALU = mybir.AluOpType
ACT = mybir.ActivationFunctionType
AX_X = mybir.AxisListType.X

T = 256
TT = T // P
D = 1024
KD = D // P
HB = 4
FF = 2816
NF = FF // P
NE = 8
DEPTH = 2
EPS = 1e-6
LB_FLOOR = 1e-30
GROUP = 512
RING = 11
PANEL = 2048
NLEV = 9

CAP = 104
JEX = -(-T // CAP) - 1
REX = (2 * T) // (CAP + 1)
MAXI = NE + REX

COLS = {n: 512 * c for c, n in enumerate(["ab", "ac", "ah", "q", "f", "i", "g", "u", "v"])}
GATE0 = {"a": 4608, "b": 5632, "c": 6656}
HEAD_GROUPS = ["f", "q", "ab", "ac", "ah", "i", "v", "u", "g"]
BRANCHES = ["a", "c", "b"]

ADA_B, C_ROW, LB_ROW, NA_ROWS = 0, 96, 104, 112
NMIX, NFFN, CONV, HNW, SNW, NB_ROWS = 0, 16, 32, 56, 64, 72

ADA_PANELS = 8
DOWN0 = NF // 2 - 1

PIECE = 1024
GROUPS = [list(range(4 * g, min(4 * g + 4, NF))) for g in range(-(-NF // 4))]
HID_PIECES = [8 if len(g) == 4 else 4 for g in GROUPS]
HID = sum(HID_PIECES)
NPC = HID + NF
RAW = 11
SPL = 6
AHEAD = SPL - 1
USED0 = SPL
assert NPC % RAW == 0 and NPC % SPL == 0 and NPC % 3 == 0
G_END = [sum(HID_PIECES[:g + 1]) for g in range(len(GROUPS))]
G_W1 = [G_END[g] - HID_PIECES[g] // 2 for g in range(len(GROUPS))]
GATHER_AT = HID + 8


def low_part(n):
    return ("G", n // 3 + 1) if n % 3 == 2 else ("V", n - n // 3 + (1 if n % 3 < 2 else 0))


LOWS = {"V": 2 * NPC // 3, "G": NPC // 3}


def unit_plan():
    plan = [(("x", j), "A") for j in range(4)] + [(("vec", 0), "A"), (("wt", 0), "D"), (("wt", 1), "D")]
    for l in range(DEPTH):
        for g in HEAD_GROUPS:
            plan += [((l, g, j), "A" if g in ("f", "ab", "ac", "i", "u") else "D") for j in range(2)]
        for b in BRANCHES:
            plan += [((l, "gate" + b, j), "A") for j in range(4)]
            plan += [((l, "y" + b, j), "D") for j in range(4)]
        plan += [((l, "wo", j), "D") for j in range(4)]
        if l == 0:
            plan += [(("ffn", j), "D") for j in range(NF)]
    plan += [("logits", "D"), ("rank", "D")]
    plan += [(("htok", j), "A") for j in range(4)] + [(("xtok", j), "A") for j in range(4)]
    plan += [(("g2", j), "A") for j in range(2)] + [("sel0", "gates")]
    return plan


def event_plan():
    plan = [(("ada", 0), "D"), (("ada", 1), "D")]
    for l in range(DEPTH):
        plan += [((l, "norm1"), "A")] + [((l, "lev", j), "D") for j in range(NLEV)]
        plan += [((l, "sgu"), "D"), ((l, "o"), "D"), ((l, "ostat"), "A")]
        if l == 0:
            plan += [(("ada", s), "D") for s in (2, 3, 4)]
        plan += [((l, "norm2"), "A")]
        if l == 0:
            plan += [(("ada", s), "D") for s in range(5, 12)]
            plan += [("down0", "D"), ("down1", "D")]
    plan += [("gather0", "tokens")]
    return plan


def panel_plan():
    plan = [("ada", j + 1) for j in range(ADA_PANELS)]
    down = 0
    for l in range(DEPTH):
        for g in HEAD_GROUPS:
            plan += [("unit", UNIT_AT[(l, g, 1)] + 1)] * 2
        for b in BRANCHES:
            plan += [("unit", UNIT_AT[(l, "gate" + b, 1)] + 1)] * 2 + [("unit", UNIT_AT[(l, "gate" + b, 3)] + 1)] * 2
            plan += [("unit", UNIT_AT[(l, "y" + b, 3)] + 1)] * 2
        plan += [("unit", UNIT_AT[(l, "wo", 1)] + 1)] * 2 + [("unit", UNIT_AT[(l, "wo", 3)] + 1)] * 2
        if l == 0:
            for g in range(FF // GROUP):
                plan += [("unit", UNIT_AT[("ffn", 4 * g + 3)] + 1)] * 4
            plan += [("unit", UNIT_AT[("ffn", NF - 1)] + 1)] * 2
            plan += [("down", j + 1) for j in range(NF // 2 - 1)] + [("event", EVENT_AT["down1"] + 1)]
    return plan


UNITS = unit_plan()
EVENTS = event_plan()
UNIT_AT = {k: n for n, (k, _) in enumerate(UNITS)}
EVENT_AT = {k: n for n, (k, _) in enumerate(EVENTS)}


PANELS = panel_plan()


def emptied(plan, upto, who):
    return sum(1 for _, w in plan[:upto + 1] if w == who)


def program(nc, x, c, ada_w, ada_b, norm_mix_w, norm_ffn_w, w_in, conv_w, lb_logits, hgrn_norm_w,
            sgu_norm_w, sgu_w, sgu_b, w_br_a, w_br_b, w_br_c, w_o, ffn_w1, ffn_w3, ffn_w2,
            router_w, router_b, moe_w1, moe_w3, moe_w2, final_norm_w, out):
    W_BR = {"a": w_br_a, "b": w_br_b, "c": w_br_c}
    with ExitStack() as ctx:
        def sb(name, shape, dt=F32):
            return ctx.enter_context(nc.sbuf_tensor(name, shape, dt))

        def sem(name):
            return ctx.enter_context(nc.semaphore(name))

        psU = [ctx.enter_context(nc.psum_tensor(f"psU{i}", [P, 512], F32)) for i in range(4)]
        psA = [ctx.enter_context(nc.psum_tensor(f"psA{i}", [P, 512], F32)) for i in range(4)]

        T_BANKS = [psA[2 * (EVENT_AT["gather0"] % 2) + j] for j in range(2)]
        Y_BANKS = [psA[2 * ((EVENT_AT["gather0"] + 1) % 2) + j] for j in range(2)]

        with ExitStack() as dense:
            ring, adar, hT, merged = (dense.enter_context(nc.sbuf_tensor(n, shape, F32)) for n, shape in (
                ("ring", [P, RING, PANEL]), ("adar", [P, 2, PANEL]), ("hT", [P, KD, T]), ("merged", [P, KD, T])))
        moe = [("raw", [P, RAW, PIECE], F32), ("split", [P, SPL, 2, PIECE], F32R),
               ("hidE", [P, 2, NF, CAP], F32R), ("xE", [P, 2, KD, CAP], F32R)]
        raw, split, hidE, xE = (sb(*m) for m in moe)
        pad = (RING + 4) * PANEL - RAW * PIECE - 2 * SPL * PIECE - 2 * (NF + KD) * CAP
        sb("pad", [P, pad])
        adacc = sb("adacc", [P, 2, D])
        xT = sb("xT", [P, KD, T])
        sig = sb("sig", [P, 4, 512])
        work = sb("work", [P, 10, 1024])
        sc = sb("sc", [P, 3, HB, P])
        masks = sb("masks", [P, NLEV - 1, P], U8)
        wT = sb("wT", [P, DEPTH, HB, P])
        sgub = sb("sgub", [P, DEPTH, HB, P])
        vecs = sb("vecs", [P, NA_ROWS + NB_ROWS])
        mod = sb("mod", [P, DEPTH, 48])
        wm = sb("wm", [P, DEPTH, 2, KD])
        cact = sb("cact", [P, KD])
        lbs = sb("lbs", [P, DEPTH, 3, HB])
        ident = sb("ident", [P, P])
        ones = sb("ones", [P, P])
        tri = sb("tri", [P, P])
        rstd = sb("rstd", [P, T])
        vst = sb("vst", [P, 8])
        eps = sb("eps", [P, 1])
        small = sb("small", [P, 16])
        iotas = sb("iotas", [P, 2, P], I32)
        rtw = sb("rtw", [P, KD, NE])
        rtb = sb("rtb", [P, NE])
        route = sb("route", [P, 12, 2 * NE])
        cur = sb("cur", [P, 8])
        slots = sb("slots", [P, CAP])
        items = sb("items", [P, MAXI + 1, 2])
        itemi = sb("itemi", [P, MAXI + 1], I32)
        nitem = sb("nitem", [P, 1], I32)
        mx8 = sb("mx8", [P, 2, 8])
        ix8 = sb("ix8", [P, 2, 8], U32)
        ov = sb("ov", [P, 8, NE * JEX])

        FB, KB, QB, GB, QT, KT, ITOK, AB, AC, AH = (work[:, j, :] for j in range(10))
        VTOK, UB, GS, YB, OSQ, OSD = AB, AC, KB, FB, KT, QT
        hidden0 = work[:, 0:6, :].rearrange("p a b -> p (a b)")[:, 0:NF * T].rearrange("p (f t) -> p f t", t=T)
        xrow = sig[:, :, :].rearrange("p a b -> p (a b)").rearrange("p (t d) -> p t d", t=TT)
        stackA = merged[:, 0, 0:P]
        stackB = merged[:, 1, 0:P]
        wrow = merged[:, 2:6, :].rearrange("p a b -> p (a b)").rearrange("p (l g s) -> p l g s", l=DEPTH, g=HB)
        htok = work[:, 0:2, :]
        xtok = work[:, 2:4, :]
        oacc = work[:, 4:6, :]
        ye = work[:, 6, :]
        scf = sc[:, :, :, :].rearrange("p a b c -> p (a b c)")
        gwT = scf[:, 0:2 * T].rearrange("p (a t) -> p a t", t=T)
        sel = scf[:, 2 * T:2 * T + 4 * CAP].rearrange("p (a t s) -> p a t s", a=2, t=TT)
        g2bc = adacc[:, 0, :]
        fwbc = adacc[:, 1, :]

        s_small = sem("small_loaded")
        s_x = sem("x_loaded")
        s_panel = [sem(f"panel{i}_loaded") for i in range(RING)]
        s_adap = [sem(f"adapanel{i}_loaded") for i in range(2)]
        s_fw = sem("finalw_loaded")
        s_out = sem("out_stored")
        s_down = sem("down_panel_used")
        s_afree = sem("dve_adapanel_used")
        s_pool = sem("pool_step")
        s_const = sem("constants_ready")
        s_masks = sem("masks_ready")
        s_unit = sem("unit_ready")
        s_uA = sem("act_unit_emptied")
        s_uD = sem("dve_unit_emptied")
        s_ev = sem("event_ready")
        s_eA = sem("act_event_emptied")
        s_eD = sem("dve_event_emptied")
        s_cact = sem("cact_ready")
        s_lbsig = sem("lb_sigmoid_ready")
        s_mod = sem("modulation_ready")
        s_sq = sem("squares_ready")
        s_r = sem("rstd_ready")
        s_xr = sem("normed_chunk_ready")
        s_h = sem("h_chunk_ready")
        s_a = sem("act_step")
        s_v = sem("dve_step")
        s_sig = sem("sigmoid_ready")
        s_qk = sem("level_operands_ready")
        s_sc = sem("scores_zeroed")
        s_vst = sem("v_stat_ready")
        s_osq = sem("o_squares_ready")
        s_y = sem("branch_input_ready")
        s_mg = sem("merged_ready")
        s_sel = sem("selection_ready")
        s_gw = sem("gate_rows_ready")
        s_items = sem("items_ready")
        s_prob = sem("top2_prob_ready")
        s_zero = sem("expert_buffers_zeroed")
        s_rt = sem("routing_ready")
        s_fin = sem("final_rows_ready")
        s_fst = sem("final_stat_ready")
        s_raw = [sem(f"piece{i}_loaded") for i in range(RAW)]
        s_hi = sem("act_high_parts")
        s_lo = {"V": sem("dve_low_parts"), "G": sem("pool_low_parts")}
        s_used = sem("pieces_used")
        s_silu = sem("hidden_sigmoid_rows")
        s_hrow = sem("hidden_rows_ready")
        s_turn = sem("hidden_rows_turned")
        s_hhi = sem("hidden_high_ready")
        s_hlo = sem("hidden_low_ready")
        s_gath = sem("tokens_gathered")
        s_xhi = sem("tokens_high_ready")
        s_xlo = sem("tokens_low_ready")
        s_sct = sem("scatter_results")
        s_add = sem("scatter_added")
        s_gate = sem("gate_columns_ready")
        s_ye = sem("expert_rows_ready")

        block = ctx.enter_context(nc.Block())

        def panel(pos):
            return ring[:, pos % RING, :]

        def khalf(w, half, col):
            return w[half * 512:(half + 1) * 512, col:col + GROUP].rearrange("(k p) n -> p k n", p=P)

        def rows2(w, j):
            return w[j * 256:(j + 1) * 256, :].rearrange("(k p) n -> p k n", p=P)

        def mixer_sources(l):
            src = []
            for g in HEAD_GROUPS:
                src += [(4, khalf(w_in[l], h, COLS[g])) for h in range(2)]
            for b in BRANCHES:
                for gg in range(2):
                    src += [(4, khalf(w_in[l], h, GATE0[b] + gg * GROUP)) for h in range(2)]
                src += [(2, rows2(W_BR[b][l], j)) for j in range(2)]
            for gg in range(2):
                src += [(4, khalf(w_o[l], h, gg * GROUP)) for h in range(2)]
            return src

        def ffn_sources(w1, w3, w2):
            src = []
            for g in range(FF // GROUP):
                src += [(4, khalf(w, h, g * GROUP)) for w in (w1, w3) for h in range(2)]
            rest = FF // GROUP * GROUP
            src += [(8, w[:, rest:FF].rearrange("(k p) n -> p k n", p=P)) for w in (w1, w3)]
            return src + [(2, rows2(w2, j)) for j in range(NF // 2)]

        N_SMALL = 12

        @block.sync
        def _(sp):
            def load(pos, k, src):
                sp.dma_start(panel(pos).rearrange("p (k n) -> p k n", k=k), src).then_inc(s_panel[pos % RING], 16)

            xr = x[0].rearrange("(t p) d -> p t d", p=P)
            sp.dma_start(xrow, xr).then_inc(s_x, 16)
            for j in range(ADA_PANELS):
                s, q = j // 4, j % 4
                load(j, 2, ada_w[0][q * 256:(q + 1) * 256, s * D:(s + 1) * D].rearrange("(k p) n -> p k n", p=P))
            used = {"unit": s_unit, "down": s_down, "event": s_ev, "ada": s_afree}
            srcs = mixer_sources(0) + ffn_sources(ffn_w1[0], ffn_w3[0], ffn_w2[0]) + mixer_sources(1)
            assert len(PANELS) == ADA_PANELS + len(srcs) and len(PANELS) % RING == 0
            for n, (k, src) in enumerate(srcs):
                pos = ADA_PANELS + n
                if pos >= RING:
                    what, count = PANELS[pos - RING]
                    sp.wait_ge(used[what], count)
                load(pos, k, src)

            def item_sources(e):
                w1, w3 = (w[0, bass.ds(e, 1)].rearrange("a d f -> (a d) f") for w in (moe_w1, moe_w3))
                w2 = moe_w2[0, bass.ds(e, 1)].rearrange("a f d -> (a f) d")
                src = []
                for g, tiles in enumerate(GROUPS):
                    k = PIECE // (P * len(tiles))
                    cols = slice(tiles[0] * P, (tiles[-1] + 1) * P)
                    src += [(k, w[q * k * P:(q + 1) * k * P, cols].rearrange("(k p) n -> p k n", p=P))
                            for w in (w1, w3) for q in range(KD // k)]
                return src + [(1, w2[f * P:(f + 1) * P, :].rearrange("(k p) n -> p k n", p=P)) for f in range(NF)]

            def load_piece(n, k, src):
                sp.dma_start(raw[:, n % RAW, :].rearrange("p (k n) -> p k n", k=k), src).then_inc(s_raw[n % RAW], 16)

            def first_pieces(i, e):
                for n, (k, src) in enumerate(item_sources(e)[:RAW]):
                    sp.lower_ap(src)
                    who, count = low_part(NPC - RAW + n)
                    sp.wait_ge(s_lo[who], (i - 1) * LOWS[who] + count)
                    load_piece(n, k, src)

            def other_pieces(i, e):
                for n, (k, src) in list(enumerate(item_sources(e)))[RAW:]:
                    sp.lower_ap(src)
                    who, count = low_part(n - RAW)
                    sp.wait_ge(s_lo[who], i * LOWS[who] + count)
                    load_piece(n, k, src)

            for n, (k, src) in enumerate(item_sources(0)[:RAW]):
                what, count = PANELS[len(PANELS) - RING + n * PIECE // PANEL]
                sp.wait_ge(used[what], count)
                load_piece(n, k, src)
            with sp.Fori(0, NE - 1) as e:
                other_pieces(e, e)
                first_pieces(e + 1, e + 1)
            other_pieces(NE - 1, NE - 1)
            sp.wait_ge(s_items, 1)
            n_items = sp.value_load(nitem[0:1, 0:1], min_val=NE, max_val=MAXI)
            with sp.If(n_items > NE):
                with sp.Fori(NE, n_items) as i:
                    e = sp.value_load(itemi[0:1, bass.ds(i, 1)], min_val=0, max_val=NE - 1)
                    first_pieces(i, e)
                    other_pieces(i, e)
            sp.wait_ge(s_fin, 2)
            sp.dma_start(out[0].rearrange("(t p) d -> p t d", p=P), oacc).then_inc(s_out, 16)
            sp.wait_ge(s_out, 16)

        @block.gpsimd
        def _(pool):
            step = 0

            def link(ins):
                nonlocal step
                step += 1
                ins.then_inc(s_pool, 1)
                pool.wait_ge(s_pool, step)

            pool.memset(ones[:, :], 1.0).then_inc(s_const, 1)
            link(pool.memset(ident[:, :], 0.0))
            pool.affine_select(out=ident[:, :], in_=ident[:, :], compare_op=ALU.not_equal, fill=1.0, base=0,
                               pattern=[[-1, P]], channel_multiplier=1).then_inc(s_const, 1)
            pool.iota(iotas[:, 0, :], pattern=[[0, P]], base=0, channel_multiplier=1).then_inc(s_const, 1)
            pool.iota(iotas[:, 1, :], pattern=[[1, P]], base=0, channel_multiplier=0).then_inc(s_const, 1)
            link(pool.memset(tri[:, :], 1.0))
            pool.affine_select(out=tri[:, :], in_=tri[:, :], compare_op=ALU.is_ge, fill=0.0, base=0,
                               pattern=[[1, P]], channel_multiplier=-1).then_inc(s_const, 1)
            pool.iota(slots[:, :], pattern=[[1, CAP]], base=1, channel_multiplier=0,
                      allow_small_or_imprecise_dtypes=True).then_inc(s_const, 1)
            pool.iota(small[:, 8:16], pattern=[[1, NE]], base=0, channel_multiplier=0,
                      allow_small_or_imprecise_dtypes=True).then_inc(s_const, 1)
            pool.iota(ov[:, 0, :], pattern=[[0, JEX], [1, NE]], base=1, channel_multiplier=0,
                      allow_small_or_imprecise_dtypes=True).then_inc(s_const, 1)
            pool.iota(ov[:, 1, :], pattern=[[CAP, JEX], [0, NE]], base=CAP, channel_multiplier=0,
                      allow_small_or_imprecise_dtypes=True).then_inc(s_const, 1)
            pool.memset(sc[:, :, :, :], 0.0).then_inc(s_sc, 1)
            for j in range(40):
                s, q = 2 + j // 4, j % 4
                if j >= 2:
                    pool.wait_ge(s_afree, ADA_PANELS + j - 1)
                pool.dma_start(adar[:, j % 2, :].rearrange("p (k n) -> p k n", k=2),
                               ada_w[s // 6][q * 256:(q + 1) * 256, (s % 6) * D:(s % 6 + 1) * D]
                               .rearrange("(k p) n -> p k n", p=P)).then_inc(s_adap[j % 2], 16)
                if j == 20:
                    pool.wait_ge(s_ev, EVENT_AT[(0, "o")] + 1)
                    pool.memset(sc[:, :, :, :], 0.0).then_inc(s_sc, 1)
            pool.wait_ge(s_ev, EVENT_AT[("ada", 11)] + 1)
            pool.dma_start(fwbc, final_norm_w.rearrange("(a d) -> a d", a=1).to_broadcast([P, D])).then_inc(s_fw, 16)
            pool.wait_ge(s_uD, emptied(UNITS, UNIT_AT[(1, "wo", 3)], "D"))
            pool.memset(oacc, 0.0).then_inc(s_zero, 1)
            pool.memset(ye, 0.0).then_inc(s_zero, 1)
            pool.memset(gwT[:, 0, :], 0.0).then_inc(s_zero, 1)
            pool.wait_ge(s_items, 1)
            n_items = pool.value_load(nitem[0:1, 0:1], min_val=NE, max_val=MAXI)
            with pool.Fori(0, n_items) as i:
                for n in range(NPC):
                    if low_part(n)[0] == "G":
                        pool.wait_ge(s_hi, i * NPC + (n + 1))
                        pool.tensor_tensor(split[:, n % SPL, 1, :], raw[:, n % RAW, :],
                                           split[:, n % SPL, 0, :].bitcast(F32), ALU.subtract).then_inc(s_lo["G"], 1)

        @block.tensor
        def _(pe):
            units, events, panels = [0], [0], [ADA_PANELS]

            def open_unit(key):
                n = units[0]
                assert UNITS[n][0] == key, (key, UNITS[n])
                if n >= 4:
                    who = UNITS[n - 4][1]
                    pe.wait_ge(s_uA if who == "A" else s_uD, emptied(UNITS, n - 4, who))
                units[0] += 1
                return psU[n % 4]

            def open_event(key):
                n = events[0]
                assert EVENTS[n][0] == key, (key, EVENTS[n])
                if n >= 2:
                    who = EVENTS[n - 2][1]
                    pe.wait_ge(s_eA if who == "A" else s_eD, emptied(EVENTS, n - 2, who))
                events[0] += 1
                return psA[2 * (n % 2)], psA[2 * (n % 2) + 1]

            def take_panels(count):
                got = list(range(panels[0], panels[0] + count))
                panels[0] += count
                return got

            def arrived(pos):
                pe.wait_ge(s_panel[pos % RING], 16 * (pos // RING + 1))

            def mm(o, a, b, start, stop):
                return pe.matmul(o, a, b, start=start, stop=stop, skip_group_check=True)

            def project(key, rhs, split_first=None):
                lo, hi = take_panels(2)
                for j in range(2):
                    bank = open_unit(key(j))
                    if j == 0:
                        arrived(lo)
                    for m in range(2):
                        for k in range(KD):
                            if j == 0 and m == 0:
                                if k == 4:
                                    arrived(hi)
                                if split_first:
                                    split_first(k)
                            w = panel(lo if k < 4 else hi).rearrange("p (k n) -> p k n", k=4)
                            col = (2 * j + m) * P
                            last = mm(bank[:, m * T:(m + 1) * T], w[:, k % 4, col:col + P], rhs[:, k, :],
                                      k == 0, k == KD - 1)
                    last.then_inc(s_unit, 1)
                    yield j

            def project_rows(key):
                lo, hi = take_panels(2)
                for tt in range(TT):
                    bank = open_unit(key(tt))
                    if tt == 0:
                        arrived(lo)
                        arrived(hi)
                    for k in range(KD):
                        w = panel(lo if k < 4 else hi).rearrange("p (k n) -> p k n", k=4)
                        last = mm(bank[:, :], hT[:, k, tt * P:(tt + 1) * P], w[:, k % 4, :], k == 0, k == KD - 1)
                    last.then_inc(s_unit, 1)
                    yield tt

            def norm_stat(key, count):
                pe.wait_ge(s_sq, count)
                bank, _ = open_event(key)
                for k in range(KD):
                    last = mm(bank[:, 0:T], ones[:, :], merged[:, k, :], k == 0, k == KD - 1)
                last.then_inc(s_ev, 1)

            def ada_sum(s):
                pe.wait_ge(s_afree, 4 * (s + 1))
                bank, _ = open_event(("ada", s))
                for k in range(KD):
                    last = mm(bank[:, k:k + 1], adacc[:, s % 2, k * P:(k + 1) * P], ones[:, 0:1], True, True)
                last.then_inc(s_ev, 1)

            def level(l, j):
                if j == 0:
                    pe.wait_ge(s_uD, emptied(UNITS, UNIT_AT[(l, "q", 1)], "D"))
                else:
                    pe.wait_ge(s_qk, l * (NLEV - 1) + j)
                banks = open_event((l, "lev", j))
                ks, qs = (KB, QB) if j == 0 else (KT, QT)
                for tt in range(TT if j < NLEV - 1 else 1):
                    for h in range(HB):
                        s0 = h * T + tt * P
                        t0 = s0 if j < NLEV - 1 else h * T + P
                        last = mm(banks[tt][:, h * P:(h + 1) * P], ks[:, s0:s0 + P], qs[:, t0:t0 + P], True, True)
                last.then_inc(s_ev, 1)

            def sgu_mix(l):
                pe.wait_ge(s_uD, emptied(UNITS, UNIT_AT[(l, "v", 1)], "D"))
                banks = open_event((l, "sgu"))
                for g in range(HB):
                    for tt in range(TT):
                        col = (g % 2) * T + tt * P
                        last = mm(banks[g // 2][:, col:col + P], VTOK[:, tt * 512 + g * P:tt * 512 + (g + 1) * P],
                                  wT[:, l, g, :], True, True)
                last.then_inc(s_ev, 1)

            def attend(l):
                pe.wait_ge(s_eD, emptied(EVENTS, EVENT_AT[(l, "lev", NLEV - 1)], "D"))
                pe.wait_ge(s_uA, emptied(UNITS, UNIT_AT[(l, "i", 1)], "A"))
                banks = open_event((l, "o"))
                for h in range(HB):
                    v0, v1 = (ITOK[:, tt * 512 + h * P:tt * 512 + (h + 1) * P] for tt in range(TT))
                    col = (h % 2) * T
                    o = banks[h // 2]
                    mm(o[:, col:col + P], v0, sc[:, 0, h, :], True, True)
                    mm(o[:, col + P:col + T], v0, sc[:, 2, h, :], True, False)
                    last = mm(o[:, col + P:col + T], v1, sc[:, 1, h, :], False, True)
                last.then_inc(s_ev, 1)

            def head_stat(l):
                pe.wait_ge(s_osq, l + 1)
                banks = open_event((l, "ostat"))
                for j in range(2):
                    last = mm(banks[j][:, :], ones[:, :], OSQ[:, j * 512:(j + 1) * 512], True, True)
                last.then_inc(s_ev, 1)

            def mixer(l):
                if l == 0:
                    for s in range(2):
                        ada_sum(s)
                norm_stat((l, "norm1"), 2 * l + 1)

                def chunk(k):
                    pe.wait_ge(s_h, 2 * KD * l + k + 1)
                lev = 0
                for g in HEAD_GROUPS:
                    rows = g in ("i", "v")
                    run = project_rows(lambda j: (l, g, j)) if rows else \
                        project(lambda j: (l, g, j), hT, chunk if g == "f" else None)
                    for j in run:
                        if lev < NLEV and (g, j) not in (("f", 0), ("f", 1), ("q", 0), ("q", 1), ("ab", 0)):
                            level(l, lev)
                            lev += 1
                        if (g, j) == ("g", 0):
                            sgu_mix(l)
                            attend(l)
                for b in BRANCHES:
                    for gg in range(2):
                        for j in project(lambda j: (l, "gate" + b, 2 * gg + j), hT):
                            if b == "a" and gg == 0 and j == 0:
                                head_stat(l)
                    ps = take_panels(2)
                    src = {"a": AH, "c": UB, "b": YB}[b]
                    pe.wait_ge(s_y, 3 * l + {"a": 1, "c": 2, "b": 3}[b])
                    for j in range(4):
                        bank = open_unit((l, "y" + b, j))
                        if j == 0:
                            for pos in ps:
                                arrived(pos)
                        for m in range(2):
                            for k in range(4):
                                w = panel(ps[k // 2]).rearrange("p (k n) -> p k n", k=2)
                                col = (2 * j + m) * P
                                last = mm(bank[:, m * T:(m + 1) * T], w[:, k % 2, col:col + P],
                                          src[:, k * T:(k + 1) * T], k == 0, k == 3)
                        last.then_inc(s_unit, 1)
                    if l == 0 and b in ("a", "c"):
                        ada_sum({"a": 2, "c": 3}[b])

                def chunk_m(k):
                    if k % 2 == 0:
                        pe.wait_ge(s_mg, 8 * l + 4 + k // 2 + 1)
                for gg in range(2):
                    for _ in project(lambda j: (l, "wo", 2 * gg + j), merged, chunk_m if gg == 0 else None):
                        pass
                if l == 0:
                    ada_sum(4)
                norm_stat((l, "norm2"), 2 * l + 2)

            def hidden(base, after):
                for f in range(NF):
                    g, m = f // 4, f % 4
                    full = g < FF // GROUP
                    bank = open_unit(("ffn", f))
                    for which in range(2):
                        for k in range(KD):
                            if full:
                                n = base + 4 * g + 2 * which + k // 4
                                w = panel(n).rearrange("p (k n) -> p k n", k=4)[:, k % 4, m * P:(m + 1) * P]
                                fresh = m == 0 and k % 4 == 0
                            else:
                                n = base + 4 * g + which
                                w = panel(n).rearrange("p (k n) -> p k n", k=8)[:, k, m * P:(m + 1) * P]
                                fresh = m == 0 and k == 0
                            if fresh:
                                arrived(n)
                            if f == 0 and which == 0:
                                pe.wait_ge(s_h, KD + k + 1)
                            last = mm(bank[:, which * T:(which + 1) * T], w, hT[:, k, :], k == 0, k == KD - 1)
                    last.then_inc(s_unit, 1)
                    after(f)

            def dense_ffn():
                base = panels[0]
                take_panels(3 * RING)
                sums = {-(-8 * (n + 1) // 3) + 1: 5 + n for n in range(7)}

                def after(f):
                    if f in sums:
                        ada_sum(sums[f])
                hidden(base, after)
                for key in ("down0", "down1"):
                    banks = open_event(key)
                    if key == "down0":
                        four = list(banks)
                    else:
                        four += list(banks)
                for j in range(NF // 2):
                    pos = base + 2 * RING + j
                    arrived(pos)
                    for kk in range(2):
                        f = 2 * j + kk
                        pe.wait_ge(s_uD, emptied(UNITS, UNIT_AT[("ffn", f)], "D"))
                        w = panel(pos).rearrange("p (k n) -> p k n", k=2)
                        for m in range(KD):
                            last = mm(four[m // 2][:, (m % 2) * T:(m % 2 + 1) * T], w[:, kk, m * P:(m + 1) * P],
                                      hidden0[:, f, :], f == 0 and m % 2 == 0, f == NF - 1)
                            if f == NF - 1 and m == 3:
                                last.then_inc(s_ev, 1)
                    last.then_inc(s_down if j < NF // 2 - 1 else s_ev, 1)

            pe.wait_ge(s_const, 2)
            pe.wait_ge(s_x, 16)
            for j in range(4):
                bank = open_unit(("x", j))
                for m in range(2):
                    for tt in range(TT):
                        last = pe.transpose(bank[:, m * T + tt * P:m * T + (tt + 1) * P],
                                            xrow[:, tt, (2 * j + m) * P:(2 * j + m + 1) * P], ident[:, :])
                last.then_inc(s_unit, 1)
            pe.wait_ge(s_small, 16 * N_SMALL)
            bank = open_unit(("vec", 0))
            pe.transpose(bank[:, 0:NA_ROWS], stackA[0:NA_ROWS, :], ident[0:NA_ROWS, 0:NA_ROWS])
            pe.transpose(bank[:, NA_ROWS:NA_ROWS + NB_ROWS], stackB[0:NB_ROWS, :],
                         ident[0:NB_ROWS, 0:NB_ROWS]).then_inc(s_unit, 1)
            for l in range(DEPTH):
                bank = open_unit(("wt", l))
                for g in range(HB):
                    last = pe.transpose(bank[:, g * P:(g + 1) * P], wrow[:, l, g, :], ident[:, :])
                last.then_inc(s_unit, 1)
            mixer(0)
            dense_ffn()
            mixer(1)

            pe.wait_ge(s_zero, 3)
            pe.wait_ge(s_eA, emptied(EVENTS, EVENT_AT[(1, "norm2")], "A"))
            for half in range(2):
                last = mm(Y_BANKS[half][0:CAP, :], gwT[:, 0, 0:CAP], ye[:, half * 512:(half + 1) * 512], True, True)
            last.then_inc(s_used, USED0)

            bank = open_unit("logits")
            for tt in range(TT):
                for k in range(KD):
                    if tt == 0:
                        pe.wait_ge(s_h, 3 * KD + k + 1)
                    last = mm(bank[:, tt * NE:(tt + 1) * NE], hT[:, k, tt * P:(tt + 1) * P], rtw[:, k, :],
                              k == 0, k == KD - 1)
            last.then_inc(s_unit, 1)
            pe.wait_ge(s_rt, 1)
            bank = open_unit("rank")
            mm(bank[:, 0:NE], tri[:, :], route[:, 0, 0:NE], True, True)
            mm(bank[:, NE:2 * NE], ones[:, :], route[:, 0, 0:NE], True, False)
            mm(bank[:, NE:2 * NE], tri[:, :], route[:, 0, NE:2 * NE], False, True)
            mm(bank[:, 2 * NE:3 * NE], ones[:, :], route[:, 0, 0:NE], True, False)
            mm(bank[:, 2 * NE:3 * NE], ones[:, :], route[:, 0, NE:2 * NE], False, True).then_inc(s_unit, 1)
            for key, src in (("htok", hT), ("xtok", xT)):
                for j in range(4):
                    bank = open_unit((key, j))
                    tt, half = j // 2, j % 2
                    for m in range(4):
                        last = pe.transpose(bank[:, m * P:(m + 1) * P],
                                            src[:, 4 * half + m, tt * P:(tt + 1) * P], ident[:, :])
                    last.then_inc(s_unit, 1)
            pe.wait_ge(s_gw, 1)
            for j in range(2):
                bank = open_unit(("g2", j))
                for m in range(4):
                    last = mm(bank[:, m * P:(m + 1) * P], merged[:, 4 * j + m, 0:P], ident[:, :], True, True)
                last.then_inc(s_unit, 1)

            def gather(banks):
                for m in range(KD):
                    for tt in range(TT):
                        last = mm(banks[m // 4][:, (m % 4) * CAP:(m % 4 + 1) * CAP], htok[:, tt, m * P:(m + 1) * P],
                                  sel[:, 0, tt, :], tt == 0, tt == 1)
                return last

            def turn_gates(bank):
                for tt in range(TT):
                    last = pe.transpose(bank[0:CAP, tt * P:(tt + 1) * P], sel[:, 1, tt, :], ident[:, :])
                return last

            def scatter(j):
                tt, half = j // 2, j % 2
                mm(psU[j][:, :], gwT[0:CAP, 0, tt * P:(tt + 1) * P], ye[0:CAP, half * 512:(half + 1) * 512],
                   True, True).then_inc(s_sct, 1)

            pe.wait_ge(s_sel, 1)
            pe.wait_ge(s_uA, emptied(UNITS, UNIT_AT[("htok", 3)], "A"))
            turn_gates(open_unit("sel0")).then_inc(s_unit, 1)
            gather(open_event("gather0")).then_inc(s_ev, 1)
            assert units[0] == len(UNITS) and events[0] == len(EVENTS) and panels[0] == len(PANELS)

            pe.wait_ge(s_uA, emptied(UNITS, len(UNITS), "A"))
            pe.wait_ge(s_items, 1)
            n_items = pe.value_load(nitem[0:1, 0:1], min_val=NE, max_val=MAXI)
            with pe.Fori(0, n_items) as i:
                def piece(n, stationary, outs):
                    who, count = low_part(n)
                    pe.wait_ge(s_lo[who], i * LOWS[who] + count)
                    for xs, ws in ((0, 0), (0, 1), (1, 0)):
                        for o, k, cols, first, end in outs:
                            last = mm(o, stationary(xs, k), split[:, n % SPL, ws, cols],
                                      first and xs == 0 and ws == 0, end and xs == 1)
                    last.then_inc(s_used, 1)

                def turn(g):
                    pe.wait_ge(s_hrow, i * len(GROUPS) + (g + 1))
                    if g >= 2:
                        pe.wait_ge(s_hlo, i * len(GROUPS) + (g - 1))
                    for m in range(len(GROUPS[g])):
                        last = pe.transpose(T_BANKS[g % 2][:, m * CAP:(m + 1) * CAP],
                                            sig[0:CAP, 2 + g % 2, m * P:(m + 1) * P], ident[0:CAP, 0:CAP])
                    last.then_inc(s_turn, 1)

                n = 0
                for g, tiles in enumerate(GROUPS):
                    width = len(tiles) * P
                    if g == 0:
                        pe.wait_ge(s_xlo, i + 1)
                    elif g == 1:
                        pe.wait_ge(s_gate, i + 1)
                    else:
                        pe.wait_ge(s_hrow, i * len(GROUPS) + (g - 1))
                    for which in range(2):
                        o = psU[2 * (g % 2) + which][0:CAP, 0:width]
                        per = PIECE // width
                        for q in range(KD // per):
                            piece(n, lambda xs, k: xE[:, xs, k, :],
                                  [(o, q * per + kk, slice(kk * width, (kk + 1) * width),
                                    q == 0 and kk == 0, q == KD // per - 1 and kk == per - 1) for kk in range(per)])
                            n += 1
                    if g:
                        turn(g - 1)
                pe.wait_ge(s_ye, i + 1)
                for j in range(2):
                    scatter(j)
                turn(len(GROUPS) - 1)
                for j in range(2, 4):
                    scatter(j)
                pe.wait_ge(s_sel, i + 2)
                pe.wait_ge(s_add, i * 4 + 1)
                turn_gates(psU[0]).then_inc(s_sct, 1)
                for f in range(NF):
                    if n == GATHER_AT:
                        pe.wait_ge(s_gate, i + 2)
                        gather(psU[0:2]).then_inc(s_gath, 1)
                    if f % 4 == 0:
                        pe.wait_ge(s_hlo, i * len(GROUPS) + (f // 4 + 1))
                    piece(n, lambda xs, k: hidE[:, xs, k, :],
                          [(Y_BANKS[half][0:CAP, :], f, slice(half * 512, (half + 1) * 512), f == 0, f == NF - 1)
                           for half in range(2)])
                    n += 1
            pe.wait_ge(s_ye, n_items + 1)
            pe.wait_ge(s_gate, n_items + 1)
            pe.wait_ge(s_xlo, n_items + 1)
            for j in range(4):
                scatter(j)

        @block.scalar
        def _(act):
            step = [0]

            def link(ins):
                step[0] += 1
                ins.then_inc(s_a, 1)
                act.wait_ge(s_a, step[0])

            def unit(key):
                n = UNIT_AT[key]
                act.wait_ge(s_unit, n + 1)
                return psU[n % 4]

            def event(key):
                n = EVENT_AT[key]
                act.wait_ge(s_ev, n + 1)
                return psA[2 * (n % 2)], psA[2 * (n % 2) + 1]

            def copy(o, i):
                return act.activation(o, i, ACT.Copy)

            small_loads = [
                (stackA[ADA_B:ADA_B + 96, :], ada_b.rearrange("l (r p) -> (l r) p", p=P)),
                (stackA[C_ROW:C_ROW + KD, :], c.rearrange("b (r p) -> (b r) p", p=P)),
                (stackA[LB_ROW:LB_ROW + 8, :], lb_logits.rearrange("l (r p) -> (l r) p", p=P)),
                (stackB[NMIX:NMIX + 16, :], norm_mix_w.rearrange("l (r p) -> (l r) p", p=P)),
                (stackB[NFFN:NFFN + 16, :], norm_ffn_w.rearrange("l (r p) -> (l r) p", p=P)),
                (stackB[CONV:CONV + 24, :], conv_w.rearrange("l w (r p) -> (l w r) p", p=P)),
                (stackB[HNW:HNW + 8, :], hgrn_norm_w.rearrange("l (r p) -> (l r) p", p=P)),
                (stackB[SNW:SNW + 8, :], sgu_norm_w.rearrange("l (r p) -> (l r) p", p=P)),
                (wrow.rearrange("p l g s -> p (l g) s"), sgu_w.rearrange("l g t s -> t (l g) s")),
                (sgub[:, :, :, :].rearrange("p l g t -> p (l g t)"),
                 sgu_b.rearrange("(a l) g t -> a (l g t)", a=1).to_broadcast([P, DEPTH * HB * P])),
                (rtw[:, :, :], router_w[0].rearrange("(k p) e -> p k e", p=P)),
                (rtb[:, :], router_b.to_broadcast([P, NE])),
            ]
            assert len(small_loads) == N_SMALL
            for dst, src in small_loads:
                act.dma_start(dst, src).then_inc(s_small, 16)

            for j in range(4):
                copy(xT[:, 2 * j:2 * j + 2, :].rearrange("p a b -> p (a b)"), unit(("x", j))[:, :]).then_inc(s_uA, 1)
            copy(vecs[:, :], unit(("vec", 0))[:, 0:NA_ROWS + NB_ROWS]).then_inc(s_uA, 1)
            act.wait_ge(s_uA, 5)
            act.activation(cact[:, :], vecs[:, C_ROW:C_ROW + KD], ACT.Sigmoid).then_inc(s_cact, 1)
            act.wait_ge(s_lbsig, 1)
            act.activation(lbs[:, 1, 0, :], lbs[:, 1, 1, :], ACT.Sigmoid).then_inc(s_cact, 1)
            act.wait_ge(s_uD, 2)

            def std(o, i, n):
                return act.activation(o, i, ACT.Sqrt, scale=1.0 / n, bias=eps[:, :])

            def norm(l, second):
                if second:
                    act.wait_ge(s_uD, emptied(UNITS, UNIT_AT[(l, "wo", 3)], "D"))
                elif l:
                    act.wait_ge(s_eD, emptied(EVENTS, EVENT_AT["down1"], "D"))
                act.activation(merged[:, :, :].rearrange("p a b -> p (a b)"),
                               xT[:, :, :].rearrange("p a b -> p (a b)"), ACT.Square).then_inc(s_sq, 1)
                bank, _ = event((l, "norm2" if second else "norm1"))
                std(rstd[:, :], bank[:, 0:T], D).then_inc(s_eA, 1)
                act.wait_ge(s_mod, 2 * l + 1 + second)
                for k in range(KD):
                    n = KD * (2 * l + second) + k
                    act.wait_ge(s_xr, n + 1)
                    sh = 24 * second + k
                    act.activation(hT[:, k, :], hT[:, k, :], ACT.Identity, scale=wm[:, l, second, k:k + 1],
                                   bias=mod[:, l, sh:sh + 1]).then_inc(s_h, 1)

            def half(buf, j):
                return buf[:, j * 512:(j + 1) * 512]

            def mixer(l):
                norm(l, 0)
                for g in HEAD_GROUPS:
                    for j in range(2):
                        if g == "ah":
                            continue
                        bank = unit((l, g, j))
                        if g == "f":
                            act.activation(half(FB, j), bank[:, :], ACT.Sigmoid)
                            act.activation(half(KB, j), bank[:, :], ACT.Sigmoid, scale=-1.0).then_inc(s_uA, 1)
                        elif g in ("q", "g"):
                            act.activation(sig[:, j, :], bank[:, :], ACT.Sigmoid).then_inc(s_sig, 1)
                        elif g == "v":
                            link(act.activation(sig[:, 2 + j, :], bank[:, :], ACT.Square, accum_out=vst[:, j:j + 1]))
                            std(vst[:, 2 + j:3 + j], vst[:, j:j + 1], 512).then_inc(s_vst, 1)
                        else:
                            if g == "u" and j == 0:
                                act.wait_ge(s_y, 3 * l + 1)
                            copy(half({"ab": AB, "ac": AC, "i": ITOK, "u": UB}[g], j), bank[:, :]).then_inc(s_uA, 1)
                        if (g, j) == ("g", 0):
                            banks = event((l, "o"))
                            act.activation(half(OSQ, 0), banks[0][:, :], ACT.Square)
                            act.activation(half(OSQ, 1), banks[1][:, :], ACT.Square).then_inc(s_osq, 1)
                for n, b in enumerate(BRANCHES):
                    for j in range(4):
                        bank = unit((l, "gate" + b, j))
                        if n == 0:
                            act.wait_ge(s_uD, emptied(UNITS, UNIT_AT[(l, "g", 1)], "D"))
                        elif n == 1:
                            act.wait_ge(s_uD, emptied(UNITS, UNIT_AT[(l, "ya", j)], "D"))
                        else:
                            act.wait_ge(s_mg, 8 * l + j + 1)
                        act.activation(sig[:, j, :], bank[:, :], ACT.Sigmoid).then_inc(s_uA, 1)
                        if n == 0 and j == 0:
                            banks = event((l, "ostat"))
                            std(half(OSD, 0), banks[0][:, :], P)
                            std(half(OSD, 1), banks[1][:, :], P).then_inc(s_eA, 1)
                norm(l, 1)

            mixer(0)
            for f in range(NF):
                bank = unit(("ffn", f))
                act.activation(sig[:, f % 4, 0:T], bank[:, 0:T], ACT.Sigmoid).then_inc(s_sig, 1)
            mixer(1)

            act.wait_ge(s_prob, 1)
            act.activation(cur[:, 2:4], cur[:, 0:2], ACT.Sigmoid)
            act.activation(cur[:, 4:6], cur[:, 0:2], ACT.Sigmoid, scale=-1.0).then_inc(s_prob, 1)
            for key, dst in (("htok", htok), ("xtok", xtok)):
                for j in range(4):
                    copy(dst[:, j // 2, (j % 2) * 512:(j % 2 + 1) * 512], unit((key, j))[:, :]).then_inc(s_uA, 1)
            for j in range(2):
                copy(g2bc[:, j * 512:(j + 1) * 512], unit(("g2", j))[:, :]).then_inc(s_uA, 1)

            def tokens(banks):
                for j in range(2):
                    last = copy(xE[:, 0, 4 * j:4 * j + 4, :].rearrange("p a b -> p (a b)"), banks[j][:, 0:4 * CAP])
                last.then_inc(s_xhi, 1)

            def expert_rows():
                for half in range(2):
                    last = copy(ye[0:CAP, half * 512:(half + 1) * 512], Y_BANKS[half][0:CAP, :])
                last.then_inc(s_ye, 1)
            tokens(event("gather0"))
            act.wait_ge(s_items, 1)
            n_items = act.value_load(nitem[0:1, 0:1], min_val=NE, max_val=MAXI)
            with act.Fori(0, n_items) as i:
                def sigmoid_rows(g):
                    width = len(GROUPS[g]) * P
                    act.wait_ge(s_used, i * NPC + (USED0 + G_W1[g]))
                    act.activation(sig[0:CAP, g % 2, 0:width], psU[2 * (g % 2)][0:CAP, 0:width],
                                   ACT.Sigmoid).then_inc(s_silu, 1)

                def tiles_high(g):
                    tiles = GROUPS[g]
                    act.wait_ge(s_turn, i * len(GROUPS) + (g + 1))
                    copy(hidE[:, 0, tiles[0]:tiles[-1] + 1, :].rearrange("p a b -> p (a b)"),
                         T_BANKS[g % 2][:, 0:len(tiles) * CAP]).then_inc(s_hhi, 1)

                for n in range(NPC):
                    act.wait_ge(s_raw[n % RAW], i * (16 * NPC // RAW) + 16 * (n // RAW + 1))
                    act.wait_ge(s_used, i * NPC + (USED0 + n - SPL + 1))
                    copy(split[:, n % SPL, 0, :], raw[:, n % RAW, :]).then_inc(s_hi, 1)
                    if n == AHEAD:
                        act.wait_ge(s_used, i * NPC + USED0)
                        expert_rows()
                    for g in range(len(GROUPS)):
                        if n == G_W1[g] - 1 + AHEAD:
                            sigmoid_rows(g)
                        if n == (G_END[g + 1] - 1 + AHEAD if g < len(GROUPS) - 1 else HID + AHEAD):
                            tiles_high(g)
                    if n == GATHER_AT - 1 + AHEAD:
                        act.wait_ge(s_gath, i + 1)
                        tokens(psU[0:2])
            act.wait_ge(s_used, n_items * NPC + USED0)
            expert_rows()
            for tt in range(TT):
                act.wait_ge(s_fst, tt + 1)
                act.activation(work[:, 7 + tt, :], oacc[:, tt, :], ACT.Square, accum_out=vst[:, tt:tt + 1]).then_inc(s_a, 1)
                step[0] += 1
                act.wait_ge(s_a, step[0])
                std(vst[:, 2 + tt:3 + tt], vst[:, tt:tt + 1], D).then_inc(s_vst, 1)

        @block.vector
        def _(dve):
            step = [0]

            def link(ins):
                step[0] += 1
                ins.then_inc(s_v, 1)

            def settle():
                dve.wait_ge(s_v, step[0])

            def unit(key):
                n = UNIT_AT[key]
                dve.wait_ge(s_unit, n + 1)
                return psU[n % 4]

            def unit_done(key):
                dve.wait_ge(s_uD, emptied(UNITS, UNIT_AT[key], "D"))

            def event(key):
                n = EVENT_AT[key]
                dve.wait_ge(s_ev, n + 1)
                return psA[2 * (n % 2)], psA[2 * (n % 2) + 1]

            TTN, TS, STT = dve.tensor_tensor, dve.tensor_scalar, dve.scalar_tensor_tensor
            BV = NA_ROWS

            link(dve.memset(eps[:, :], EPS))
            link(dve.memset(work[:, 4:6, :], 0.0))
            link(dve.memset(items[:, :, :], 0.0))
            dve.wait_ge(s_const, 9)
            xor = work[:, 0, 0:P].bitcast(I32)
            above = work[:, 1, 0:P]
            link(TTN(xor, iotas[:, 0, :], iotas[:, 1, :], ALU.bitwise_xor))
            link(TTN(above, iotas[:, 1, :], iotas[:, 0, :], ALU.is_gt))
            settle()
            for j in range(8):
                link(STT(work[:, 2, j * P:(j + 1) * P], xor, float(2 ** j), above, ALU.is_ge, ALU.mult))
            link(dve.tensor_copy(masks[:, 0, :], ident[:, :]))
            settle()
            for j in range(1, 8):
                a = work[:, 2, (j - 1) * P:j * P]
                link(TTN(masks[:, j, :], a, work[:, 2, j * P:(j + 1) * P], ALU.subtract))
            dve.wait_ge(s_cact, 1)
            link(TTN(cact[:, :], cact[:, :], vecs[:, C_ROW:C_ROW + KD], ALU.mult))
            TTN(lbs[:, 1, 1, :], vecs[:, LB_ROW + HB:LB_ROW + 2 * HB], vecs[:, LB_ROW:LB_ROW + HB],
                ALU.subtract).then_inc(s_lbsig, 1)
            link(dve.memset(lbs[:, 0, 1, :], 1.0))
            link(dve.memset(lbs[:, 0, 2, :], LB_FLOOR))
            for l in range(DEPTH):
                bank = unit(("wt", l))
                for g in range(HB):
                    ins = TTN(wT[:, l, g, :], bank[:, g * P:(g + 1) * P], tri[:, :], ALU.mult)
                ins.then_inc(s_uD, 1)
            dve.wait_ge(s_cact, 2)
            link(TS(lbs[:, 1, 0, :], lbs[:, 1, 0, :], 0.0, 1.0, ALU.max, ALU.min))
            settle()
            link(TS(lbs[:, 1, 1, :], lbs[:, 1, 0, :], -1.0, 1.0, ALU.mult, ALU.add))
            link(TS(lbs[:, 1, 2, :], lbs[:, 1, 0, :], LB_FLOOR, None, ALU.max))
            settle()

            def product(s, k):
                n = 4 * s + k // 2
                if s < 2:
                    src, ready, turn = ring[:, n, :], s_panel[n], 1
                else:
                    m = n - ADA_PANELS
                    src, ready, turn = adar[:, m % 2, :], s_adap[m % 2], m // 2 + 1
                src = src[:, (k % 2) * D:(k % 2 + 1) * D]
                acc = adacc[:, s % 2, :]
                if k % 2 == 0:
                    dve.wait_ge(ready, 16 * turn)
                    if k:
                        dve.wait_ge(s_afree, n)
                else:
                    settle()
                if k == 0:
                    if s >= 2:
                        dve.wait_ge(s_ev, EVENT_AT[("ada", s - 2)] + 1)
                    ins = TS(acc, src, cact[:, 0:1], None, ALU.mult)
                else:
                    ins = STT(acc, src, cact[:, k:k + 1], acc, ALU.mult, ALU.add)
                if k % 2:
                    ins.then_inc(s_afree, 1)
                else:
                    link(ins)

            def modulate(s):
                l, part = s // 6, s % 6
                bank, _ = event(("ada", s))
                dst = mod[:, l, 8 * part:8 * part + 8]
                TTN(dst, bank[:, 0:KD], vecs[:, ADA_B + 8 * s:ADA_B + 8 * s + 8], ALU.add).then_inc(s_eD, 1)
                if part in (1, 4):
                    second = part // 4
                    dve.wait_ge(s_eD, emptied(EVENTS, EVENT_AT[("ada", s)], "D"))
                    w = BV + (NFFN if second else NMIX) + KD * l
                    STT(wm[:, l, second, :], dst, 1.0, vecs[:, w:w + KD], ALU.add, ALU.mult).then_inc(s_mod, 1)

            def norm(l, second):
                dve.wait_ge(s_eA, emptied(EVENTS, EVENT_AT[(l, "norm2" if second else "norm1")], "A"))
                link(dve.reciprocal(rstd[:, :], rstd[:, :]))
                settle()
                for k in range(KD):
                    TTN(hT[:, k, :], xT[:, k, :], rstd[:, :], ALU.mult).then_inc(s_xr, 1)

            def half(buf, j):
                return buf[:, j * 512:(j + 1) * 512]

            def prepare(l, j):
                h = 2 ** (j - 1)
                F, G, q, k, qt, kt = (b.rearrange("p (n c h) -> p n c h", c=2, h=h) for b in (FB, GB, QB, KB, QT, KT))
                if j > 1:
                    dve.wait_ge(s_ev, EVENT_AT[(l, "lev", j - 1)] + 1)
                settle()
                if j == 1:
                    link(dve.tensor_copy(kt[:, :, 0, :], k[:, :, 0, :]))
                else:
                    link(TTN(kt[:, :, 0, :], k[:, :, 0, :], G[:, :, 0, :], ALU.mult))
                TTN(qt[:, :, 1, :], q[:, :, 1, :], F[:, :, 1, :], ALU.mult).then_inc(s_qk, 1)
                if j == NLEV - 1:
                    return
                n = 1024 // (2 * h)
                if j == 1:
                    link(dve.tensor_copy(G[:, :, 0, :], F[:, :, 1, :]))
                else:
                    link(TTN(G[:, :, 0, :], G[:, :, 0, :], F[:, :, 1, h - 1:h].to_broadcast([P, n, h]), ALU.mult))
                settle()
                dve.wait_ge(s_qk, l * (NLEV - 1) + j)
                link(TTN(F[:, :, 1, :], F[:, :, 1, :], F[:, :, 0, h - 1:h].to_broadcast([P, n, h]), ALU.mult))

            def keep_scores(l, j):
                banks = event((l, "lev", j))
                if j == 0:
                    dve.wait_ge(s_sc, l + 1)
                else:
                    dve.wait_ge(s_eD, emptied(EVENTS, EVENT_AT[(l, "lev", j - 1)], "D"))
                if j == NLEV - 1:
                    ins = dve.tensor_copy(sc[:, 2, :, :].rearrange("p h t -> p (h t)"), banks[0][:, :])
                else:
                    m = masks[:, j:j + 1, :].to_broadcast([P, HB, P])
                    for tt in range(TT):
                        ins = dve.copy_predicated(sc[:, tt, :, :], m, banks[tt][:, :].rearrange("p (h t) -> p h t", h=HB))
                ins.then_inc(s_eD, 1)

            def gated(l, g, j, dst):
                bank = unit((l, g, j))
                dve.wait_ge(s_sig, SIG0[l] + {"q": 0, "g": 2}[g] + j + 1)
                TTN(half(dst, j), sig[:, j, :], bank[:, :], ALU.mult).then_inc(s_uD, 1)

            SIG0 = [0, 4 + NF]

            def mixer(l):
                if l == 0:
                    for s in range(2):
                        for k in range(KD):
                            product(s, k)
                    for s in range(2):
                        modulate(s)
                norm(l, 0)
                settle()
                link(dve.memset(GB, 1.0))
                for h in range(HB):
                    dve.wait_ge(s_uA, emptied(UNITS, UNIT_AT[(l, "f", h // 2)], "A"))
                    o = slice(h * T, (h + 1) * T)
                    link(TS(FB[:, o], FB[:, o], lbs[:, l, 1, h:h + 1], lbs[:, l, 2, h:h + 1], ALU.mult, ALU.add))
                    link(TS(KB[:, o], KB[:, o], lbs[:, l, 1, h:h + 1], None, ALU.mult))
                for j in range(2):
                    gated(l, "q", j, QB)
                unit_done((l, "q", 1))
                prepare(l, 1)
                ada = [0]

                def more_ada(n):
                    if l == 0:
                        for _ in range(n):
                            if ada[0] < 24:
                                product(2 + ada[0] // 8, ada[0] % 8)
                                ada[0] += 1
                for j in range(2):
                    keep_scores(l, j)
                    more_ada(2)
                    prepare(l, j + 2)
                for j in range(2):
                    bank = unit((l, "ah", j))
                    dve.wait_ge(s_uA, emptied(UNITS, UNIT_AT[(l, "ac", j)], "A"))
                    TTN(half(AC, j), half(AC, j), bank[:, :], ALU.mult).then_inc(s_uD, 1)
                    keep_scores(l, j + 2)
                    more_ada(1)
                    prepare(l, j + 4)
                unit_done((l, "ah", 1))
                z, y = (b.rearrange("p (c t) -> p c t", t=T) for b in (AC, AH))
                cw = BV + CONV + 12 * l
                for cc in range(4):
                    link(TS(y[:, cc, :], z[:, cc, :], vecs[:, cw + cc:cw + cc + 1], None, ALU.mult))
                for back in (1, 2):
                    settle()
                    for cc in range(4):
                        w = cw + 4 * back + cc
                        link(STT(y[:, cc, back:T], z[:, cc, 0:T - back], vecs[:, w:w + 1], y[:, cc, back:T],
                                 ALU.mult, ALU.add))
                settle()
                TTN(AH, AH, AB, ALU.mult).then_inc(s_y, 1)
                for j in range(4, 6):
                    keep_scores(l, j)
                    prepare(l, j + 2)
                keep_scores(l, 6)
                for j in range(2):
                    bank = unit((l, "v", j))
                    dve.wait_ge(s_vst, 2 * l + j + 1)
                    link(dve.reciprocal(vst[:, 4 + j:5 + j], vst[:, 2 + j:3 + j]))
                    settle()
                    if j == 0:
                        dve.wait_ge(s_y, 3 * l + 1)
                    TS(half(VTOK, j), bank[:, :], vst[:, 4 + j:5 + j], None, ALU.mult).then_inc(s_uD, 1)
                    if j == 0:
                        prepare(l, 8)
                    keep_scores(l, 7 + j)
                more_ada(4)
                settle()
                dve.wait_ge(s_qk, (l + 1) * (NLEV - 1))
                gated(l, "g", 0, GS)
                banks = event((l, "sgu"))
                for g in range(HB):
                    w = BV + SNW + HB * l + g
                    ins = STT(YB[:, g * T:(g + 1) * T].rearrange("p (n t) -> p n t", n=TT),
                              banks[g // 2][:, (g % 2) * T:(g % 2 + 1) * T].rearrange("p (n t) -> p n t", n=TT),
                              vecs[:, w:w + 1], sgub[:, l, g:g + 1, :].to_broadcast([P, TT, P]), ALU.mult, ALU.add)
                    if g < HB - 1:
                        link(ins)
                ins.then_inc(s_eD, 1)
                dve.wait_ge(s_eD, emptied(EVENTS, EVENT_AT[(l, "sgu")], "D"))
                dve.wait_ge(s_uA, emptied(UNITS, UNIT_AT[(l, "u", 1)], "A"))
                TTN(UB, UB, YB, ALU.mult).then_inc(s_y, 1)
                gated(l, "g", 1, GS)
                dve.wait_ge(s_eA, emptied(EVENTS, EVENT_AT[(l, "ostat")], "A"))
                link(dve.reciprocal(OSD, OSD))
                settle()
                dve.wait_ge(s_y, 3 * l + 2)
                banks = event((l, "o"))
                link(TTN(half(YB, 0), half(OSD, 0), banks[0][:, :], ALU.mult))
                TTN(half(YB, 1), half(OSD, 1), banks[1][:, :], ALU.mult).then_inc(s_eD, 1)
                settle()
                dve.wait_ge(s_eD, emptied(EVENTS, EVENT_AT[(l, "o")], "D"))
                unit_done((l, "g", 1))
                for h in range(HB):
                    w = BV + HNW + HB * l + h
                    o = slice(h * T, (h + 1) * T)
                    ins = STT(YB[:, o], YB[:, o], vecs[:, w:w + 1], GS[:, o], ALU.mult, ALU.mult)
                ins.then_inc(s_y, 1)
                for n, b in enumerate(BRANCHES):
                    for j in range(4):
                        bank = unit((l, "y" + b, j))
                        dve.wait_ge(s_uA, emptied(UNITS, UNIT_AT[(l, "gate" + b, j)], "A"))
                        m = merged[:, 2 * j:2 * j + 2, :].rearrange("p a b -> p (a b)")
                        if n == 0:
                            TTN(m, sig[:, j, :], bank[:, :], ALU.mult).then_inc(s_uD, 1)
                        else:
                            TTN(sig[:, j, :], sig[:, j, :], bank[:, :], ALU.mult).then_inc(s_uD, 1)
                            unit_done((l, "y" + b, j))
                            if n == 2:
                                dve.wait_ge(s_mg, 8 * l + j + 1)
                            TTN(m, m, sig[:, j, :], ALU.add).then_inc(s_mg, 1)
                        more_ada(2)
                    if l == 0 and n < 2:
                        modulate(2 + n)
                dve.wait_ge(s_eD, emptied(EVENTS, EVENT_AT[("ada", 6 * l + 2)], "D"))
                for j in range(4):
                    bank = unit((l, "wo", j))
                    for m in range(2):
                        ch = 2 * j + m
                        ins = STT(xT[:, ch, :], bank[:, m * T:(m + 1) * T], mod[:, l, 16 + ch:17 + ch], xT[:, ch, :],
                                  ALU.mult, ALU.add)
                        if m:
                            ins.then_inc(s_uD, 1)
                        else:
                            link(ins)
                if l == 0:
                    assert ada[0] == 24
                    modulate(4)
                settle()
                unit_done((l, "wo", 3))
                norm(l, 1)

            mixer(0)
            turn = {-(-8 * (n + 1) // 3) + 2: 5 + n for n in range(7)}
            done = 0
            for f in range(NF):
                bank = unit(("ffn", f))
                dve.wait_ge(s_sig, 4 + f + 1)
                link(TTN(sig[:, f % 4, 0:T], sig[:, f % 4, 0:T], bank[:, 0:T], ALU.mult))
                settle()
                TTN(hidden0[:, f, :], sig[:, f % 4, 0:T], bank[:, T:2 * T], ALU.mult).then_inc(s_uD, 1)
                if f in turn:
                    modulate(turn[f])
                for _ in range(3):
                    if done < 56:
                        product(5 + done // 8, done % 8)
                        done += 1
            dve.wait_ge(s_eD, emptied(EVENTS, EVENT_AT[("ada", 11)], "D"))
            for e in range(2):
                banks = event(f"down{e}")
                for m in range(4):
                    ch = 4 * e + m
                    ins = STT(xT[:, ch, :], banks[m // 2][:, (m % 2) * T:(m % 2 + 1) * T],
                              mod[:, 0, 40 + ch:41 + ch], xT[:, ch, :], ALU.mult, ALU.add)
                    if m == 3:
                        ins.then_inc(s_eD, 1)
                    else:
                        link(ins)
            settle()
            dve.wait_ge(s_eD, emptied(EVENTS, EVENT_AT["down1"], "D"))
            mixer(1)

            iota8 = small[:, 8:16]

            def pair(row):
                return route[:, row, :].rearrange("p (t e) -> p t e", t=TT)
            SEL, LG, ONE, TWO, GATE, POS, IDX, TMP, CNT = 0, 1, 2, 3, 4, 5, 6, 7, 11
            bank = unit("logits")
            TTN(pair(LG), bank[:, 0:2 * NE].rearrange("p (t e) -> p t e", t=TT),
                rtb[:, :].rearrange("p (a e) -> p a e", a=1).to_broadcast([P, TT, NE]), ALU.add).then_inc(s_uD, 1)
            unit_done("logits")
            for tt in range(TT):
                link(dve.max(mx8[:, tt, :], route[:, LG, tt * NE:(tt + 1) * NE]))
            settle()
            TTN(cur[:, 0:2], mx8[:, :, 0], mx8[:, :, 1], ALU.subtract).then_inc(s_prob, 1)
            for tt in range(TT):
                link(dve.max_index(ix8[:, tt, :], mx8[:, tt, :], route[:, LG, tt * NE:(tt + 1) * NE]))
            settle()
            link(dve.tensor_copy(route[:, IDX, :], ix8[:, :, :].rearrange("p t e -> p (t e)")))
            settle()
            for tt in range(TT):
                for row, k in ((ONE, 0), (TWO, 1)):
                    link(TS(route[:, row, tt * NE:(tt + 1) * NE], iota8,
                            route[:, IDX, tt * NE + k:tt * NE + k + 1], None, ALU.is_equal))
            settle()
            TTN(route[:, SEL, :], route[:, ONE, :], route[:, TWO, :], ALU.add).then_inc(s_rt, 1)
            dve.wait_ge(s_prob, 2)
            for tt in range(TT):
                o = slice(tt * NE, (tt + 1) * NE)
                link(TS(route[:, TMP, o], route[:, ONE, o], cur[:, 2 + tt:3 + tt], None, ALU.mult))
            settle()
            for tt in range(TT):
                o = slice(tt * NE, (tt + 1) * NE)
                link(STT(route[:, GATE, o], route[:, TWO, o], cur[:, 4 + tt:5 + tt], route[:, TMP, o],
                         ALU.mult, ALU.add))
            dve.wait_ge(s_rt, 1)
            bank = unit("rank")
            link(TTN(route[:, POS, :], bank[:, 0:2 * NE], route[:, SEL, :], ALU.mult))
            dve.tensor_copy(route[:, CNT, 0:NE], bank[:, 2 * NE:3 * NE]).then_inc(s_uD, 1)
            unit_done("rank")
            NO = NE * JEX
            link(dve.memset(items[:, MAXI, 0:1], -1.0))
            link(dve.tensor_copy(items[:, 0:NE, 0], iota8))
            for j in range(JEX):
                link(TS(ov[:, 2, j * NE:(j + 1) * NE], route[:, CNT, 0:NE], float(CAP * (j + 1)), None, ALU.is_gt))
            src, shift = 2, 1
            while shift < NO:
                dst = 4 if src == 3 else 3
                settle()
                link(dve.tensor_copy(ov[:, dst, 0:shift], ov[:, src, 0:shift]))
                link(TTN(ov[:, dst, shift:NO], ov[:, src, shift:NO], ov[:, src, 0:NO - shift], ALU.add))
                src, shift = dst, 2 * shift
            settle()
            for r in range(REX):
                link(STT(ov[:, 5, :], ov[:, src, :], float(r + 1), ov[:, 2, :], ALU.is_equal, ALU.mult))
                settle()
                for col in range(2):
                    link(TTN(ov[:, 6 + col, :], ov[:, 5, :], ov[:, col, :], ALU.mult))
                settle()
                for col in range(2):
                    link(dve.reduce_sum(items[:, NE + r, col:col + 1], ov[:, 6 + col, :], AX_X))
            settle()
            link(TS(items[:, NE:MAXI, 0], items[:, NE:MAXI, 0], -1.0, None, ALU.add))
            link(TS(nitem[:, :], ov[:, src, NO - 1:NO], float(NE), None, ALU.add))
            settle()
            dve.tensor_copy(itemi[:, :], items[:, :, 0]).then_inc(s_items, 1)

            both = route[:, GATE:POS + 1, :].rearrange("p r (t e) -> p (r t) e", t=TT)
            picked = route[:, TMP:TMP + 3, :].rearrange("p r e -> p (r e)")[:, 0:4 * NE] \
                .rearrange("p (r e) -> p r e", e=NE)
            hot = route[:, 10, 0:NE]

            def select(row, last):
                if last is not None:
                    dve.wait_ge(s_sel, last)
                link(dve.tensor_copy(cur[:, 6:8], row))
                settle()
                link(TS(hot, iota8, cur[:, 6:7], None, ALU.is_equal))
                settle()
                link(TTN(picked, both, route[:, 10:11, 0:NE].to_broadcast([P, 4, NE]), ALU.mult))
                settle()
                link(dve.reduce_sum(cur[:, 0:4], picked, AX_X))
                settle()
                link(TS(cur[:, 4:6], cur[:, 2:4], cur[:, 7:8], None, ALU.subtract))
                settle()
                for tt in range(TT):
                    link(TS(sel[:, 0, tt, :], slots[:, :], cur[:, 4 + tt:5 + tt], None, ALU.is_equal))
                    ins = TS(sel[:, 1, tt, :], slots[:, :], cur[:, 4 + tt:5 + tt], cur[:, tt:tt + 1],
                             ALU.is_equal, ALU.mult)
                    if tt == 0:
                        link(ins)
                ins.then_inc(s_sel, 1)

            for ch in range(KD):
                ins = TS(merged[:, ch, 0:P], ones[:, :], mod[:, 1, 40 + ch:41 + ch], None, ALU.mult)
            ins.then_inc(s_gw, 1)
            select(items[:, 0, :], None)
            bank = unit("sel0")
            dve.tensor_copy(gwT[0:CAP, 1, :], bank[0:CAP, 0:T]).then_inc(s_gate, 1)

            def tokens_low(banks):
                for j in range(2):
                    x_hi, x_lo = (xE[:, part, 4 * j:4 * j + 4, :].rearrange("p a b -> p (a b)") for part in range(2))
                    last = TTN(x_lo, banks[j][:, 0:4 * CAP], x_hi.bitcast(F32), ALU.subtract)
                last.then_inc(s_xlo, 1)
            dve.wait_ge(s_xhi, 1)
            tokens_low(event("gather0"))
            dve.wait_ge(s_zero, 3)
            dve.wait_ge(s_items, 1)
            n_items = dve.value_load(nitem[0:1, 0:1], min_val=NE, max_val=MAXI)
            before = step[0]
            STEPS = len(GROUPS) + 9
            with dve.Fori(0, n_items) as i:
                n_link = [0]

                def ilink(ins):
                    n_link[0] += 1
                    ins.then_inc(s_v, 1)

                def isettle():
                    dve.wait_ge(s_v, i * STEPS + (before + n_link[0]))
                link, settle = ilink, isettle

                def hidden_rows(g):
                    width = len(GROUPS[g]) * P
                    one = psU[2 * (g % 2)][0:CAP, 0:width]
                    three = psU[2 * (g % 2) + 1][0:CAP, 0:width]
                    dve.wait_ge(s_silu, i * len(GROUPS) + (g + 1))
                    s = sig[0:CAP, g % 2, 0:width]
                    link(TTN(s, s, one, ALU.mult))
                    dve.wait_ge(s_used, i * NPC + (USED0 + G_END[g]))
                    settle()
                    TTN(sig[0:CAP, 2 + g % 2, 0:width], s, three, ALU.mult).then_inc(s_hrow, 1)

                def tiles_low(g):
                    tiles = GROUPS[g]
                    dve.wait_ge(s_hhi, i * len(GROUPS) + (g + 1))
                    h_hi, h_lo = (hidE[:, part, tiles[0]:tiles[-1] + 1, :].rearrange("p a b -> p (a b)")
                                  for part in range(2))
                    TTN(h_lo, T_BANKS[g % 2][:, 0:len(tiles) * CAP], h_hi.bitcast(F32), ALU.subtract).then_inc(s_hlo, 1)

                def add_rows(j):
                    dve.wait_ge(s_sct, i * 5 + (j + 1))
                    o = oacc[:, j // 2, (j % 2) * 512:(j % 2 + 1) * 512]
                    TTN(o, o, psU[j][:, :], ALU.add).then_inc(s_add, 1)

                LAST = len(GROUPS) - 1
                for n in range(NPC):
                    if low_part(n)[0] == "V":
                        dve.wait_ge(s_hi, i * NPC + (n + 1))
                        TTN(split[:, n % SPL, 1, :], raw[:, n % RAW, :], split[:, n % SPL, 0, :].bitcast(F32),
                            ALU.subtract).then_inc(s_lo["V"], 1)
                    for g in range(len(GROUPS)):
                        if n == G_END[g] + 3:
                            hidden_rows(g)
                        if n == (G_END[g + 1] if g < LAST else HID + 1) + 3:
                            tiles_low(g)
                    if n == G_END[0] + 5:
                        select(items[:, bass.ds(i + 1, 1), :].rearrange("p a b -> p (a b)"), i + 1)
                    if n == HID + 3:
                        for j in range(2):
                            add_rows(j)
                    if n == HID + 4:
                        for j in range(2, 4):
                            add_rows(j)
                        dve.wait_ge(s_add, i * 4 + 4)
                        link(dve.tensor_copy(gwT[0:CAP, 0, :], gwT[0:CAP, 1, :]))
                        settle()
                        dve.wait_ge(s_sct, i * 5 + 5)
                        dve.tensor_copy(gwT[0:CAP, 1, :], psU[0][0:CAP, 0:T]).then_inc(s_gate, 1)
                    if n == GATHER_AT + 4:
                        dve.wait_ge(s_xhi, i + 2)
                        tokens_low(psU[0:2])
                assert n_link[0] == STEPS, n_link
            dve.wait_ge(s_v, n_items * STEPS + before)
            for j in range(4):
                dve.wait_ge(s_sct, n_items * 5 + (j + 1))
                o = oacc[:, j // 2, (j % 2) * 512:(j % 2 + 1) * 512]
                TTN(o, o, psU[j][:, :], ALU.add).then_inc(s_add, 1)
            dve.wait_ge(s_add, n_items * 4 + 4)
            dve.wait_ge(s_uA, emptied(UNITS, len(UNITS), "A"))
            dve.wait_ge(s_fw, 16)
            for tt in range(TT):
                TTN(oacc[:, tt, :], oacc[:, tt, :], g2bc, ALU.mult).then_inc(s_gw, 1)
            for tt in range(TT):
                dve.wait_ge(s_gw, 2 + tt)
                TTN(oacc[:, tt, :], oacc[:, tt, :], xtok[:, tt, :], ALU.add).then_inc(s_fst, 1)
            for tt in range(TT):
                dve.wait_ge(s_vst, 2 * TT + tt + 1)
                dve.reciprocal(vst[:, 4 + tt:5 + tt], vst[:, 2 + tt:3 + tt]).then_inc(s_gw, 1)
                dve.wait_ge(s_gw, 4 + tt)
                STT(oacc[:, tt, :], oacc[:, tt, :], vst[:, 4 + tt:5 + tt], fwbc, ALU.mult,
                    ALU.mult).then_inc(s_fin, 1)


_INS = ["x", "c", "ada_w", "ada_b", "norm_mix_w", "norm_ffn_w", "w_in", "conv_w", "hgrn_lb_logits", "hgrn_norm_w",
        "sgu_norm_w", "sgu_w", "sgu_b", "w_br_a", "w_br_b", "w_br_c", "w_o", "ffn_w1", "ffn_w3", "ffn_w2",
        "moe_router_w", "moe_router_b", "moe_w1", "moe_w3", "moe_w2", "final_norm_w"]


def kernel(**inputs):
    import numpy as _np
    import concourse.bacc as _bacc
    from concourse import mybir as _mybir
    from concourse.bass_utils import run_bass_kernel_spmd as _run

    nc = _bacc.Bacc("TRN2", target_bir_lowering=False, num_devices=1)
    arrays, args = {}, []
    for name in _INS:
        a = _np.ascontiguousarray(inputs[name])
        arrays[f"in_{name}_dram"] = a
        args.append(nc.dram_tensor(f"in_{name}_dram", a.shape, _mybir.dt.from_np(a.dtype), kind="ExternalInput").ap())
    o = nc.dram_tensor("out_0_dram", (1, T, D), F32, kind="ExternalOutput").ap()
    program(nc, *args, o)
    r = _run(nc, [arrays], core_ids=[0])
    return r.results[0]["out_0_dram"]
```

```python
from contextlib import ExitStack

import concourse.bass as bass
from concourse import mybir

P = 128
F32 = mybir.dt.float32
F32R = mybir.dt.float32r
I32 = mybir.dt.int32
U32 = mybir.dt.uint32
U8 = mybir.dt.uint8
ALU = mybir.AluOpType
ACT = mybir.ActivationFunctionType
AX_X = mybir.AxisListType.X

T = 256
TT = T // P
D = 1024
KD = D // P
HB = 4
FF = 2816
NF = FF // P
NE = 8
DEPTH = 2
EPS = 1e-6
LB_FLOOR = 1e-30
NLEV = 9

CAP = 104
JEX = -(-T // CAP) - 1
REX = (2 * T) // (CAP + 1)
MAXI = NE + REX

COLS = {n: 512 * c for c, n in enumerate(["ab", "ac", "ah", "q", "f", "i", "g", "u", "v"])}
GATE0 = {"a": 4608, "b": 5632, "c": 6656}
NO_LEVEL = [("f", 0), ("f", 1), ("q", 0), ("q", 1), ("i", 1)]
HEAD_GROUPS = ["f", "q", "ab", "ac", "ah", "i", "v", "u", "g"]
BRANCHES = ["a", "c", "b"]

ADA_B, C_ROW, LB_ROW, NA_ROWS = 0, 96, 104, 112
NMIX, NFFN, CONV, HNW, SNW, NB_ROWS = 0, 16, 32, 56, 64, 72

PIECE = 1024
GROUPS = [list(range(4 * g, min(4 * g + 4, NF))) for g in range(-(-NF // 4))]
HID_PIECES = [8 if len(g) == 4 else 4 for g in GROUPS]
HID = sum(HID_PIECES)
NPC = HID + NF
RAW = 11
SPL = 6
AHEAD = SPL - 1
assert NPC % RAW == 0 and NPC % SPL == 0 and NPC % 3 == 0

NADA = 6 * DEPTH
ADA_ORDER = [0, 1, 2, 3, 4, 5, 6, 7, 11, 8, 9, 10]
FFN_ADA = [5, 6, 7, 11]
DOWN_ADA = [8, 9, 10]
DOWN_TAKE = [2, 2, 1, 1, 1, 1] * 3 + [0] * (NF - 18)
assert sum(DOWN_TAKE) == KD * len(DOWN_ADA)
FFN_TAKE = [4, 4] + [3] * 8 + [0]
assert sum(FFN_TAKE) == KD * len(FFN_ADA)
FFN_SUMS = {next(p for p in range(NF // 2) if sum(FFN_TAKE[:p + 1]) >= KD * (n + 1)) + 1: s
            for n, s in enumerate(FFN_ADA)}

G_END = [sum(HID_PIECES[:g + 1]) for g in range(len(GROUPS))]
G_W1 = [G_END[g] - HID_PIECES[g] // 2 for g in range(len(GROUPS))]
GATHER_AT = HID + 8


def low_part(n):
    return ("G", n // 3 + 1) if n % 3 == 2 else ("V", n - n // 3 + (1 if n % 3 < 2 else 0))


LOWS = {"V": 2 * NPC // 3, "G": NPC // 3}


def unit_plan():
    plan = [(("x", j), "A") for j in range(4)] + [(("vec", 0), "A")]
    for l in range(DEPTH):
        for g in HEAD_GROUPS:
            plan += [((l, g, j), "A" if g in ("f", "ab", "ac", "i", "u") else "D") for j in range(2)]
            if l == 0 and g == "q":
                plan += [(("wt", 0), "D"), (("wt", 1), "D")]
        for b in BRANCHES:
            plan += [((l, "gate" + b, j), "A") for j in range(4)]
            plan += [((l, "y" + b, j), "D") for j in range(4)]
        plan += [((l, "wo", j), "D") for j in range(4)]
        if l == 0:
            plan += [(("ffn", j), "D") for j in range(NF)] + [(("mod", s), "D") for s in DOWN_ADA]
    plan += [("logits", "D"), ("rank", "D")]
    plan += [(("htok", j), "A") for j in range(4)] + [(("xtok", j), "A") for j in range(4)]
    plan += [(("g2", j), "A") for j in range(2)] + [("sel0", "gates")]
    return plan


def event_plan():
    plan = []
    for l in range(DEPTH):
        plan += [((l, "norm1"), "A")]
        if l == 0:
            plan += [(("ada", 1), "D"), (("ada", 0), "D")]
        plan += [((l, "lev", j), "D") for j in range(NLEV)]
        plan += [((l, "sgu"), "D"), ((l, "o"), "D"), ((l, "ostat"), "A")]
        if l == 0:
            plan += [(("ada", s), "D") for s in (2, 3, 4)]
        plan += [((l, "norm2"), "A")]
        if l == 0:
            plan += [(("ada", s), "D") for s in FFN_ADA]
            plan += [("down0", "D"), ("down1", "D")]
    plan += [("gather0", "tokens")]
    return plan


UNITS = unit_plan()
EVENTS = event_plan()
UNIT_AT = {k: n for n, (k, _) in enumerate(UNITS)}
EVENT_AT = {k: n for n, (k, _) in enumerate(EVENTS)}


def unit_signals():
    used = direct = 0
    signal = {}
    for key, _ in UNITS:
        kind = key[1] if len(key) == 3 and isinstance(key, tuple) else key[0]
        if kind in ("i", "v", "ffn"):
            used += 4 if key[-1] % 2 == 0 else 0
            signal[key] = ("used", used, used)
        elif kind in HEAD_GROUPS or kind in ("gatea", "gateb", "gatec", "wo", "ya", "yb", "yc"):
            used += 1 if kind[0] == "y" else 2
            signal[key] = ("used", used, used)
        else:
            direct += 1
            signal[key] = ("direct", direct, used)
    return signal, used


SIGNAL, NSPLIT = unit_signals()
USED0 = NSPLIT + 1


def dense_pieces():
    sections = iter(ADA_ORDER)
    out = []

    def section():
        s = next(sections)
        return [(("ada", k), "ada_w", s // 6, k * P, (s % 6) * D, PIECE) for k in range(KD)]

    for k, (zero, one) in enumerate(zip(section(), section())):
        use = ("mod", k // 2) if k % 2 else ("ada1", k)
        out += [zero, (use,) + one[1:]]
    for l in range(DEPTH):
        for g in HEAD_GROUPS:
            if g in ("i", "v"):
                out += [("split", "w_in", l, q * 256, COLS[g], 512) for q in range(4)]
            else:
                out += [("split", "w_in", l, q * 512, COLS[g] + 256 * j, 256) for j in range(2) for q in range(2)]
            if l == 0 and g == "f":
                two = section()
                out += two[:4]
            if l == 0 and g == "u":
                out += two[4:]
        for b in BRANCHES:
            gates = [("split", "w_in", l, q * 512, GATE0[b] + 256 * j, 256) for j in range(4) for q in range(2)]
            ada = section() if l == 0 and b != BRANCHES[0] else []
            for q, gate in enumerate(gates):
                out += [gate] + ada[q:q + 1]
            out += [("split", "w_br_" + b, l, 0, 256 * j, 256) for j in range(4)]
        out += [("split", "w_o", l, q * 512, 256 * j, 256) for j in range(4) for q in range(2)]
        if l == 0:
            ada = sum((section() for _ in FFN_ADA), [])
            for pair in range(NF // 2):
                out += [("split", w, 0, q * 512, 256 * pair, 256) for w in ("ffn_w1", "ffn_w3") for q in range(2)]
                out += ada[:FFN_TAKE[pair]]
                ada = ada[FFN_TAKE[pair]:]
            assert not ada
            ada = sum((section() for _ in DOWN_ADA), [])
            for f in range(NF):
                out += [(("down", f), "ffn_w2", 0, f * P, 0, PIECE)] + ada[:DOWN_TAKE[f]]
                ada = ada[DOWN_TAKE[f]:]
    assert next(sections, None) is None
    return out


PIECES = dense_pieces()
RAW0 = len(PIECES)
SPLIT_POS = [pos for pos, p in enumerate(PIECES) if p[0] == "split"]
ADA_POS = [pos for pos, p in enumerate(PIECES) if p[0][0] in ("ada", "ada1")]
MOD_POS = [pos for pos, p in enumerate(PIECES) if p[0][0] == "mod"]
START_ADA = KD * 3 // 2
ADA_DONE = {s: START_ADA + KD * n for n, s in enumerate(s for s in ADA_ORDER if s != 1)}
DIRECT_POS = [pos for pos, p in enumerate(PIECES) if p[0][0] == "down"]
assert len(SPLIT_POS) == NSPLIT and len(ADA_POS) == NADA * KD - KD // 2


def heads_piece(n):
    per = 4 * (len(HEAD_GROUPS) + 3 * len(BRANCHES) + 2)
    return n % (per + 2 * NF) < 4 * len(HEAD_GROUPS)


def low_owners():
    count = {"V": 0, "G": 0}
    out = []
    for n in range(NSPLIT):
        who = "G" if heads_piece(n) or n % 4 else "V"
        count[who] += 1
        out.append((who, count[who]))
    return out, count


LOW, LOW0 = low_owners()


def emptied(plan, upto, who):
    return sum(1 for _, w in plan[:upto + 1] if w == who)


def program(nc, x, c, ada_w, ada_b, norm_mix_w, norm_ffn_w, w_in, conv_w, lb_logits, hgrn_norm_w,
            sgu_norm_w, sgu_w, sgu_b, w_br_a, w_br_b, w_br_c, w_o, ffn_w1, ffn_w3, ffn_w2,
            router_w, router_b, moe_w1, moe_w3, moe_w2, final_norm_w, out):
    W_BR = {"a": w_br_a, "b": w_br_b, "c": w_br_c}
    with ExitStack() as ctx:
        def sb(name, shape, dt=F32):
            return ctx.enter_context(nc.sbuf_tensor(name, shape, dt))

        def sem(name):
            return ctx.enter_context(nc.semaphore(name))

        psU = [ctx.enter_context(nc.psum_tensor(f"psU{i}", [P, 512], F32)) for i in range(4)]
        psA = [ctx.enter_context(nc.psum_tensor(f"psA{i}", [P, 512], F32)) for i in range(4)]

        T_BANKS = [psA[2 * (EVENT_AT["gather0"] % 2) + j] for j in range(2)]
        Y_BANKS = [psA[2 * ((EVENT_AT["gather0"] + 1) % 2) + j] for j in range(2)]

        raw = sb("raw", [P, RAW, PIECE])
        split = sb("split", [P, SPL, 2, PIECE], F32R)
        yS = sb("yS", [P, 2, HB, T], F32R)
        with ExitStack() as dense:
            hS = dense.enter_context(nc.sbuf_tensor("hS", [P, 2, KD, T], F32R))
            merged = dense.enter_context(nc.sbuf_tensor("merged", [P, KD, T], F32))
        hidE = sb("hidE", [P, 2, NF, CAP], F32R)
        xE = sb("xE", [P, 2, KD, CAP], F32R)
        sb("spare", [P, max(3 * KD * T - 2 * (NF + KD) * CAP, 0) + 2])
        adacc = sb("adacc", [P, D])
        xT = sb("xT", [P, KD, T])
        sig = sb("sig", [P, 4, 512])
        work = sb("work", [P, 10, 1024])
        sc = sb("sc", [P, 3, HB, P])
        masks = sb("masks", [P, NLEV - 1, P], U8)
        wT = sb("wT", [P, DEPTH, HB, P])
        sgub = sb("sgub", [P, DEPTH, HB, P])
        vecs = sb("vecs", [P, NA_ROWS + NB_ROWS])
        mod = sb("mod", [P, DEPTH, 48])
        wm = sb("wm", [P, DEPTH, 2, KD])
        cact = sb("cact", [P, KD])
        lbs = sb("lbs", [P, DEPTH, 3, HB])
        ident = sb("ident", [P, P])
        ones = sb("ones", [P, P])
        tri = sb("tri", [P, P])
        rstd = sb("rstd", [P, T])
        vst = sb("vst", [P, 8])
        eps = sb("eps", [P, 1])
        small = sb("small", [P, 16])
        iotas = sb("iotas", [P, 2, P], I32)
        rtw = sb("rtw", [P, KD, NE])
        rtb = sb("rtb", [P, NE])
        route = sb("route", [P, 12, 2 * NE])
        cur = sb("cur", [P, 8])
        slots = sb("slots", [P, CAP])
        items = sb("items", [P, MAXI + 1, 2])
        itemi = sb("itemi", [P, MAXI + 1], I32)
        nitem = sb("nitem", [P, 1], I32)
        mx8 = sb("mx8", [P, 2, 8])
        ix8 = sb("ix8", [P, 2, 8], U32)
        ov = sb("ov", [P, 8, NE * JEX])

        FB, KB, QB, GB, QT, KT, ITOK, AB, AC, AH = (work[:, j, :] for j in range(10))
        VTOK, UB, GS, YB, OSQ, OSD = AB, AC, KB, FB, KT, QT
        hidden0 = work[:, 0:6, :].rearrange("p a b -> p (a b)")[:, 0:NF * T].rearrange("p (f t) -> p f t", t=T)
        xrow = sig[:, :, :].rearrange("p a b -> p (a b)").rearrange("p (t d) -> p t d", t=TT)
        stackA = merged[:, 0, 0:P]
        stackB = merged[:, 1, 0:P]
        wrow = AC.rearrange("p (l g s) -> p l g s", l=DEPTH, g=HB)
        htok = work[:, 0:2, :]
        oacc = work[:, 4:6, :]
        ye = work[:, 6, :]
        scf = sc[:, :, :, :].rearrange("p a b c -> p (a b c)")
        gwT = scf[:, 0:2 * T].rearrange("p (a t) -> p a t", t=T)
        sel = scf[:, 2 * T:2 * T + 4 * CAP].rearrange("p (a t s) -> p a t s", a=2, t=TT)
        ada1 = work[:, 9, :]
        g2bc = work[:, 7, :]
        g2col = work[:, 8, :]
        fwbc = adacc[:, :]

        s_small = sem("small_loaded")
        s_x = sem("x_loaded")
        s_more = sem("later_small_loaded")
        s_fw = sem("finalw_loaded")
        s_out = sem("out_stored")
        s_down = sem("down_piece_used")
        s_afree = sem("ada_products")
        s_mpc = sem("mod_piece_used")
        s_pool = sem("pool_step")
        s_const = sem("constants_ready")
        s_unit = sem("unit_ready")
        s_uA = sem("act_unit_emptied")
        s_uD = sem("dve_unit_emptied")
        s_ev = sem("event_ready")
        s_eA = sem("act_event_emptied")
        s_eD = sem("dve_event_emptied")
        s_cact = sem("cact_ready")
        s_lbsig = sem("lb_sigmoid_ready")
        s_mod = sem("modulation_ready")
        s_sq = sem("squares_ready")
        s_xr = sem("normed_chunk_ready")
        s_hh = sem("h_high_ready")
        s_h = sem("h_low_ready")
        s_a = sem("act_step")
        s_v = sem("dve_step")
        s_sig = sem("sigmoid_ready")
        s_qk = sem("level_operands_ready")
        s_sc = sem("scores_zeroed")
        s_vst = sem("v_stat_ready")
        s_osq = sem("o_squares_ready")
        s_y = sem("branch_input_ready")
        s_yh = sem("branch_input_high")
        s_yl = sem("branch_input_low")
        s_mh = sem("merged_high")
        s_ml = sem("merged_low")
        s_mg = sem("merged_ready")
        s_sel = sem("selection_ready")
        s_gw = sem("gate_rows_ready")
        s_items = sem("items_ready")
        s_prob = sem("top2_prob_ready")
        s_zero = sem("expert_buffers_zeroed")
        s_rt = sem("routing_ready")
        s_fin = sem("final_rows_ready")
        s_raw = [sem(f"piece{i}_loaded") for i in range(RAW)]
        s_hi = sem("act_high_parts")
        s_lo = {"V": sem("dve_low_parts"), "G": sem("pool_low_parts")}
        s_used = sem("pieces_used")
        s_silu = sem("hidden_sigmoid_rows")
        s_hrow = sem("hidden_rows_ready")
        s_turn = sem("hidden_rows_turned")
        s_hhi = sem("hidden_high_ready")
        s_hlo = sem("hidden_low_ready")
        s_gath = sem("tokens_gathered")
        s_xhi = sem("tokens_high_ready")
        s_xlo = sem("tokens_low_ready")
        s_sct = sem("scatter_results")
        s_add = sem("scatter_added")
        s_gate = sem("gate_columns_ready")
        s_ye = sem("expert_rows_ready")

        block = ctx.enter_context(nc.Block())

        stacks = [
            (stackA[ADA_B:ADA_B + 96, :], ada_b.rearrange("l (r p) -> (l r) p", p=P)),
            (stackA[C_ROW:C_ROW + KD, :], c.rearrange("b (r p) -> (b r) p", p=P)),
            (stackA[LB_ROW:LB_ROW + 8, :], lb_logits.rearrange("l (r p) -> (l r) p", p=P)),
            (stackB[NMIX:NMIX + 16, :], norm_mix_w.rearrange("l (r p) -> (l r) p", p=P)),
            (stackB[NFFN:NFFN + 16, :], norm_ffn_w.rearrange("l (r p) -> (l r) p", p=P)),
            (stackB[CONV:CONV + 24, :], conv_w.rearrange("l w (r p) -> (l w r) p", p=P)),
            (stackB[HNW:HNW + 8, :], hgrn_norm_w.rearrange("l (r p) -> (l r) p", p=P)),
            (stackB[SNW:SNW + 8, :], sgu_norm_w.rearrange("l (r p) -> (l r) p", p=P)),
        ]
        more_small = [
            (wrow.rearrange("p l g s -> p (l g) s"), sgu_w.rearrange("l g t s -> t (l g) s")),
            (sgub[:, :, :, :].rearrange("p l g t -> p (l g t)"),
             sgu_b.rearrange("(a l) g t -> a (l g t)", a=1).to_broadcast([P, DEPTH * HB * P])),
            (rtw[:, :, :], router_w[0].rearrange("(k p) e -> p k e", p=P)),
            (rtb[:, :], router_b.to_broadcast([P, NE])),
        ]

        @block.sync
        def _(sp):
            xr = x[0].rearrange("(t p) d -> p t d", p=P)
            sp.dma_start(xrow, xr).then_inc(s_x, 16)
            tensors = {"ada_w": ada_w, "w_in": w_in, "w_o": w_o, "ffn_w1": ffn_w1, "ffn_w3": ffn_w3, "ffn_w2": ffn_w2,
                       "w_br_a": w_br_a, "w_br_b": w_br_b, "w_br_c": w_br_c}
            ordinal = {pos: n for n, pos in enumerate(SPLIT_POS)}
            ada_n = {pos: n for n, pos in enumerate(ADA_POS)}

            def released(pos):
                use = PIECES[pos][0]
                if use == "split":
                    who, count = LOW[ordinal[pos]]
                    sp.wait_ge(s_lo[who], count)
                elif use[0] in ("ada", "ada1"):
                    sp.wait_ge(s_afree, ada_n[pos] + 1)
                elif use[0] == "mod":
                    sp.wait_ge(s_mpc, use[1] + 1)
                elif use[1] < NF - 1:
                    sp.wait_ge(s_down, use[1] + 1)
                else:
                    sp.wait_ge(s_ev, EVENT_AT["down1"] + 1)

            sp.wait_ge(s_small, 16 * len(stacks))
            for pos, (_, name, l, row, col, cols) in enumerate(PIECES):
                if pos >= RAW:
                    released(pos - RAW)
                k = PIECE // cols
                src = tensors[name][l, row:row + k * P, col:col + cols].rearrange("(k p) n -> p k n", p=P)
                sp.dma_start(raw[:, pos % RAW, :].rearrange("p (k n) -> p k n", k=k), src) \
                    .then_inc(s_raw[pos % RAW], 16)

            def item_sources(e):
                w1, w3 = (w[0, bass.ds(e, 1)].rearrange("a d f -> (a d) f") for w in (moe_w1, moe_w3))
                w2 = moe_w2[0, bass.ds(e, 1)].rearrange("a f d -> (a f) d")
                src = []
                for g, tiles in enumerate(GROUPS):
                    k = PIECE // (P * len(tiles))
                    cols = slice(tiles[0] * P, (tiles[-1] + 1) * P)
                    src += [(k, w[q * k * P:(q + 1) * k * P, cols].rearrange("(k p) n -> p k n", p=P))
                            for w in (w1, w3) for q in range(KD // k)]
                return src + [(1, w2[f * P:(f + 1) * P, :].rearrange("(k p) n -> p k n", p=P)) for f in range(NF)]

            def load_piece(n, k, src):
                slot = (RAW0 + n) % RAW
                sp.dma_start(raw[:, slot, :].rearrange("p (k n) -> p k n", k=k), src).then_inc(s_raw[slot], 16)

            def first_pieces(i, e):
                for n, (k, src) in enumerate(item_sources(e)[:RAW]):
                    sp.lower_ap(src)
                    who, count = low_part(NPC - RAW + n)
                    sp.wait_ge(s_lo[who], (i - 1) * LOWS[who] + (LOW0[who] + count))
                    load_piece(n, k, src)

            def other_pieces(i, e):
                for n, (k, src) in list(enumerate(item_sources(e)))[RAW:]:
                    sp.lower_ap(src)
                    who, count = low_part(n - RAW)
                    sp.wait_ge(s_lo[who], i * LOWS[who] + (LOW0[who] + count))
                    load_piece(n, k, src)

            for n, (k, src) in enumerate(item_sources(0)[:RAW]):
                released(RAW0 - RAW + n)
                load_piece(n, k, src)
            with sp.Fori(0, NE - 1) as e:
                other_pieces(e, e)
                first_pieces(e + 1, e + 1)
            other_pieces(NE - 1, NE - 1)
            sp.wait_ge(s_items, 1)
            n_items = sp.value_load(nitem[0:1, 0:1], min_val=NE, max_val=MAXI)
            with sp.If(n_items > NE):
                with sp.Fori(NE, n_items) as i:
                    e = sp.value_load(itemi[0:1, bass.ds(i, 1)], min_val=0, max_val=NE - 1)
                    first_pieces(i, e)
                    other_pieces(i, e)
            for tt in range(TT):
                sp.wait_ge(s_fin, tt + 1)
                sp.dma_start(out[0, tt * P:(tt + 1) * P, :], oacc[:, tt, :]).then_inc(s_out, 16)
            sp.wait_ge(s_out, 16 * TT)

        @block.gpsimd
        def _(pool):
            step = 0

            def link(ins):
                nonlocal step
                step += 1
                ins.then_inc(s_pool, 1)
                pool.wait_ge(s_pool, step)

            pool.memset(ones[:, :], 1.0).then_inc(s_const, 1)
            link(pool.memset(ident[:, :], 0.0))
            pool.affine_select(out=ident[:, :], in_=ident[:, :], compare_op=ALU.not_equal, fill=1.0, base=0,
                               pattern=[[-1, P]], channel_multiplier=1).then_inc(s_const, 1)
            pool.iota(iotas[:, 0, :], pattern=[[0, P]], base=0, channel_multiplier=1).then_inc(s_const, 1)
            pool.iota(iotas[:, 1, :], pattern=[[1, P]], base=0, channel_multiplier=0).then_inc(s_const, 1)
            link(pool.memset(tri[:, :], 1.0))
            pool.affine_select(out=tri[:, :], in_=tri[:, :], compare_op=ALU.is_ge, fill=0.0, base=0,
                               pattern=[[1, P]], channel_multiplier=-1).then_inc(s_const, 1)
            pool.iota(slots[:, :], pattern=[[1, CAP]], base=1, channel_multiplier=0,
                      allow_small_or_imprecise_dtypes=True).then_inc(s_const, 1)
            pool.iota(small[:, 8:16], pattern=[[1, NE]], base=0, channel_multiplier=0,
                      allow_small_or_imprecise_dtypes=True).then_inc(s_const, 1)
            pool.iota(ov[:, 0, :], pattern=[[0, JEX], [1, NE]], base=1, channel_multiplier=0,
                      allow_small_or_imprecise_dtypes=True).then_inc(s_const, 1)
            pool.iota(ov[:, 1, :], pattern=[[CAP, JEX], [0, NE]], base=CAP, channel_multiplier=0,
                      allow_small_or_imprecise_dtypes=True).then_inc(s_const, 1)
            pool.memset(sc[:, :, :, :], 0.0).then_inc(s_sc, 1)
            def low(n):
                pool.wait_ge(s_hi, n + 1)
                pool.tensor_tensor(split[:, n % SPL, 1, :], raw[:, SPLIT_POS[n] % RAW, :],
                                   split[:, n % SPL, 0, :].bitcast(F32), ALU.subtract).then_inc(s_lo["G"], 1)

            for n in range(NSPLIT):
                if n == (NSPLIT + 2 * NF) // 2:
                    pool.wait_ge(s_ev, EVENT_AT[(0, "o")] + 1)
                    pool.memset(sc[:, :, :, :], 0.0).then_inc(s_sc, 1)
                if LOW[n][0] == "G":
                    low(n)
            pool.wait_ge(s_unit, SIGNAL["mod", 10][1])
            pool.dma_start(fwbc, final_norm_w.rearrange("(a d) -> a d", a=1).to_broadcast([P, D])).then_inc(s_fw, 16)
            pool.wait_ge(s_uD, emptied(UNITS, UNIT_AT[(1, "wo", 3)], "D"))
            pool.memset(ye, 0.0).then_inc(s_zero, 1)
            pool.memset(gwT[:, 0, :], 0.0).then_inc(s_zero, 1)
            pool.wait_ge(s_items, 1)
            n_items = pool.value_load(nitem[0:1, 0:1], min_val=NE, max_val=MAXI)
            with pool.Fori(0, n_items) as i:
                for n in range(NPC):
                    if low_part(n)[0] == "G":
                        pool.wait_ge(s_hi, i * NPC + (NSPLIT + n + 1))
                        slot = (NSPLIT + n) % SPL
                        pool.tensor_tensor(split[:, slot, 1, :], raw[:, (RAW0 + n) % RAW, :],
                                           split[:, slot, 0, :].bitcast(F32), ALU.subtract).then_inc(s_lo["G"], 1)

        @block.tensor
        def _(pe):
            units, events, pieces, direct = [0], [0], [0], [0]

            def open_unit(key):
                n = units[0]
                assert UNITS[n][0] == key, (key, UNITS[n])
                if n >= 4:
                    who = UNITS[n - 4][1]
                    pe.wait_ge(s_uA if who == "A" else s_uD, emptied(UNITS, n - 4, who))
                units[0] += 1
                return psU[n % 4]

            def open_event(key):
                n = events[0]
                assert EVENTS[n][0] == key, (key, EVENTS[n])
                if n >= 2:
                    who = EVENTS[n - 2][1]
                    pe.wait_ge(s_eA if who == "A" else s_eD, emptied(EVENTS, n - 2, who))
                events[0] += 1
                return psA[2 * (n % 2)], psA[2 * (n % 2) + 1]

            def mm(o, a, b, start, stop):
                return pe.matmul(o, a, b, start=start, stop=stop, skip_group_check=True)

            def next_split():
                n = pieces[0]
                pieces[0] += 1
                who, count = LOW[n]
                pe.wait_ge(s_lo[who], count)
                return split[:, n % SPL, 0, :], split[:, n % SPL, 1, :]

            def next_direct():
                pos = DIRECT_POS[direct[0]]
                direct[0] += 1
                pe.wait_ge(s_raw[pos % RAW], 16 * (pos // RAW + 1))
                return raw[:, pos % RAW, :]

            PASSES = ((0, 0), (0, 1), (1, 0))

            def tile(o, w, k, cols, first, end, x=None):
                for wp, hp in PASSES:
                    last = mm(o, w[wp][:, cols:cols + P], (x or hS)[:, hp, k, :], first and (wp, hp) == PASSES[0],
                              end and (wp, hp) == PASSES[-1])
                return last

            def project(key, chunk=None):
                for j in range(2):
                    bank = open_unit(key(j))
                    for q in range(2):
                        w = next_split()
                        for m in range(2):
                            for kk in range(4):
                                if chunk and j == 0 and m == 0:
                                    chunk(4 * q + kk)
                                last = tile(bank[:, m * T:(m + 1) * T], w, 4 * q + kk, kk * 256 + m * P,
                                            q == 0 and m == 0 and kk == 0, q == 1 and kk == 3)
                        last.then_inc(s_used, 1)
                    yield j

            def project_rows(key):
                banks = [open_unit(key(tt)) for tt in range(TT)]
                for q in range(4):
                    w = next_split()
                    for tt in range(TT):
                        for kk in range(2):
                            for wp, hp in ((0, 0), (1, 0), (0, 1)):
                                last = mm(banks[tt][:, :], hS[:, hp, 2 * q + kk, tt * P:(tt + 1) * P],
                                          w[wp][:, kk * 512:(kk + 1) * 512], (q, kk, wp, hp) == (0, 0, 0, 0),
                                          (q, kk, hp) == (3, 1, 1))
                    last.then_inc(s_used, 1)
                    if q % 2:
                        yield q // 2

            def norm_stat(key, count):
                bank, _ = open_event(key)
                for k in range(KD):
                    if k % 2 == 0:
                        pe.wait_ge(s_sq, 4 * (count - 1) + k // 2 + 1)
                    last = mm(bank[:, 0:T], ones[:, :], sig[:, k // 2, (k % 2) * T:(k % 2 + 1) * T],
                              k == 0, k == KD - 1)
                last.then_inc(s_ev, 1)

            def ada_sum(s):
                pe.wait_ge(s_afree, ADA_DONE[s])
                bank = open_unit(("mod", s)) if s in DOWN_ADA else open_event(("ada", s))[0]
                for k in range(KD):
                    last = mm(bank[:, k:k + 1], adacc[:, k * P:(k + 1) * P], ones[:, 0:1], True, True)
                last.then_inc(s_unit if s in DOWN_ADA else s_ev, 1)

            def ada_direct():
                bank, _ = open_event(("ada", 1))
                pe.wait_ge(s_afree, 1)
                for n, pos in enumerate(MOD_POS):
                    pe.wait_ge(s_raw[pos % RAW], 16 * (pos // RAW + 1))
                    for m in range(KD):
                        last = mm(bank[:, m:m + 1], raw[:, pos % RAW, m * P:(m + 1) * P], cact[:, 2 * n + 1:2 * n + 2],
                                  n == 0 and m == 0, False)
                    last.then_inc(s_mpc, 1)
                pe.wait_ge(s_afree, START_ADA)
                for m in range(KD):
                    last = mm(bank[:, m:m + 1], ada1[:, m * P:(m + 1) * P], ones[:, 0:1], False, True)
                last.then_inc(s_ev, 1)

            def level(l, j):
                if j == 0:
                    pe.wait_ge(s_uD, emptied(UNITS, UNIT_AT[(l, "q", 1)], "D"))
                else:
                    pe.wait_ge(s_qk, l * (NLEV - 1) + j)
                banks = open_event((l, "lev", j))
                ks, qs = (KB, QB) if j == 0 else (KT, QT)
                for tt in range(TT if j < NLEV - 1 else 1):
                    for h in range(HB):
                        s0 = h * T + tt * P
                        t0 = s0 if j < NLEV - 1 else h * T + P
                        last = mm(banks[tt][:, h * P:(h + 1) * P], ks[:, s0:s0 + P], qs[:, t0:t0 + P], True, True)
                last.then_inc(s_ev, 1)

            def sgu_mix(l):
                pe.wait_ge(s_uD, emptied(UNITS, UNIT_AT[(l, "v", 1)], "D"))
                banks = open_event((l, "sgu"))
                for g in range(HB):
                    for tt in range(TT):
                        col = (g % 2) * T + tt * P
                        last = mm(banks[g // 2][:, col:col + P], VTOK[:, tt * 512 + g * P:tt * 512 + (g + 1) * P],
                                  wT[:, l, g, :], True, True)
                last.then_inc(s_ev, 1)

            def attend(l):
                pe.wait_ge(s_eD, emptied(EVENTS, EVENT_AT[(l, "lev", NLEV - 1)], "D"))
                pe.wait_ge(s_uA, emptied(UNITS, UNIT_AT[(l, "i", 1)], "A"))
                banks = open_event((l, "o"))
                for h in range(HB):
                    v0, v1 = (ITOK[:, tt * 512 + h * P:tt * 512 + (h + 1) * P] for tt in range(TT))
                    col = (h % 2) * T
                    o = banks[h // 2]
                    mm(o[:, col:col + P], v0, sc[:, 0, h, :], True, True)
                    mm(o[:, col + P:col + T], v0, sc[:, 2, h, :], True, False)
                    last = mm(o[:, col + P:col + T], v1, sc[:, 1, h, :], False, True)
                last.then_inc(s_ev, 1)

            def head_stat(l):
                pe.wait_ge(s_osq, l + 1)
                banks = open_event((l, "ostat"))
                for j in range(2):
                    last = mm(banks[j][:, :], ones[:, :], OSQ[:, j * 512:(j + 1) * 512], True, True)
                last.then_inc(s_ev, 1)

            def mixer(l):
                norm_stat((l, "norm1"), 2 * l + 1)
                if l == 0:
                    ada_direct()
                    ada_sum(0)

                def chunk(k):
                    if k % 2 == 0:
                        pe.wait_ge(s_h, 8 * l + k // 2 + 1)
                lev = 0
                for g in HEAD_GROUPS:
                    rows = g in ("i", "v")
                    run = project_rows(lambda j: (l, g, j)) if rows else \
                        project(lambda j: (l, g, j), chunk if g == "f" else None)
                    for j in run:
                        if lev < NLEV and (g, j) not in NO_LEVEL:
                            level(l, lev)
                            lev += 1
                        if (g, j) == ("u", 0):
                            sgu_mix(l)
                            attend(l)
                        if (g, j) == ("g", 0):
                            head_stat(l)
                    if l == 0 and g == "q":
                        turn_gating()
                for n, b in enumerate(BRANCHES):
                    for gg in range(2):
                        for _ in project(lambda j: (l, "gate" + b, 2 * gg + j)):
                            pass
                    for j in range(4):
                        bank = open_unit((l, "y" + b, j))
                        if j == 0:
                            pe.wait_ge(s_yl, 3 * l + n + 1)
                        w = next_split()
                        for m in range(2):
                            for k in range(4):
                                last = tile(bank[:, m * T:(m + 1) * T], w, k, k * 256 + m * P,
                                            m == 0 and k == 0, k == 3, yS)
                        last.then_inc(s_used, 1)
                    if l == 0 and n < 2:
                        ada_sum(2 + n)

                def chunk_m(k):
                    if k % 2 == 0:
                        pe.wait_ge(s_ml, 4 * l + k // 2 + 1)
                for j in range(4):
                    bank = open_unit((l, "wo", j))
                    for q in range(2):
                        w = next_split()
                        for m in range(2):
                            for kk in range(4):
                                if j == 0 and m == 0:
                                    chunk_m(4 * q + kk)
                                last = tile(bank[:, m * T:(m + 1) * T], w, 4 * q + kk, kk * 256 + m * P,
                                            q == 0 and m == 0 and kk == 0, q == 1 and kk == 3)
                        last.then_inc(s_used, 1)
                if l == 0:
                    ada_sum(4)
                norm_stat((l, "norm2"), 2 * l + 2)

            def dense_ffn():
                for pair in range(NF // 2):
                    banks = [open_unit(("ffn", 2 * pair + m)) for m in range(2)]
                    for which in range(2):
                        for q in range(2):
                            w = next_split()
                            for m in range(2):
                                for kk in range(4):
                                    k = 4 * q + kk
                                    if pair == 0 and which == 0 and m == 0 and k % 2 == 0:
                                        pe.wait_ge(s_h, 4 + k // 2 + 1)
                                    last = tile(banks[m][:, which * T:(which + 1) * T], w, k, kk * 256 + m * P,
                                                k == 0, k == KD - 1)
                            last.then_inc(s_used, 1)
                    if pair in FFN_SUMS:
                        ada_sum(FFN_SUMS[pair])
                for key in ("down0", "down1"):
                    banks = open_event(key)
                    if key == "down0":
                        four = list(banks)
                    else:
                        four += list(banks)
                for f in range(NF):
                    w = next_direct()
                    if f % 2 == 0:
                        pe.wait_ge(s_uD, emptied(UNITS, UNIT_AT[("ffn", f + 1)], "D"))
                    for m in range(KD):
                        last = mm(four[m // 2][:, (m % 2) * T:(m % 2 + 1) * T], w[:, m * P:(m + 1) * P],
                                  hidden0[:, f, :], f == 0 and m % 2 == 0, f == NF - 1)
                        if f == NF - 1 and m == 3:
                            last.then_inc(s_ev, 1)
                    last.then_inc(s_down if f < NF - 1 else s_ev, 1)
                    if f in (6, 12, 18):
                        ada_sum(DOWN_ADA[f // 6 - 1])

            def turn_gating():
                pe.wait_ge(s_more, 16 * len(more_small))
                for l in range(DEPTH):
                    bank = open_unit(("wt", l))
                    for g in range(HB):
                        last = pe.transpose(bank[:, g * P:(g + 1) * P], wrow[:, l, g, :], ident[:, :])
                    last.then_inc(s_unit, 1)

            pe.wait_ge(s_const, 2)
            pe.wait_ge(s_x, 16)
            for j in range(4):
                bank = open_unit(("x", j))
                for m in range(2):
                    for tt in range(TT):
                        last = pe.transpose(bank[:, m * T + tt * P:m * T + (tt + 1) * P],
                                            xrow[:, tt, (2 * j + m) * P:(2 * j + m + 1) * P], ident[:, :])
                last.then_inc(s_unit, 1)
            pe.wait_ge(s_small, 16 * len(stacks))
            bank = open_unit(("vec", 0))
            pe.transpose(bank[:, 0:NA_ROWS], stackA[0:NA_ROWS, :], ident[0:NA_ROWS, 0:NA_ROWS])
            pe.transpose(bank[:, NA_ROWS:NA_ROWS + NB_ROWS], stackB[0:NB_ROWS, :],
                         ident[0:NB_ROWS, 0:NB_ROWS]).then_inc(s_unit, 1)
            mixer(0)
            dense_ffn()
            mixer(1)

            pe.wait_ge(s_zero, 2)
            pe.wait_ge(s_eA, emptied(EVENTS, EVENT_AT[(1, "norm2")], "A"))
            for half in range(2):
                last = mm(Y_BANKS[half][0:CAP, :], gwT[:, 0, 0:CAP], ye[:, half * 512:(half + 1) * 512], True, True)
            last.then_inc(s_used, 1)

            bank = open_unit("logits")
            for tt in range(TT):
                for k in range(KD):
                    if tt == 0:
                        pe.wait_ge(s_hh, 3 * KD // 2 + k // 2 + 1)
                    last = mm(bank[:, tt * NE:(tt + 1) * NE], merged[:, k, tt * P:(tt + 1) * P], rtw[:, k, :],
                              k == 0, k == KD - 1)
            last.then_inc(s_unit, 1)
            pe.wait_ge(s_rt, 1)
            bank = open_unit("rank")
            mm(bank[:, 0:NE], tri[:, :], route[:, 0, 0:NE], True, True)
            mm(bank[:, NE:2 * NE], ones[:, :], route[:, 0, 0:NE], True, False)
            mm(bank[:, NE:2 * NE], tri[:, :], route[:, 0, NE:2 * NE], False, True)
            mm(bank[:, 2 * NE:3 * NE], ones[:, :], route[:, 0, 0:NE], True, False)
            mm(bank[:, 2 * NE:3 * NE], ones[:, :], route[:, 0, NE:2 * NE], False, True).then_inc(s_unit, 1)
            for key, src in (("htok", merged), ("xtok", xT)):
                for j in range(4):
                    bank = open_unit((key, j))
                    tt, half = j // 2, j % 2
                    for m in range(4):
                        last = pe.transpose(bank[:, m * P:(m + 1) * P],
                                            src[:, 4 * half + m, tt * P:(tt + 1) * P], ident[:, :])
                    last.then_inc(s_unit, 1)
            pe.wait_ge(s_gw, 1)
            for j in range(2):
                bank = open_unit(("g2", j))
                for m in range(4):
                    last = mm(bank[:, m * P:(m + 1) * P], g2col[:, (4 * j + m) * P:(4 * j + m + 1) * P], ident[:, :], True, True)
                last.then_inc(s_unit, 1)

            def gather(banks):
                for m in range(KD):
                    for tt in range(TT):
                        last = mm(banks[m // 4][:, (m % 4) * CAP:(m % 4 + 1) * CAP], htok[:, tt, m * P:(m + 1) * P],
                                  sel[:, 0, tt, :], tt == 0, tt == 1)
                return last

            def turn_gates(bank):
                for tt in range(TT):
                    last = pe.transpose(bank[0:CAP, tt * P:(tt + 1) * P], sel[:, 1, tt, :], ident[:, :])
                return last

            def scatter(j):
                tt, half = j // 2, j % 2
                mm(psU[j][:, :], gwT[0:CAP, 0, tt * P:(tt + 1) * P], ye[0:CAP, half * 512:(half + 1) * 512],
                   True, True).then_inc(s_sct, 1)

            pe.wait_ge(s_sel, 1)
            pe.wait_ge(s_uA, emptied(UNITS, UNIT_AT[("htok", 3)], "A"))
            turn_gates(open_unit("sel0")).then_inc(s_unit, 1)
            gather(open_event("gather0")).then_inc(s_ev, 1)
            assert (units[0], events[0], pieces[0], direct[0]) == (len(UNITS), len(EVENTS), NSPLIT, len(DIRECT_POS))

            pe.wait_ge(s_uA, emptied(UNITS, len(UNITS), "A"))
            pe.wait_ge(s_items, 1)
            n_items = pe.value_load(nitem[0:1, 0:1], min_val=NE, max_val=MAXI)
            with pe.Fori(0, n_items) as i:
                def piece(n, stationary, outs):
                    who, count = low_part(n)
                    pe.wait_ge(s_lo[who], i * LOWS[who] + (LOW0[who] + count))
                    for xs, ws in ((0, 0), (0, 1), (1, 0)):
                        for o, k, cols, first, end in outs:
                            last = mm(o, stationary(xs, k), split[:, (NSPLIT + n) % SPL, ws, cols],
                                      first and xs == 0 and ws == 0, end and xs == 1)
                    last.then_inc(s_used, 1)

                def turn(g):
                    pe.wait_ge(s_hrow, i * len(GROUPS) + (g + 1))
                    if g >= 2:
                        pe.wait_ge(s_hlo, i * len(GROUPS) + (g - 1))
                    for m in range(len(GROUPS[g])):
                        last = pe.transpose(T_BANKS[g % 2][:, m * CAP:(m + 1) * CAP],
                                            sig[0:CAP, 2 + g % 2, m * P:(m + 1) * P], ident[0:CAP, 0:CAP])
                    last.then_inc(s_turn, 1)

                n = 0
                for g, tiles in enumerate(GROUPS):
                    width = len(tiles) * P
                    if g == 0:
                        pe.wait_ge(s_xlo, i + 1)
                    elif g == 1:
                        pe.wait_ge(s_gate, i + 1)
                    else:
                        pe.wait_ge(s_hrow, i * len(GROUPS) + (g - 1))
                    for which in range(2):
                        o = psU[2 * (g % 2) + which][0:CAP, 0:width]
                        per = PIECE // width
                        for q in range(KD // per):
                            piece(n, lambda xs, k: xE[:, xs, k, :],
                                  [(o, q * per + kk, slice(kk * width, (kk + 1) * width),
                                    q == 0 and kk == 0, q == KD // per - 1 and kk == per - 1) for kk in range(per)])
                            n += 1
                    if g:
                        turn(g - 1)
                pe.wait_ge(s_ye, i + 1)
                for j in range(2):
                    scatter(j)
                turn(len(GROUPS) - 1)
                for j in range(2, 4):
                    scatter(j)
                pe.wait_ge(s_sel, i + 2)
                pe.wait_ge(s_add, i * 4 + 1)
                turn_gates(psU[0]).then_inc(s_sct, 1)
                for f in range(NF):
                    if n == GATHER_AT:
                        pe.wait_ge(s_gate, i + 2)
                        gather(psU[0:2]).then_inc(s_gath, 1)
                    if f % 4 == 0:
                        pe.wait_ge(s_hlo, i * len(GROUPS) + (f // 4 + 1))
                    piece(n, lambda xs, k: hidE[:, xs, k, :],
                          [(Y_BANKS[half][0:CAP, :], f, slice(half * 512, (half + 1) * 512), f == 0, f == NF - 1)
                           for half in range(2)])
                    n += 1
            pe.wait_ge(s_ye, n_items + 1)
            pe.wait_ge(s_gate, n_items + 1)
            pe.wait_ge(s_xlo, n_items + 1)
            for j in range(4):
                scatter(j)

        @block.scalar
        def _(act):
            step = [0]

            def link(ins):
                step[0] += 1
                ins.then_inc(s_a, 1)
                act.wait_ge(s_a, step[0])

            split_now = [0]

            def high_parts(upto):
                for n in range(split_now[0], min(upto, NSPLIT)):
                    pos = SPLIT_POS[n]
                    act.wait_ge(s_raw[pos % RAW], 16 * (pos // RAW + 1))
                    if n >= SPL:
                        act.wait_ge(s_used, n - SPL + 1)
                    copy(split[:, n % SPL, 0, :], raw[:, pos % RAW, :]).then_inc(s_hi, 1)
                split_now[0] = max(split_now[0], min(upto, NSPLIT))

            def unit(key):
                kind, count, used = SIGNAL[key]
                upto = used + AHEAD
                if "gate" in str(key):
                    upto = min(upto, SIGNAL[key[0], key[1], 3][2] + 4)
                elif key[0] == "ffn":
                    upto = min(used + 4, SIGNAL["ffn", NF - 1][2])
                if used:
                    high_parts(upto)
                act.wait_ge(s_used if kind == "used" else s_unit, count)
                return psU[UNIT_AT[key] % 4]

            def event(key):
                n = EVENT_AT[key]
                act.wait_ge(s_ev, n + 1)
                return psA[2 * (n % 2)], psA[2 * (n % 2) + 1]

            def copy(o, i):
                return act.activation(o, i, ACT.Copy)

            for dst, src in stacks:
                act.dma_start(dst, src).then_inc(s_small, 16)
            for j in range(4):
                copy(xT[:, 2 * j:2 * j + 2, :].rearrange("p a b -> p (a b)"), unit(("x", j))[:, :]).then_inc(s_uA, 1)
            copy(vecs[:, :], unit(("vec", 0))[:, 0:NA_ROWS + NB_ROWS]).then_inc(s_uA, 1)
            act.wait_ge(s_uA, 5)
            act.activation(cact[:, :], vecs[:, C_ROW:C_ROW + KD], ACT.Sigmoid).then_inc(s_cact, 1)
            act.wait_ge(s_lbsig, 1)
            act.activation(lbs[:, 1, 0, :], lbs[:, 1, 1, :], ACT.Sigmoid).then_inc(s_cact, 1)

            def std(o, i, n):
                return act.activation(o, i, ACT.Sqrt, scale=1.0 / n, bias=eps[:, :])

            def norm(l, second):
                used = SIGNAL[l, "wo", 3][2] if second else SIGNAL["ffn", NF - 1][2] if l else 0
                if l and not second:
                    high_parts(used + 4)
                for j in range(4):
                    if second:
                        high_parts(SIGNAL[l, "wo", j][2] + AHEAD)
                        act.wait_ge(s_uD, emptied(UNITS, UNIT_AT[(l, "wo", j)], "D"))
                    elif l and j % 2 == 0:
                        act.wait_ge(s_eD, emptied(EVENTS, EVENT_AT[f"down{j // 2}"], "D"))
                    act.activation(sig[:, j, :], xT[:, 2 * j:2 * j + 2, :].rearrange("p a b -> p (a b)"),
                                   ACT.Square).then_inc(s_sq, 1)
                bank, _ = event((l, "norm2" if second else "norm1"))
                std(rstd[:, :], bank[:, 0:T], D).then_inc(s_eA, 1)
                high_parts(used + (SPL if l or second else 4))
                for k in range(KD):
                    act.wait_ge(s_xr, KD * (2 * l + second) + k + 1)
                    sh = 24 * second + k
                    experts = (l, second) == (1, 1)
                    dst = merged[:, k, :] if experts else hS[:, 0, k, :]
                    ins = act.activation(dst, merged[:, k, :], ACT.Identity, bias=mod[:, l, sh:sh + 1])
                    if k % 2:
                        ins.then_inc(s_hh, 1)

            def half(buf, j):
                return buf[:, j * 512:(j + 1) * 512]

            def mixer(l):
                norm(l, 0)
                if l == 0:
                    for dst, src in more_small:
                        act.dma_start(dst, src).then_inc(s_more, 16)
                for g in HEAD_GROUPS:
                    for j in range(2):
                        if g == "ah":
                            continue
                        bank = unit((l, g, j))
                        if g == "f":
                            act.activation(half(FB, j), bank[:, :], ACT.Sigmoid)
                            act.activation(half(KB, j), bank[:, :], ACT.Sigmoid, scale=-1.0).then_inc(s_uA, 1)
                        elif g in ("q", "g"):
                            act.activation(sig[:, j, :], bank[:, :], ACT.Sigmoid).then_inc(s_sig, 1)
                        elif g == "v":
                            link(act.activation(sig[:, 2 + j, :], bank[:, :], ACT.Square, accum_out=vst[:, j:j + 1]))
                            std(vst[:, 2 + j:3 + j], vst[:, j:j + 1], 512).then_inc(s_vst, 1)
                        else:
                            if g == "u" and j == 0:
                                act.wait_ge(s_y, 3 * l + 1)
                            copy(half({"ab": AB, "ac": AC, "i": ITOK, "u": UB}[g], j), bank[:, :]).then_inc(s_uA, 1)
                        if (g, j) == ("g", 0):
                            banks = event((l, "ostat"))
                            std(half(OSD, 0), banks[0][:, :], P)
                            std(half(OSD, 1), banks[1][:, :], P).then_inc(s_eA, 1)
                        if (g, j) == ("u", 0):
                            banks = event((l, "o"))
                            act.activation(half(OSQ, 0), banks[0][:, :], ACT.Square)
                            act.activation(half(OSQ, 1), banks[1][:, :], ACT.Square).then_inc(s_osq, 1)
                for n, b in enumerate(BRANCHES):
                    for j in range(4):
                        bank = unit((l, "gate" + b, j))
                        if n == 0:
                            act.wait_ge(s_uD, emptied(UNITS, UNIT_AT[(l, "g", 1)], "D"))
                        elif n == 1:
                            act.wait_ge(s_uD, emptied(UNITS, UNIT_AT[(l, "ya", j)], "D"))
                        else:
                            act.wait_ge(s_mg, 8 * l + j + 1)
                        act.activation(sig[:, j, :], bank[:, :], ACT.Sigmoid).then_inc(s_uA, 1)
                        if j == 0:
                            act.wait_ge(s_y, 3 * l + {"a": 1, "c": 2, "b": 3}[b])
                            src = {"a": AH, "c": UB, "b": YB}[b]
                            copy(yS[:, 0, :, :].rearrange("p a b -> p (a b)"), src).then_inc(s_yh, 1)
                high_parts(SIGNAL[l, "gateb", 3][2] + 4 + 4)
                for j in range(4):
                    act.wait_ge(s_mg, 8 * l + 4 + j + 1)
                    copy(hS[:, 0, 2 * j:2 * j + 2, :].rearrange("p a b -> p (a b)"),
                         merged[:, 2 * j:2 * j + 2, :].rearrange("p a b -> p (a b)")).then_inc(s_mh, 1)
                norm(l, 1)

            mixer(0)
            for f in range(NF):
                bank = unit(("ffn", f))
                act.activation(sig[:, f % 4, 0:T], bank[:, 0:T], ACT.Sigmoid).then_inc(s_sig, 1)
            mixer(1)

            def item_high(i, n):
                pos = RAW0 + n
                act.wait_ge(s_raw[pos % RAW], i * (16 * NPC // RAW) + 16 * (pos // RAW + 1))
                act.wait_ge(s_used, i * NPC + (USED0 + n - SPL + 1))
                copy(split[:, (NSPLIT + n) % SPL, 0, :], raw[:, pos % RAW, :]).then_inc(s_hi, 1)

            for n in range(SPL):
                item_high(0, n)
            act.wait_ge(s_prob, 1)
            act.activation(cur[:, 2:4], cur[:, 0:2], ACT.Sigmoid)
            act.activation(cur[:, 4:6], cur[:, 0:2], ACT.Sigmoid, scale=-1.0).then_inc(s_prob, 1)
            for key, dst in (("htok", htok), ("xtok", oacc)):
                for j in range(4):
                    copy(dst[:, j // 2, (j % 2) * 512:(j % 2 + 1) * 512], unit((key, j))[:, :]).then_inc(s_uA, 1)
            for j in range(2):
                copy(g2bc[:, j * 512:(j + 1) * 512], unit(("g2", j))[:, :]).then_inc(s_uA, 1)

            def tokens(banks):
                for j in range(2):
                    last = copy(xE[:, 0, 4 * j:4 * j + 4, :].rearrange("p a b -> p (a b)"), banks[j][:, 0:4 * CAP])
                last.then_inc(s_xhi, 1)

            tokens(event("gather0"))
            act.wait_ge(s_items, 1)
            n_items = act.value_load(nitem[0:1, 0:1], min_val=NE, max_val=MAXI)

            def item(i, first):
                def sigmoid_rows(g):
                    width = len(GROUPS[g]) * P
                    act.wait_ge(s_used, i * NPC + (USED0 + G_W1[g]))
                    act.activation(sig[0:CAP, g % 2, 0:width], psU[2 * (g % 2)][0:CAP, 0:width],
                                   ACT.Sigmoid).then_inc(s_silu, 1)

                def tiles_high(g):
                    tiles = GROUPS[g]
                    act.wait_ge(s_turn, i * len(GROUPS) + (g + 1))
                    copy(hidE[:, 0, tiles[0]:tiles[-1] + 1, :].rearrange("p a b -> p (a b)"),
                         T_BANKS[g % 2][:, 0:len(tiles) * CAP]).then_inc(s_hhi, 1)

                for n in range(NPC):
                    if n >= first:
                        item_high(i, n)
                    for g in range(len(GROUPS)):
                        if n == G_W1[g] - 1 + AHEAD:
                            sigmoid_rows(g)
                        if n == (G_END[g + 1] - 1 + AHEAD if g < len(GROUPS) - 1 else HID + AHEAD):
                            tiles_high(g)
                    if n == GATHER_AT - 1 + AHEAD:
                        act.wait_ge(s_gath, i + 1)
                        tokens(psU[0:2])
            item(0, SPL)
            with act.Fori(1, n_items) as i:
                item(i, 0)
            for tt in range(TT):
                act.wait_ge(s_add, n_items * 4 + (2 * tt + 2))
                act.activation(work[:, 8 + tt, :], oacc[:, tt, :], ACT.Square, accum_out=vst[:, tt:tt + 1]).then_inc(s_a, 1)
                step[0] += 1
                act.wait_ge(s_a, step[0])
                std(vst[:, 2 + tt:3 + tt], vst[:, tt:tt + 1], D).then_inc(s_vst, 1)

        @block.vector
        def _(dve):
            step = [0]

            def link(ins):
                step[0] += 1
                ins.then_inc(s_v, 1)

            def settle():
                dve.wait_ge(s_v, step[0])

            split_now = [0]

            def low_parts(upto):
                for n in range(split_now[0], min(upto, NSPLIT)):
                    if LOW[n][0] == "V":
                        dve.wait_ge(s_hi, n + 1)
                        TTN(split[:, n % SPL, 1, :], raw[:, SPLIT_POS[n] % RAW, :],
                            split[:, n % SPL, 0, :].bitcast(F32), ALU.subtract).then_inc(s_lo["V"], 1)
                split_now[0] = max(split_now[0], min(upto, NSPLIT))

            def unit(key):
                kind, count, used = SIGNAL[key]
                upto = used + AHEAD - 1
                if key[0] in ("ffn", "mod"):
                    upto = min(upto, SIGNAL["ffn", NF - 1][2])
                if used:
                    low_parts(upto)
                dve.wait_ge(s_used if kind == "used" else s_unit, count)
                return psU[UNIT_AT[key] % 4]

            def unit_done(key):
                dve.wait_ge(s_uD, emptied(UNITS, UNIT_AT[key], "D"))

            def event(key):
                n = EVENT_AT[key]
                dve.wait_ge(s_ev, n + 1)
                return psA[2 * (n % 2)], psA[2 * (n % 2) + 1]

            TTN, TS, STT = dve.tensor_tensor, dve.tensor_scalar, dve.scalar_tensor_tensor
            BV = NA_ROWS

            link(dve.memset(eps[:, :], EPS))
            link(dve.memset(work[:, 4:6, :], 0.0))
            link(dve.memset(items[:, :, :], 0.0))
            dve.wait_ge(s_const, 9)
            xor = work[:, 0, 0:P].bitcast(I32)
            above = work[:, 1, 0:P]
            link(TTN(xor, iotas[:, 0, :], iotas[:, 1, :], ALU.bitwise_xor))
            link(TTN(above, iotas[:, 1, :], iotas[:, 0, :], ALU.is_gt))
            settle()
            for j in range(8):
                link(STT(work[:, 2, j * P:(j + 1) * P], xor, float(2 ** j), above, ALU.is_ge, ALU.mult))
            link(dve.tensor_copy(masks[:, 0, :], ident[:, :]))
            settle()
            for j in range(1, 8):
                a = work[:, 2, (j - 1) * P:j * P]
                link(TTN(masks[:, j, :], a, work[:, 2, j * P:(j + 1) * P], ALU.subtract))
            dve.wait_ge(s_cact, 1)
            link(TTN(cact[:, :], cact[:, :], vecs[:, C_ROW:C_ROW + KD], ALU.mult))
            TTN(lbs[:, 1, 1, :], vecs[:, LB_ROW + HB:LB_ROW + 2 * HB], vecs[:, LB_ROW:LB_ROW + HB],
                ALU.subtract).then_inc(s_lbsig, 1)
            link(dve.memset(lbs[:, 0, 1, :], 1.0))
            link(dve.memset(lbs[:, 0, 2, :], LB_FLOOR))
            dve.wait_ge(s_cact, 2)
            link(TS(lbs[:, 1, 0, :], lbs[:, 1, 0, :], 0.0, 1.0, ALU.max, ALU.min))
            settle()
            link(TS(lbs[:, 1, 1, :], lbs[:, 1, 0, :], -1.0, 1.0, ALU.mult, ALU.add))
            link(TS(lbs[:, 1, 2, :], lbs[:, 1, 0, :], LB_FLOOR, None, ALU.max))
            settle()

            def product(s, k):
                n = ADA_DONE[s] - KD + k
                pos = ADA_POS[n]
                dve.wait_ge(s_raw[pos % RAW], 16 * (pos // RAW + 1))
                if k == 0:
                    if s > 1:
                        last = [t for t in ADA_ORDER if t != 1]
                        last = last[last.index(s) - 1]
                        dve.wait_ge(*((s_unit, SIGNAL["mod", last][1]) if last in DOWN_ADA else
                                      (s_ev, EVENT_AT[("ada", last)] + 1)))
                    TS(adacc[:, :], raw[:, pos % RAW, :], cact[:, 0:1], None, ALU.mult).then_inc(s_afree, 1)
                else:
                    dve.wait_ge(s_afree, n)
                    STT(adacc[:, :], raw[:, pos % RAW, :], cact[:, k:k + 1], adacc[:, :], ALU.mult, ALU.add).then_inc(s_afree, 1)

            def modulate(s):
                l, part = s // 6, s % 6
                unit_sum = s in DOWN_ADA
                bank = unit(("mod", s)) if unit_sum else event(("ada", s))[0]
                dst = mod[:, l, 8 * part:8 * part + 8]
                TTN(dst, bank[:, 0:KD], vecs[:, ADA_B + 8 * s:ADA_B + 8 * s + 8],
                    ALU.add).then_inc(s_uD if unit_sum else s_eD, 1)
                if part in (1, 4):
                    second = part // 4
                    if unit_sum:
                        unit_done(("mod", s))
                    else:
                        dve.wait_ge(s_eD, emptied(EVENTS, EVENT_AT[("ada", s)], "D"))
                    w = BV + (NFFN if second else NMIX) + KD * l
                    STT(wm[:, l, second, :], dst, 1.0, vecs[:, w:w + KD], ALU.add, ALU.mult).then_inc(s_mod, 1)

            def norm(l, second):
                dve.wait_ge(s_eA, emptied(EVENTS, EVENT_AT[(l, "norm2" if second else "norm1")], "A"))
                link(dve.reciprocal(rstd[:, :], rstd[:, :]))
                if (l, second) == (0, 0):
                    modulate(1)
                    modulate(0)
                dve.wait_ge(s_mod, 2 * l + 1 + second)
                settle()
                for k in range(KD):
                    STT(merged[:, k, :], xT[:, k, :], wm[:, l, second, k:k + 1], rstd[:, :], ALU.mult,
                        ALU.mult).then_inc(s_xr, 1)
                    if k in (3, 5, 7) and (l, second) != (1, 1):
                        norm_low(l, second, k - 3)
                if (l, second) != (1, 1):
                    norm_low(l, second, KD - 2)

            def norm_low(l, second, first):
                dve.wait_ge(s_hh, 4 * (2 * l + second) + first // 2 + 1)
                dve.wait_ge(s_xr, KD * (2 * l + second) + first + 2)
                for k in (first, first + 1):
                    sh = 24 * second + k
                    ins = STT(hS[:, 1, k, :], merged[:, k, :], mod[:, l, sh:sh + 1], hS[:, 0, k, :].bitcast(F32),
                              ALU.add, ALU.subtract)
                    if k % 2:
                        ins.then_inc(s_h, 1)
                    else:
                        link(ins)

            def half(buf, j):
                return buf[:, j * 512:(j + 1) * 512]

            def prepare(l, j):
                h = 2 ** (j - 1)
                F, G, q, k, qt, kt = (b.rearrange("p (n c h) -> p n c h", c=2, h=h) for b in (FB, GB, QB, KB, QT, KT))
                if j > 1:
                    dve.wait_ge(s_ev, EVENT_AT[(l, "lev", j - 1)] + 1)
                settle()
                if j == 1:
                    link(dve.tensor_copy(kt[:, :, 0, :], k[:, :, 0, :]))
                else:
                    link(TTN(kt[:, :, 0, :], k[:, :, 0, :], G[:, :, 0, :], ALU.mult))
                TTN(qt[:, :, 1, :], q[:, :, 1, :], F[:, :, 1, :], ALU.mult).then_inc(s_qk, 1)
                if j == NLEV - 1:
                    return
                n = 1024 // (2 * h)
                if j == 1:
                    link(dve.tensor_copy(G[:, :, 0, :], F[:, :, 1, :]))
                else:
                    link(TTN(G[:, :, 0, :], G[:, :, 0, :], F[:, :, 1, h - 1:h].to_broadcast([P, n, h]), ALU.mult))
                settle()
                dve.wait_ge(s_qk, l * (NLEV - 1) + j)
                link(TTN(F[:, :, 1, :], F[:, :, 1, :], F[:, :, 0, h - 1:h].to_broadcast([P, n, h]), ALU.mult))

            def keep_scores(l, j):
                banks = event((l, "lev", j))
                if j == 0:
                    dve.wait_ge(s_sc, l + 1)
                else:
                    dve.wait_ge(s_eD, emptied(EVENTS, EVENT_AT[(l, "lev", j - 1)], "D"))
                if j == NLEV - 1:
                    ins = dve.tensor_copy(sc[:, 2, :, :].rearrange("p h t -> p (h t)"), banks[0][:, :])
                else:
                    m = masks[:, j:j + 1, :].to_broadcast([P, HB, P])
                    for tt in range(TT):
                        ins = dve.copy_predicated(sc[:, tt, :, :], m, banks[tt][:, :].rearrange("p (h t) -> p h t", h=HB))
                ins.then_inc(s_eD, 1)

            def gated(l, g, j, dst):
                bank = unit((l, g, j))
                dve.wait_ge(s_sig, SIG0[l] + {"q": 0, "g": 2}[g] + j + 1)
                TTN(half(dst, j), sig[:, j, :], bank[:, :], ALU.mult).then_inc(s_uD, 1)

            SIG0 = [0, 4 + NF]

            def turn_gating():
                for l in range(DEPTH):
                    bank = unit(("wt", l))
                    for g in range(HB):
                        ins = TTN(wT[:, l, g, :], bank[:, g * P:(g + 1) * P], tri[:, :], ALU.mult)
                    ins.then_inc(s_uD, 1)

            def mixer(l):
                if l == 0:
                    for n in range(START_ADA):
                        k, which = 2 * (n // 3) + (n % 3) // 2, n % 3 % 2
                        pos = ADA_POS[n]
                        assert PIECES[pos][0] == (("ada", "ada1")[which], k)
                        dve.wait_ge(s_raw[pos % RAW], 16 * (pos // RAW + 1))
                        out_, src = (adacc[:, :], ada1)[which], raw[:, pos % RAW, :]
                        if k == 0:
                            ins = TS(out_, src, cact[:, 0:1], None, ALU.mult)
                        else:
                            dve.wait_ge(s_afree, n - (0, 2, 1)[n % 3])
                            ins = STT(out_, src, cact[:, k:k + 1], out_, ALU.mult, ALU.add)
                        ins.then_inc(s_afree, 1)
                norm(l, 0)
                if l == 0:
                    for k in range(4):
                        product(2, k)
                settle()
                link(dve.memset(GB, 1.0))
                for h in range(HB):
                    dve.wait_ge(s_uA, emptied(UNITS, UNIT_AT[(l, "f", h // 2)], "A"))
                    o = slice(h * T, (h + 1) * T)
                    link(TS(FB[:, o], FB[:, o], lbs[:, l, 1, h:h + 1], lbs[:, l, 2, h:h + 1], ALU.mult, ALU.add))
                    link(TS(KB[:, o], KB[:, o], lbs[:, l, 1, h:h + 1], None, ALU.mult))
                for j in range(2):
                    gated(l, "q", j, QB)
                unit_done((l, "q", 1))
                prepare(l, 1)
                if l == 0:
                    turn_gating()
                for j in range(3):
                    keep_scores(l, j)
                    prepare(l, j + 2)
                for j in range(2):
                    bank = unit((l, "ah", j))
                    dve.wait_ge(s_uA, emptied(UNITS, UNIT_AT[(l, "ac", j)], "A"))
                    TTN(half(AC, j), half(AC, j), bank[:, :], ALU.mult).then_inc(s_uD, 1)
                    keep_scores(l, j + 3)
                    prepare(l, j + 5)
                unit_done((l, "ah", 1))
                z, y = (b.rearrange("p (c t) -> p c t", t=T) for b in (AC, AH))
                cw = BV + CONV + 12 * l
                for cc in range(4):
                    link(TS(y[:, cc, :], z[:, cc, :], vecs[:, cw + cc:cw + cc + 1], None, ALU.mult))
                for back in (1, 2):
                    settle()
                    for cc in range(4):
                        w = cw + 4 * back + cc
                        link(STT(y[:, cc, back:T], z[:, cc, 0:T - back], vecs[:, w:w + 1], y[:, cc, back:T],
                                 ALU.mult, ALU.add))
                settle()
                TTN(AH, AH, AB, ALU.mult).then_inc(s_y, 1)
                keep_scores(l, 5)
                prepare(l, 7)
                keep_scores(l, 6)
                prepare(l, 8)
                for j in range(2):
                    bank = unit((l, "v", j))
                    dve.wait_ge(s_vst, 2 * l + j + 1)
                    link(dve.reciprocal(vst[:, 4 + j:5 + j], vst[:, 2 + j:3 + j]))
                    settle()
                    if j == 0:
                        dve.wait_ge(s_y, 3 * l + 1)
                    TS(half(VTOK, j), bank[:, :], vst[:, 4 + j:5 + j], None, ALU.mult).then_inc(s_uD, 1)
                    keep_scores(l, 7 + j)
                settle()
                dve.wait_ge(s_qk, (l + 1) * (NLEV - 1))
                banks = event((l, "sgu"))
                for g in range(HB):
                    w = BV + SNW + HB * l + g
                    ins = STT(YB[:, g * T:(g + 1) * T].rearrange("p (n t) -> p n t", n=TT),
                              banks[g // 2][:, (g % 2) * T:(g % 2 + 1) * T].rearrange("p (n t) -> p n t", n=TT),
                              vecs[:, w:w + 1], sgub[:, l, g:g + 1, :].to_broadcast([P, TT, P]), ALU.mult, ALU.add)
                    if g < HB - 1:
                        link(ins)
                ins.then_inc(s_eD, 1)
                dve.wait_ge(s_eD, emptied(EVENTS, EVENT_AT[(l, "sgu")], "D"))
                dve.wait_ge(s_uA, emptied(UNITS, UNIT_AT[(l, "u", 1)], "A"))
                TTN(UB, UB, YB, ALU.mult).then_inc(s_y, 1)

                def ada_part(n, ks):
                    gates = SIGNAL[(0, "gate" + BRANCHES[n], 0)][2] - 2
                    if l == 0:
                        for k in ks:
                            if n:
                                low_parts(gates + k + 1)
                            product(2 + n, k)
                ada_part(0, range(4, KD))
                gated(l, "g", 0, GS)
                dve.wait_ge(s_eA, emptied(EVENTS, EVENT_AT[(l, "ostat")], "A"))
                link(dve.reciprocal(OSD, OSD))
                gated(l, "g", 1, GS)
                settle()
                dve.wait_ge(s_y, 3 * l + 2)
                banks = event((l, "o"))
                link(TTN(half(YB, 0), half(OSD, 0), banks[0][:, :], ALU.mult))
                TTN(half(YB, 1), half(OSD, 1), banks[1][:, :], ALU.mult).then_inc(s_eD, 1)
                settle()
                dve.wait_ge(s_eD, emptied(EVENTS, EVENT_AT[(l, "o")], "D"))
                unit_done((l, "g", 1))
                for h in range(HB):
                    w = BV + HNW + HB * l + h
                    o = slice(h * T, (h + 1) * T)
                    ins = STT(YB[:, o], YB[:, o], vecs[:, w:w + 1], GS[:, o], ALU.mult, ALU.mult)
                ins.then_inc(s_y, 1)
                low_parts(SIGNAL[l, "gatea", 3][2])

                def branch_low(n):
                    dve.wait_ge(s_yh, 3 * l + n + 1)
                    src = {"a": AH, "c": UB, "b": YB}[BRANCHES[n]]
                    TTN(yS[:, 1, :, :].rearrange("p a b -> p (a b)"), src,
                        yS[:, 0, :, :].rearrange("p a b -> p (a b)").bitcast(F32), ALU.subtract).then_inc(s_yl, 1)

                def merged_low(j):
                    dve.wait_ge(s_mh, 4 * l + j + 1)
                    TTN(hS[:, 1, 2 * j:2 * j + 2, :], merged[:, 2 * j:2 * j + 2, :],
                        hS[:, 0, 2 * j:2 * j + 2, :].bitcast(F32), ALU.subtract).then_inc(s_ml, 1)
                branch_low(0)
                for n, b in enumerate(BRANCHES):
                    if n:
                        ada_part(n, range(4))
                        branch_low(n)
                        ada_part(n, range(4, KD))
                    for j in range(4):
                        bank = unit((l, "y" + b, j))
                        dve.wait_ge(s_uA, emptied(UNITS, UNIT_AT[(l, "gate" + b, j)], "A"))
                        m = merged[:, 2 * j:2 * j + 2, :].rearrange("p a b -> p (a b)")
                        if n == 0:
                            TTN(m, sig[:, j, :], bank[:, :], ALU.mult).then_inc(s_uD, 1)
                        else:
                            TTN(sig[:, j, :], sig[:, j, :], bank[:, :], ALU.mult).then_inc(s_uD, 1)
                            unit_done((l, "y" + b, j))
                            if n == 2:
                                dve.wait_ge(s_mg, 8 * l + j + 1)
                            TTN(m, m, sig[:, j, :], ALU.add).then_inc(s_mg, 1)
                            if n == 2 and j:
                                merged_low(j - 1)
                            if n == 2 and j == 3:
                                merged_low(3)
                    if l == 0 and n < 2:
                        modulate(2 + n)
                if l:
                    unit_done(("mod", 8))
                else:
                    dve.wait_ge(s_eD, emptied(EVENTS, EVENT_AT[("ada", 2)], "D"))
                for j in range(4):
                    bank = unit((l, "wo", j))
                    for m in range(2):
                        ch = 2 * j + m
                        ins = STT(xT[:, ch, :], bank[:, m * T:(m + 1) * T], mod[:, l, 16 + ch:17 + ch], xT[:, ch, :],
                                  ALU.mult, ALU.add)
                        if m:
                            ins.then_inc(s_uD, 1)
                        else:
                            link(ins)
                if l == 0:
                    modulate(4)
                settle()
                unit_done((l, "wo", 3))
                norm(l, 1)

            mixer(0)
            done = 0
            for f in range(NF):
                bank = unit(("ffn", f))
                dve.wait_ge(s_sig, 4 + f + 1)
                link(TTN(sig[:, f % 4, 0:T], sig[:, f % 4, 0:T], bank[:, 0:T], ALU.mult))
                settle()
                TTN(hidden0[:, f, :], sig[:, f % 4, 0:T], bank[:, T:2 * T], ALU.mult).then_inc(s_uD, 1)
                if f % 2:
                    pair = f // 2
                    for _ in range(FFN_TAKE[pair]):
                        if done % KD == 0 and done:
                            modulate(FFN_ADA[done // KD - 1])
                        product(FFN_ADA[done // KD], done % KD)
                        done += 1
            modulate(FFN_ADA[-1])
            for s in DOWN_ADA:
                for k in range(KD):
                    product(s, k)
                modulate(s)
            dve.wait_ge(s_eD, emptied(EVENTS, EVENT_AT[("ada", 11)], "D"))
            for e in range(2):
                banks = event(f"down{e}")
                for m in range(4):
                    ch = 4 * e + m
                    ins = STT(xT[:, ch, :], banks[m // 2][:, (m % 2) * T:(m % 2 + 1) * T],
                              mod[:, 0, 40 + ch:41 + ch], xT[:, ch, :], ALU.mult, ALU.add)
                    if m == 3:
                        ins.then_inc(s_eD, 1)
                    else:
                        link(ins)
            settle()
            dve.wait_ge(s_eD, emptied(EVENTS, EVENT_AT["down1"], "D"))
            mixer(1)

            def item_low(i, n):
                if low_part(n)[0] == "V":
                    dve.wait_ge(s_hi, i * NPC + (NSPLIT + n + 1))
                    slot = (NSPLIT + n) % SPL
                    TTN(split[:, slot, 1, :], raw[:, (RAW0 + n) % RAW, :], split[:, slot, 0, :].bitcast(F32),
                        ALU.subtract).then_inc(s_lo["V"], 1)

            for ch in range(KD):
                ins = TS(g2col[:, ch * P:(ch + 1) * P], ones[:, :], mod[:, 1, 40 + ch:41 + ch], None, ALU.mult)
            ins.then_inc(s_gw, 1)
            for n in range(SPL - 2):
                item_low(0, n)
            iota8 = small[:, 8:16]

            def pair(row):
                return route[:, row, :].rearrange("p (t e) -> p t e", t=TT)
            SEL, LG, ONE, TWO, GATE, POS, IDX, TMP, CNT = 0, 1, 2, 3, 4, 5, 6, 7, 11
            bank = unit("logits")
            TTN(pair(LG), bank[:, 0:2 * NE].rearrange("p (t e) -> p t e", t=TT),
                rtb[:, :].rearrange("p (a e) -> p a e", a=1).to_broadcast([P, TT, NE]), ALU.add).then_inc(s_uD, 1)
            unit_done("logits")
            for tt in range(TT):
                link(dve.max(mx8[:, tt, :], route[:, LG, tt * NE:(tt + 1) * NE]))
            settle()
            TTN(cur[:, 0:2], mx8[:, :, 0], mx8[:, :, 1], ALU.subtract).then_inc(s_prob, 1)
            for tt in range(TT):
                link(dve.max_index(ix8[:, tt, :], mx8[:, tt, :], route[:, LG, tt * NE:(tt + 1) * NE]))
            settle()
            link(dve.tensor_copy(route[:, IDX, :], ix8[:, :, :].rearrange("p t e -> p (t e)")))
            settle()
            for tt in range(TT):
                for row, k in ((ONE, 0), (TWO, 1)):
                    link(TS(route[:, row, tt * NE:(tt + 1) * NE], iota8,
                            route[:, IDX, tt * NE + k:tt * NE + k + 1], None, ALU.is_equal))
            settle()
            TTN(route[:, SEL, :], route[:, ONE, :], route[:, TWO, :], ALU.add).then_inc(s_rt, 1)
            dve.wait_ge(s_prob, 2)
            for tt in range(TT):
                o = slice(tt * NE, (tt + 1) * NE)
                link(TS(route[:, TMP, o], route[:, ONE, o], cur[:, 2 + tt:3 + tt], None, ALU.mult))
            settle()
            for tt in range(TT):
                o = slice(tt * NE, (tt + 1) * NE)
                link(STT(route[:, GATE, o], route[:, TWO, o], cur[:, 4 + tt:5 + tt], route[:, TMP, o],
                         ALU.mult, ALU.add))
            dve.wait_ge(s_rt, 1)
            bank = unit("rank")
            link(TTN(route[:, POS, :], bank[:, 0:2 * NE], route[:, SEL, :], ALU.mult))
            dve.tensor_copy(route[:, CNT, 0:NE], bank[:, 2 * NE:3 * NE]).then_inc(s_uD, 1)
            both = route[:, GATE:POS + 1, :].rearrange("p r (t e) -> p (r t) e", t=TT)
            picked = route[:, TMP:TMP + 3, :].rearrange("p r e -> p (r e)")[:, 0:4 * NE] \
                .rearrange("p (r e) -> p r e", e=NE)
            hot = route[:, 10, 0:NE]

            def select(row, last, link, settle):
                if last is not None:
                    dve.wait_ge(s_sel, last)
                link(dve.tensor_copy(cur[:, 6:8], row))
                settle()
                link(TS(hot, iota8, cur[:, 6:7], None, ALU.is_equal))
                settle()
                link(TTN(picked, both, route[:, 10:11, 0:NE].to_broadcast([P, 4, NE]), ALU.mult))
                settle()
                link(dve.reduce_sum(cur[:, 0:4], picked, AX_X))
                settle()
                link(TS(cur[:, 4:6], cur[:, 2:4], cur[:, 7:8], None, ALU.subtract))
                settle()
                for tt in range(TT):
                    link(TS(sel[:, 0, tt, :], slots[:, :], cur[:, 4 + tt:5 + tt], None, ALU.is_equal))
                    ins = TS(sel[:, 1, tt, :], slots[:, :], cur[:, 4 + tt:5 + tt], cur[:, tt:tt + 1],
                             ALU.is_equal, ALU.mult)
                    if tt == 0:
                        link(ins)
                ins.then_inc(s_sel, 1)

            select(items[:, 0, :], None, link, settle)
            unit_done("rank")
            NO = NE * JEX
            link(dve.memset(items[:, MAXI, 0:1], -1.0))
            link(dve.tensor_copy(items[:, 0:NE, 0], iota8))
            for j in range(JEX):
                link(TS(ov[:, 2, j * NE:(j + 1) * NE], route[:, CNT, 0:NE], float(CAP * (j + 1)), None, ALU.is_gt))
            src, shift = 2, 1
            while shift < NO:
                dst = 4 if src == 3 else 3
                settle()
                link(dve.tensor_copy(ov[:, dst, 0:shift], ov[:, src, 0:shift]))
                link(TTN(ov[:, dst, shift:NO], ov[:, src, shift:NO], ov[:, src, 0:NO - shift], ALU.add))
                src, shift = dst, 2 * shift
            settle()
            for r in range(REX):
                link(STT(ov[:, 5, :], ov[:, src, :], float(r + 1), ov[:, 2, :], ALU.is_equal, ALU.mult))
                settle()
                for col in range(2):
                    link(TTN(ov[:, 6 + col, :], ov[:, 5, :], ov[:, col, :], ALU.mult))
                settle()
                for col in range(2):
                    link(dve.reduce_sum(items[:, NE + r, col:col + 1], ov[:, 6 + col, :], AX_X))
            settle()
            link(TS(items[:, NE:MAXI, 0], items[:, NE:MAXI, 0], -1.0, None, ALU.add))
            link(TS(nitem[:, :], ov[:, src, NO - 1:NO], float(NE), None, ALU.add))
            settle()
            dve.tensor_copy(itemi[:, :], items[:, :, 0]).then_inc(s_items, 1)

            bank = unit("sel0")
            dve.tensor_copy(gwT[0:CAP, 1, :], bank[0:CAP, 0:T]).then_inc(s_gate, 1)

            def tokens_low(banks):
                for j in range(2):
                    x_hi, x_lo = (xE[:, part, 4 * j:4 * j + 4, :].rearrange("p a b -> p (a b)") for part in range(2))
                    last = TTN(x_lo, banks[j][:, 0:4 * CAP], x_hi.bitcast(F32), ALU.subtract)
                last.then_inc(s_xlo, 1)

            def expert_rows():
                for part in range(2):
                    o = slice(part * 512, (part + 1) * 512)
                    last = TTN(ye[0:CAP, o], Y_BANKS[part][0:CAP, :], g2bc[0:CAP, o], ALU.mult)
                last.then_inc(s_ye, 1)
            dve.wait_ge(s_uA, emptied(UNITS, len(UNITS), "A"))
            dve.wait_ge(s_xhi, 1)
            tokens_low(event("gather0"))
            dve.wait_ge(s_zero, 2)
            dve.wait_ge(s_items, 1)
            n_items = dve.value_load(nitem[0:1, 0:1], min_val=NE, max_val=MAXI)
            before = step[0]
            STEPS = len(GROUPS) + 9

            def item(i, first):
                n_link = [0]

                def ilink(ins):
                    n_link[0] += 1
                    ins.then_inc(s_v, 1)

                def isettle():
                    dve.wait_ge(s_v, i * STEPS + (before + n_link[0]))

                def hidden_rows(g):
                    width = len(GROUPS[g]) * P
                    one = psU[2 * (g % 2)][0:CAP, 0:width]
                    three = psU[2 * (g % 2) + 1][0:CAP, 0:width]
                    dve.wait_ge(s_silu, i * len(GROUPS) + (g + 1))
                    s = sig[0:CAP, g % 2, 0:width]
                    ilink(TTN(s, s, one, ALU.mult))
                    dve.wait_ge(s_used, i * NPC + (USED0 + G_END[g]))
                    isettle()
                    TTN(sig[0:CAP, 2 + g % 2, 0:width], s, three, ALU.mult).then_inc(s_hrow, 1)

                def tiles_low(g):
                    tiles = GROUPS[g]
                    dve.wait_ge(s_hhi, i * len(GROUPS) + (g + 1))
                    h_hi, h_lo = (hidE[:, part, tiles[0]:tiles[-1] + 1, :].rearrange("p a b -> p (a b)")
                                  for part in range(2))
                    TTN(h_lo, T_BANKS[g % 2][:, 0:len(tiles) * CAP], h_hi.bitcast(F32), ALU.subtract).then_inc(s_hlo, 1)

                def add_rows(j):
                    dve.wait_ge(s_sct, i * 5 + (j + 1))
                    o = oacc[:, j // 2, (j % 2) * 512:(j % 2 + 1) * 512]
                    TTN(o, o, psU[j][:, :], ALU.add).then_inc(s_add, 1)

                LAST = len(GROUPS) - 1
                for n in range(NPC):
                    if n >= first:
                        item_low(i, n)
                    if n == AHEAD - 1:
                        dve.wait_ge(s_used, i * NPC + USED0)
                        expert_rows()
                    for g in range(len(GROUPS)):
                        if n == G_END[g] + 3:
                            hidden_rows(g)
                        if n == (G_END[g + 1] if g < LAST else HID + 1) + 3:
                            tiles_low(g)
                    if n == G_END[0] + 5:
                        select(items[:, bass.ds(i + 1, 1), :].rearrange("p a b -> p (a b)"), i + 1, ilink, isettle)
                    if n == HID + 3:
                        for j in range(2):
                            add_rows(j)
                    if n == HID + 4:
                        for j in range(2, 4):
                            add_rows(j)
                        dve.wait_ge(s_add, i * 4 + 4)
                        ilink(dve.tensor_copy(gwT[0:CAP, 0, :], gwT[0:CAP, 1, :]))
                        isettle()
                        dve.wait_ge(s_sct, i * 5 + 5)
                        dve.tensor_copy(gwT[0:CAP, 1, :], psU[0][0:CAP, 0:T]).then_inc(s_gate, 1)
                    if n == GATHER_AT + 4:
                        dve.wait_ge(s_xhi, i + 2)
                        tokens_low(psU[0:2])
                assert n_link[0] == STEPS, n_link
            item(0, SPL - 2)
            with dve.Fori(1, n_items) as i:
                item(i, 0)
            dve.wait_ge(s_v, n_items * STEPS + before)
            dve.wait_ge(s_used, n_items * NPC + USED0)
            expert_rows()
            for j in range(4):
                dve.wait_ge(s_sct, n_items * 5 + (j + 1))
                o = oacc[:, j // 2, (j % 2) * 512:(j % 2 + 1) * 512]
                TTN(o, o, psU[j][:, :], ALU.add).then_inc(s_add, 1)
            dve.wait_ge(s_fw, 16)
            for tt in range(TT):
                dve.wait_ge(s_vst, 2 * TT + tt + 1)
                dve.reciprocal(vst[:, 4 + tt:5 + tt], vst[:, 2 + tt:3 + tt]).then_inc(s_gw, 1)
                dve.wait_ge(s_gw, 2 + tt)
                STT(oacc[:, tt, :], oacc[:, tt, :], vst[:, 4 + tt:5 + tt], fwbc, ALU.mult,
                    ALU.mult).then_inc(s_fin, 1)


_INS = ["x", "c", "ada_w", "ada_b", "norm_mix_w", "norm_ffn_w", "w_in", "conv_w", "hgrn_lb_logits", "hgrn_norm_w",
        "sgu_norm_w", "sgu_w", "sgu_b", "w_br_a", "w_br_b", "w_br_c", "w_o", "ffn_w1", "ffn_w3", "ffn_w2",
        "moe_router_w", "moe_router_b", "moe_w1", "moe_w3", "moe_w2", "final_norm_w"]


def kernel(**inputs):
    import numpy as _np
    import concourse.bacc as _bacc
    from concourse import mybir as _mybir
    from concourse.bass_utils import run_bass_kernel_spmd as _run

    nc = _bacc.Bacc("TRN2", target_bir_lowering=False, num_devices=1)
    arrays, args = {}, []
    for name in _INS:
        a = _np.ascontiguousarray(inputs[name])
        arrays[f"in_{name}_dram"] = a
        args.append(nc.dram_tensor(f"in_{name}_dram", a.shape, _mybir.dt.from_np(a.dtype), kind="ExternalInput").ap())
    o = nc.dram_tensor("out_0_dram", (1, T, D), F32, kind="ExternalOutput").ap()
    program(nc, *args, o)
    r = _run(nc, [arrays], core_ids=[0])
    return r.results[0]["out_0_dram"]
```
